# Optimizing a Trainium2 kernel written in Bass

```python
import math
import jax, jax.numpy as jnp
from jax import lax
import numpy as np

D_MODEL = 1024
BATCH = 1
SEQ = 256
DEPTH = 2

N_MIXERS = 2
N_CONV_LAYERS = (DEPTH + 1) // 2
N_MLA_LAYERS = DEPTH // 2
NORM_EPS = 1e-6
CONV_WIDTH = 31
MLA_HEADS = 16
QK_NOPE_DIM = 64
QK_ROPE_DIM = 32
V_HEAD_DIM = 64
Q_LORA_RANK = 384
KV_LORA_RANK = 256
ROPE_THETA = 10000.0
Q_BLOCK = 128
N_MEM = 256
XA_HEADS = 4
XA_HEAD_DIM = D_MODEL // XA_HEADS
N_GROUPS = 4
EXPERTS_PER_GROUP = 8
N_EXPERTS = N_GROUPS * EXPERTS_PER_GROUP
TOP_K_IN_GROUP = 2
EXPERT_FF = 256

kernel_name = "hybrid_conformer_mla_memxattn_hmoe"

def rms_norm(x, g):
    xf = x.astype(jnp.float32)
    y = xf * lax.rsqrt(jnp.mean(xf * xf, axis=-1, keepdims=True) + NORM_EPS)
    return (y * g.astype(jnp.float32)).astype(x.dtype)

def layer_norm(x, g, b):
    xf = x.astype(jnp.float32)
    mu = jnp.mean(xf, axis=-1, keepdims=True)
    var = jnp.mean(jnp.square(xf - mu), axis=-1, keepdims=True)
    y = (xf - mu) * lax.rsqrt(var + NORM_EPS)
    return (y * g.astype(jnp.float32) + b.astype(jnp.float32)).astype(x.dtype)

def conformer_conv(h, w_in, b_in, w_dw, b_dw, ln_g, ln_b, w_out, b_out):
    d = h.shape[-1]
    u = h @ w_in + b_in
    a, gate = jnp.split(u, 2, axis=-1)
    u = a * jax.nn.sigmoid(gate)
    u = lax.conv_general_dilated(
        u, w_dw.reshape(CONV_WIDTH, 1, d).astype(u.dtype),
        window_strides=(1,), padding=[(CONV_WIDTH - 1, 0)],
        dimension_numbers=("NWC", "WIO", "NWC"), feature_group_count=d) + b_dw
    u = jax.nn.silu(layer_norm(u, ln_g, ln_b))
    return u @ w_out + b_out

def rope_tables(positions, dim):
    inv_freq = 1.0 / (ROPE_THETA ** (jnp.arange(0, dim, 2, dtype=jnp.float32) / dim))
    ang = positions.astype(jnp.float32)[..., None] * inv_freq
    return jnp.cos(ang), jnp.sin(ang)

def apply_rope(x, cos, sin):
    x1, x2 = jnp.split(x.astype(jnp.float32), 2, axis=-1)
    out = jnp.concatenate([x1 * cos - x2 * sin, x2 * cos + x1 * sin], axis=-1)
    return out.astype(x.dtype)

def causal_block_attention(q, k, v, scale):
    b, s, h, dqk = q.shape
    dv = v.shape[-1]
    nb = s // Q_BLOCK
    qb = q.reshape(b, nb, Q_BLOCK, h, dqk).transpose(1, 0, 2, 3, 4)
    k_idx = jnp.arange(s)

    def one_block(args):
        q_blk, blk = args
        sc = jnp.einsum("bqhd,bkhd->bhqk", q_blk, k).astype(jnp.float32) * scale
        q_idx = blk * Q_BLOCK + jnp.arange(Q_BLOCK)
        mask = q_idx[:, None] >= k_idx[None, :]
        sc = jnp.where(mask[None, None], sc, -jnp.inf)
        p = jax.nn.softmax(sc, axis=-1).astype(v.dtype)
        return jnp.einsum("bhqk,bkhd->bqhd", p, v)

    o = lax.map(one_block, (qb, jnp.arange(nb)))
    return o.transpose(1, 0, 2, 3, 4).reshape(b, s, h * dv)

def mla(h, cos, sin, w_down, q_norm, w_uq, kv_norm, w_ukv, w_o):
    b, s, _ = h.shape
    dn = h @ w_down
    c_q, c_kv, k_r = jnp.split(dn, [Q_LORA_RANK, Q_LORA_RANK + KV_LORA_RANK], axis=-1)
    q = (rms_norm(c_q, q_norm) @ w_uq).reshape(b, s, MLA_HEADS, QK_NOPE_DIM + QK_ROPE_DIM)
    q_nope, q_r = jnp.split(q, [QK_NOPE_DIM], axis=-1)
    q_r = apply_rope(q_r, cos[:, :, None, :], sin[:, :, None, :])
    kv = (rms_norm(c_kv, kv_norm) @ w_ukv).reshape(b, s, MLA_HEADS, QK_NOPE_DIM + V_HEAD_DIM)
    k_nope, v = jnp.split(kv, [QK_NOPE_DIM], axis=-1)
    k_r = apply_rope(k_r, cos, sin)
    k_r = jnp.broadcast_to(k_r[:, :, None, :], (b, s, MLA_HEADS, QK_ROPE_DIM))
    q_full = jnp.concatenate([q_nope, q_r], axis=-1)
    k_full = jnp.concatenate([k_nope, k_r], axis=-1)
    scale = 1.0 / math.sqrt(QK_NOPE_DIM + QK_ROPE_DIM)
    o = causal_block_attention(q_full, k_full, v, scale)
    return o @ w_o

def mem_cross_attention(h, mem_n, wq, wkv, wo):
    b, s, _ = h.shape
    m = mem_n.shape[1]
    q = (h @ wq).reshape(b, s, XA_HEADS, XA_HEAD_DIM)
    k, v = jnp.split(mem_n @ wkv, 2, axis=-1)
    k = k.reshape(b, m, XA_HEADS, XA_HEAD_DIM)
    v = v.reshape(b, m, XA_HEADS, XA_HEAD_DIM)
    sc = jnp.einsum("bshd,bmhd->bhsm", q, k).astype(jnp.float32) / math.sqrt(XA_HEAD_DIM)
    p = jax.nn.softmax(sc, axis=-1).astype(v.dtype)
    o = jnp.einsum("bhsm,bmhd->bshd", p, v).reshape(b, s, D_MODEL)
    return o @ wo

def hierarchical_moe(h, w_grp, b_grp, w_exp, b_exp, w_gate, w_up, w_down):
    shp = h.shape
    xt = h.reshape(-1, shp[-1])
    g_logits = (xt @ w_grp + b_grp).astype(jnp.float32)
    g_probs = jax.nn.softmax(g_logits, axis=-1)
    g_val, g_idx = lax.top_k(g_probs, 1)
    e_logits = (xt @ w_exp + b_exp).astype(jnp.float32).reshape(-1, N_GROUPS, EXPERTS_PER_GROUP)
    e_logits = jnp.take_along_axis(e_logits, g_idx[:, :, None], axis=1)[:, 0]
    e_probs = jax.nn.softmax(e_logits, axis=-1)
    e_val, e_idx = lax.top_k(e_probs, TOP_K_IN_GROUP)
    e_val = e_val / jnp.sum(e_val, axis=-1, keepdims=True)
    within = jnp.sum(jax.nn.one_hot(e_idx, EXPERTS_PER_GROUP, dtype=jnp.float32)
                     * e_val[..., None], axis=1)
    combine = (g_val[:, :, None]
               * jax.nn.one_hot(g_idx[:, 0], N_GROUPS, dtype=jnp.float32)[:, :, None]
               * within[:, None, :]).reshape(-1, N_EXPERTS).astype(h.dtype)
    y = jnp.zeros_like(xt)
    for e in range(N_EXPERTS):
        he = jax.nn.silu(xt @ w_gate[e]) * (xt @ w_up[e])
        y = y + combine[:, e:e + 1] * (he @ w_down[e])
    return y.reshape(shp)

def setup_inputs(seed: int = 0) -> dict:
    key = jax.random.key(seed)
    ks = iter(jax.random.split(key, 64))
    f32 = jnp.float32

    def w(shape, fan_in):
        return jax.random.normal(next(ks), shape, f32) * (fan_in ** -0.5)

    def gain(shape):
        return 1.0 + 0.01 * jax.random.normal(next(ks), shape, f32)

    def bias(shape, scale=0.01):
        return scale * jax.random.normal(next(ks), shape, f32)

    D = D_MODEL
    NC, NM, L = N_CONV_LAYERS, N_MLA_LAYERS, DEPTH
    x = jax.random.normal(next(ks), (BATCH, SEQ, D), f32)
    mem = jax.random.normal(next(ks), (BATCH, N_MEM, D), f32)
    offs = jax.random.randint(next(ks), (BATCH, 1), 0, 1024, dtype=jnp.int32)
    positions = (offs + jnp.arange(SEQ, dtype=jnp.int32)[None, :]).astype(jnp.int32)
    return {
        "x": x, "mem": mem, "positions": positions,
        "norm_mix": gain((L, D)),
        "conv_w_in": w((NC, D, 2 * D), D), "conv_b_in": bias((NC, 2 * D)),
        "conv_w_dw": w((NC, CONV_WIDTH, D), CONV_WIDTH), "conv_b_dw": bias((NC, D)),
        "conv_ln_g": gain((NC, D)), "conv_ln_b": bias((NC, D)),
        "conv_w_out": w((NC, D, D), D), "conv_b_out": bias((NC, D)),
        "mla_w_down": w((NM, D, Q_LORA_RANK + KV_LORA_RANK + QK_ROPE_DIM), D),
        "mla_q_norm": gain((NM, Q_LORA_RANK)),
        "mla_w_uq": w((NM, Q_LORA_RANK, MLA_HEADS * (QK_NOPE_DIM + QK_ROPE_DIM)), Q_LORA_RANK),
        "mla_kv_norm": gain((NM, KV_LORA_RANK)),
        "mla_w_ukv": w((NM, KV_LORA_RANK, MLA_HEADS * (QK_NOPE_DIM + V_HEAD_DIM)), KV_LORA_RANK),
        "mla_w_o": w((NM, MLA_HEADS * V_HEAD_DIM, D), MLA_HEADS * V_HEAD_DIM),
        "norm_xa": gain((L, D)), "norm_mem": gain((L, D)),
        "xa_wq": w((L, D, D), D), "xa_wkv": w((L, D, 2 * D), D), "xa_wo": w((L, D, D), D),
        "norm_ffn": gain((L, D)),
        "moe_w_grp": w((L, D, N_GROUPS), D), "moe_b_grp": bias((L, N_GROUPS)),
        "moe_w_exp": w((L, D, N_EXPERTS), D), "moe_b_exp": bias((L, N_EXPERTS)),
        "moe_w_gate": w((L, N_EXPERTS, D, EXPERT_FF), D),
        "moe_w_up": w((L, N_EXPERTS, D, EXPERT_FF), D),
        "moe_w_down": w((L, N_EXPERTS, EXPERT_FF, D), EXPERT_FF),
        "final_norm": gain((D,)),
    }

def reference(x, mem, positions, norm_mix,
              conv_w_in, conv_b_in, conv_w_dw, conv_b_dw, conv_ln_g, conv_ln_b,
              conv_w_out, conv_b_out,
              mla_w_down, mla_q_norm, mla_w_uq, mla_kv_norm, mla_w_ukv, mla_w_o,
              norm_xa, norm_mem, xa_wq, xa_wkv, xa_wo,
              norm_ffn, moe_w_grp, moe_b_grp, moe_w_exp, moe_b_exp,
              moe_w_gate, moe_w_up, moe_w_down, final_norm):
    cos, sin = rope_tables(positions, QK_ROPE_DIM)
    h = x
    for i in range(DEPTH):
        j = i // N_MIXERS
        hn = rms_norm(h, norm_mix[i])
        if i % N_MIXERS == 0:
            mix = conformer_conv(hn, conv_w_in[j], conv_b_in[j], conv_w_dw[j], conv_b_dw[j],
                                 conv_ln_g[j], conv_ln_b[j], conv_w_out[j], conv_b_out[j])
        else:
            mix = mla(hn, cos, sin, mla_w_down[j], mla_q_norm[j], mla_w_uq[j],
                      mla_kv_norm[j], mla_w_ukv[j], mla_w_o[j])
        h = h + mix
        h = h + mem_cross_attention(rms_norm(h, norm_xa[i]), rms_norm(mem, norm_mem[i]),
                                    xa_wq[i], xa_wkv[i], xa_wo[i])
        h = h + hierarchical_moe(rms_norm(h, norm_ffn[i]), moe_w_grp[i], moe_b_grp[i],
                                 moe_w_exp[i], moe_b_exp[i], moe_w_gate[i], moe_w_up[i],
                                 moe_w_down[i])
    return rms_norm(h, final_norm)


_drawn_inputs = setup_inputs


def setup_inputs(seed=0):
    import zlib

    import numpy as np

    out = dict(_drawn_inputs(seed))
    spreads = {}
    factors = {'norm_mix': 2.834,
     'conv_ln_b': 2.694,
     'mla_q_norm': 7.643,
     'mla_kv_norm': 5.954,
     'norm_xa': 6.237,
     'norm_mem': 5.718,
     'moe_b_grp': 3.142,
     'moe_b_exp': 3.007,
     'final_norm': 5.798}
    for name, (base, spread) in spreads.items():
        noise = np.random.default_rng([zlib.crc32(name.encode()), seed]).standard_normal(out[name].shape)
        drawn = base * np.exp(spread * noise) if base else spread * noise
        out[name] = __import__('jax').numpy.asarray(drawn.astype(out[name].dtype))
    for name, factor in factors.items():
        out[name] = (out[name] * factor).astype(out[name].dtype)
    return out
```

```python
from contextlib import ExitStack

import numpy as np

import concourse.bass as bass
from concourse import mybir

F32 = mybir.dt.float32
I32 = mybir.dt.int32
ALU = mybir.AluOpType
ACT = mybir.ActivationFunctionType
AX = mybir.AxisListType

P = 128
EPS = 1e-6
NEG = -1e30
RING = 12
UNIT = 2048
SLOTS = 64
NBANK = 8


class Tiles:

    def __init__(self, filled=0, dve=0, act=0):
        self.n = 0
        self.count = {"filled": filled, "dve": dve, "act": act}
        self.at, self.order = {}, {}

    def add(self, name, owner):
        self.at[name] = {"n": self.n, "owner": owner, "filled": self.count["filled"] + 1,
                         "freed": self.count[owner] + 1, "per_turn": {"filled": 0, "dve": 0, "act": 0}}
        self.order[self.n] = name
        self.n += 1
        self.count["filled"] += 1
        self.count[owner] += 1

    def loop(self, names, turns):
        real = [x for x in names if x]
        per_turn = {"filled": len(real), "dve": sum(x[1] == "dve" for x in real), "act": sum(x[1] == "act" for x in real)}
        self.loop_start = self.n
        begin = dict(self.count)
        for i, x in enumerate(names):
            if x:
                self.add(*x)
                self.at[x[0]].update(n=self.loop_start + i, per_turn=per_turn)
        self.order = {n: x for n, x in self.order.items() if n < self.loop_start}
        for i, x in enumerate(names):
            if x:
                self.order[self.loop_start + len(names) * (turns - 1) + i] = x[0]
        self.n = self.loop_start + len(names) * turns
        self.count = {k: begin[k] + per_turn[k] * turns for k in begin}


def trunk(nc, A, out):
    _, T, D = A["x"].shape
    TT = T // P
    KD = D // P
    W = A["conv_w_dw"].shape[1]
    NMEM = A["mem"].shape[1]
    QR = A["mla_q_norm"].shape[1]
    KVR = A["mla_kv_norm"].shape[1]
    ROPE = A["mla_w_down"].shape[2] - QR - KVR
    DOWN = QR + KVR + ROPE
    NOPE = VD = 64
    QKD = NOPE + ROPE
    H = A["mla_w_uq"].shape[2] // QKD
    XH = 4
    XHD = D // XH
    E = A["moe_w_exp"].shape[2]
    G = A["moe_w_grp"].shape[2]
    EG = E // G
    FF = A["moe_w_gate"].shape[3]
    HALF = 512
    NH = D // HALF
    XSCALE = 1.0 / float(np.sqrt(XHD))
    MSCALE = 1.0 / float(np.sqrt(QKD))
    assert (T, D, NMEM, FF, EG, H, QKD) == (256, 1024, 256, 256, 8, 16, 96)

    N_CIN, N_KV, N_COUT, N_XQ, N_XO = 8, 8, 4, 4, 4
    N_MLA_DOWN, N_UQ, N_UKV, N_MO = 3, 3, 2, 4
    U_CIN = 0
    U_KV = [N_CIN, N_CIN + N_KV]
    U_COUT = N_CIN + 2 * N_KV
    U_XQ0 = U_COUT + N_COUT
    U_XO0 = U_XQ0 + N_XQ
    U_MOE0 = U_XO0 + N_XO
    U_DOWN = U_MOE0 + 3 * E
    U_UQ = U_DOWN + N_MLA_DOWN
    U_UKV = U_UQ + N_UQ
    U_MO = U_UKV + N_UKV
    U_XQ1 = U_MO + N_MO
    U_XO1 = U_XQ1 + N_XQ
    U_MOE1 = U_XO1 + N_XO
    U_XQ, U_XO, U_MOE = [U_XQ0, U_XQ1], [U_XO0, U_XO1], [U_MOE0, U_MOE1]
    GU = 3 * EG
    TURNS = G

    tiles = Tiles()
    alt = ("dve", "act")
    tiles.add("prm", "dve")
    for j in range(4):
        tiles.add(f"n0_{j}", alt[j % 2])
    for j in range(4):
        tiles.add(f"mem_{j}", alt[j % 2])
    for j in range(KD):
        tiles.add(f"glu_{j}", "dve")
    for l in range(2):
        for j in range(4):
            tiles.add(f"xk{l}_{j}", "act")
        for f in range(NH):
            for t in range(TT):
                tiles.add(f"xv{l}_{f}_{t}", "act")
    tiles.add("mu", "dve")
    tiles.add("var", "act")

    def add_out(name):
        for f in range(NH):
            for t in range(TT):
                tiles.add(f"{name}_{f}_{t}", "dve")

    MOE_TILES = (
        [(f"ga{k}", alt[k % 2]) for k in range(KD)]
        + [("gu0", "dve"), ("gu1", "dve"), ("st0", "act"), ("ht0", "act"), ("yd0_0", "dve"), ("yd0_1", "act")]
        + [("gu2", "dve"), ("ht1", "act"), ("yd1_0", "dve"), ("yd1_1", "act"), ("gu3", "dve")]
        + [(f"sc0_{f}_{t}", "dve") for f in range(NH) for t in range(TT)]
        + [("st1", "act"), ("ht2", "act"), ("yd2_0", "dve"), ("yd2_1", "act")]
        + [("ht3", "act"), ("yd3_0", "dve"), ("yd3_1", "act")]
        + [(f"sc1_{f}_{t}", "dve") for f in range(NH) for t in range(TT)]
    )
    MOE_TILES += [None] * (-len(MOE_TILES) % NBANK)
    TL = len(MOE_TILES)
    TL_DVE = sum(1 for x in MOE_TILES if x and x[1] == "dve")
    TL_ACT = sum(1 for x in MOE_TILES if x and x[1] == "act")
    TL_ALL = TL_DVE + TL_ACT

    add_out("cout")
    for l in range(2):
        if l == 1:
            for j in range(4):
                tiles.add(f"n4_{j}", alt[j % 2])
            for t in range(TT):
                tiles.add(f"dnA_{t}", "act")
            for t in range(TT):
                tiles.add(f"dnB_{t}", "act")
            for j in range(3):
                tiles.add(f"cT_{j}", alt[j % 2])
            for n in range(3):
                for t in range(TT):
                    tiles.add(f"uq_{n}_{t}", "act")
            for j in range(H // 2):
                tiles.add(f"qT_{j}", alt[j % 2])
            for n in range(4):
                for t in range(TT):
                    tiles.add(f"ukv_{n}_{t}", alt[t % 2])
            for j in range(H // 2):
                tiles.add(f"kT_{j}", alt[j % 2])
            tiles.add("ms_0", "dve")
            tiles.add("ms_1", "dve")
            for hd in range(H):
                if hd + 2 < H:
                    tiles.add(f"ms_{hd + 2}", "dve")
                tiles.add(f"mp_{hd}", "act")
                if hd % 2:
                    tiles.add(f"mo_{hd // 2}", "act")
            add_out("mw")
        for j in range(4):
            tiles.add(f"nx{l}_{j}", alt[j % 2])
        for j in range(4):
            tiles.add(f"xq{l}_{j}", alt[j % 2])
        for hd in range(XH):
            tiles.add(f"xs{l}_{hd}", "act")
        for hd in range(XH):
            tiles.add(f"xp{l}_{hd}", "act")
            tiles.add(f"xo{l}_{hd}", "dve")
        add_out(f"xw{l}")
        for j in range(4):
            tiles.add(f"nf{l}_{j}", alt[j % 2])
        tiles.add(f"lg{l}", "dve")
        tiles.add(f"rk{l}", "dve")
        tiles.loop([(f"m{l}" + x[0], x[1]) if x else None for x in MOE_TILES], TURNS)

    ctx = ExitStack()
    with ctx:
        def sb(name, shape, dt=F32):
            return ctx.enter_context(nc.sbuf_tensor(name, shape, dt))

        def sem(name):
            return ctx.enter_context(nc.semaphore(name))

        banks = [ctx.enter_context(nc.psum_tensor(f"bank{i}", [P, 512], F32)) for i in range(NBANK)]

        ring = sb("ring", [P, RING * UNIT])
        h = sb("h", [P, TT, D])
        xhat = sb("xhat", [P, TT, D])
        hT = sb("hT", [P, KD, T])
        kv0 = sb("kv0", [P, 4096])
        kv1 = sb("kv1", [P, 4096])
        scratch = sb("scratch", [P, 9856])
        bcast_row = sb("bcast_row", [P, D])
        ident = sb("ident", [P, P])
        before = sb("before", [P, P])
        ones = sb("ones", [P, P])
        mean_of = sb("mean_of", [P, P])
        slot_no = sb("slot_no", [P, SLOTS])
        slot_no_i = sb("slot_no_i", [P, SLOTS], I32)
        desc = sb("desc", [P, EG])
        causal = sb("causal", [P, 3 * P])
        router = sb("router", [P, 2, KD, G + E])
        router_b = sb("router_b", [P, 2, G + E])
        NA_ROWS, NB_ROWS = 8, W + 7
        prmT = sb("prmT", [P, KD * (NA_ROWS + NB_ROWS)])
        stat = sb("stat", [P, 64])
        rt = sb("rt", [P, 1024])
        pos_i = sb("pos_i", [P, TT], I32)
        rope_t = sb("rope_t", [P, 6, TT, ROPE // 2])
        rope_i = sb("rope_i", [P, TT, ROPE // 2], I32)
        most = sb("most", [P, 2], I32)

        gain_of = prmT[:, 0:KD * NA_ROWS].rearrange("p (k r) -> p k r", k=KD)
        conv_of = prmT[:, KD * NA_ROWS:].rearrange("p (k r) -> p k r", k=KD)
        R_MIX, R_XA, R_MEM, R_FFN = 0, 2, 4, 6
        R_BDW, R_LNG, R_LNB, R_BA, R_BG, R_QN, R_KVN = range(W, W + 7)
        prm_a = kv1[0:NA_ROWS, 0:D]
        prm_b = kv1[0:NB_ROWS, D:2 * D]

        def view(t, at, *shape):
            n = int(np.prod(shape))
            v = t[:, at:at + n]
            if len(shape) == 2:
                return v.rearrange("p (a b) -> p a b", a=shape[0])
            if len(shape) == 3:
                return v.rearrange("p (a b c) -> p a b c", a=shape[0], b=shape[1])
            return v

        xkT = [view(kv0, 0, KD, NMEM), view(kv1, 0, KD, NMEM)]
        xv = [view(kv0, 2048, 2, D), view(kv1, 2048, 2, D)]
        PADDED = W - 1 + T
        u_pad = view(scratch, 0, KD, PADDED)
        conv = view(scratch, 2304, KD, T)
        mem_rows = view(scratch, 4352, 2, D)
        conv_sq = view(scratch, 4352, KD, T)
        memT = [view(scratch, 6400, KD, NMEM), xhat[:, :, :].rearrange("p a b -> p (a b)").rearrange("p (k m) -> p k m", k=KD)]
        sig = view(scratch, 8448, 2, T)
        ln_rstd = view(scratch, 8960, T)
        xqT = view(scratch, 0, KD, T)
        xprob = view(scratch, 2048, XH, TT, NMEM)
        xprobT = view(scratch, 4096, 2, 2 * T)
        qtok = view(scratch, 0, TT, H * QKD)
        ktok = qtok
        qhT = view(scratch, 3072, H, T)
        khT = view(kv0, 0, H, T)
        vtok = xhat
        down = view(scratch, 7168, TT, DOWN)
        cT = view(scratch, 8512, 5, T)
        rope_tmp = scratch[:, 3072:3072 + 4 * TT * H * (ROPE // 2)].rearrange(
            "p (n t h r) -> p n t h r", n=4, t=TT, h=H)
        squares_junk = view(scratch, 5120, 2 * TT, 384)
        score = view(scratch, 7168, 2, 3 * P)
        prob = view(scratch, 7168 + 768, 2, 3 * P)
        probT = view(scratch, 7168 + 1536, 2, 3 * P)
        xg = view(scratch, 0, KD, EG * SLOTS)
        pick = view(scratch, 4096, TT, EG * SLOTS)
        yslot = view(scratch, 5120, 2, D)
        put = view(scratch, 7168, 4, TT, P)
        hmid = view(scratch, 8192, 2, FF)
        gated = view(scratch, 8704, 2, FF)
        hmidT = view(scratch, 9216, 2, P)

        bank_filled, dve_freed, act_freed = sem("bank_filled"), sem("dve_freed"), sem("act_freed")
        unit_landed = [sem(f"unit_landed{i}") for i in range(RING)]
        x_landed, mem_landed, prm_landed, small_landed, row_landed = (
            sem("x_landed"), sem("mem_landed"), sem("prm_landed"), sem("small_landed"), sem("row_landed"))
        pool_step, consts_ready, bias_added = sem("pool_step"), sem("consts_ready"), sem("bias_added")
        rms_ready, normed = sem("rms_ready"), sem("normed")
        dve_step, act_step = sem("dve_step"), sem("act_step")
        sig_ready, conv_ready, centred, squared, ln_scaled, conv_act = (
            sem("sig_ready"), sem("conv_ready"), sem("centred"), sem("squared"), sem("ln_scaled"), sem("conv_act"))
        angles_ready, sincos_ready = sem("angles_ready"), sem("sincos_ready")
        x_max_ready, x_exp_ready, x_prob_ready = sem("x_max_ready"), sem("x_exp_ready"), sem("x_prob_ready")
        down_rms_ready = sem("down_rms_ready")
        down_ready, roped, ktok_ready = sem("down_ready"), sem("roped"), sem("ktok_ready")
        m_max_ready, m_exp_ready, m_prob_ready = sem("m_max_ready"), sem("m_exp_ready"), sem("m_prob_ready")
        route_diff, route_exp, assigned, routed = (
            sem("route_diff"), sem("route_exp"), sem("assigned"), sem("routed"))
        stored = sem("stored")

        class Sweep:
            pass

        sweeps = []
        for l in range(2):
            a = Sweep()
            a.l, a.tiles, a.filled, a.dve, a.act = l, tiles, bank_filled, dve_freed, act_freed
            a.landed, a.unit0 = unit_landed, U_MOE[l]
            a.first_use = [0] * RING
            b = Sweep()
            b.l = l
            b.tiles = Tiles(TL_ALL, TL_DVE, TL_ACT)
            b.tiles.loop([(f"m{l}" + x[0], x[1]) if x else None for x in MOE_TILES], 3 * TURNS)
            b.filled, b.dve, b.act = sem(f"more_filled{l}"), sem(f"more_dve{l}"), sem(f"more_act{l}")
            b.landed = [sem(f"more_landed{l}_{i}") for i in range(RING)]
            b.unit0 = U_MOE[l] % RING
            b.first_use = [1 if i < b.unit0 else 0 for i in range(RING)]
            for s, tag in ((a, ""), (b, "more_")):
                s.picked, s.weighted, s.gate_ready = sem(f"{tag}picked{l}"), sem(f"{tag}weighted{l}"), sem(f"{tag}gate_ready{l}")
            b.shifted = sem(f"slots_shifted{l}")
            sweeps.append((a, b))

        class Main:
            pass

        main = Main()
        main.tiles, main.filled, main.dve, main.act = tiles, bank_filled, dve_freed, act_freed

        def evac_value(s, name, it=0):
            x = s.tiles.at[name]
            return it * x["per_turn"][x["owner"]] + x["freed"]

        def filled_value(s, name, it=0):
            x = s.tiles.at[name]
            return it * x["per_turn"]["filled"] + x["filled"]

        def wait_filled(eng, name, it=0, s=main):
            eng.wait_ge(s.filled, filled_value(s, name, it))
            return banks[s.tiles.at[name]["n"] % NBANK]

        def wait_evac(eng, name, it=0, s=main):
            owner = s.tiles.at[name]["owner"]
            eng.wait_ge(s.dve if owner == "dve" else s.act, evac_value(s, name, it))

        def evac(ins, name, s=main):
            owner = s.tiles.at[name]["owner"]
            ins.then_inc(s.dve if owner == "dve" else s.act, 1)

        def open_bank(pe, name):
            n = tiles.at[name]["n"] - NBANK
            while n >= 0 and n not in tiles.order:
                n -= NBANK
            if n >= 0:
                last = tiles.order[n]
                wait_evac(pe, last, TURNS - 1 if tiles.at[last]["per_turn"]["filled"] else 0)
            return banks[n % NBANK]

        def bank_before(name):
            n = [i for i, x in enumerate(MOE_TILES) if x and x[0] == name][0] - NBANK
            back = 0
            while n < 0 or MOE_TILES[n] is None:
                if n < 0:
                    n, back = n + TL, back + 1
                else:
                    n -= NBANK
            return MOE_TILES[n][0], back

        def wait_in_turn(pe, s, it, banks_of=(), copies_of=()):
            need = {}
            for name, back in [bank_before(x) for x in banks_of] + [(x, 0) for x in copies_of]:
                x = s.tiles.at[f"m{s.l}{name}"]
                o = x["owner"]
                need[o] = max(need.get(o, 0), x["freed"] - back * x["per_turn"][o])
            for o, value in need.items():
                pe.wait_ge(s.dve if o == "dve" else s.act, it * (TL_DVE if o == "dve" else TL_ACT) + value)
            return [banks[s.tiles.at[f"m{s.l}{x}"]["n"] % NBANK] for x in banks_of]

        def unit(i, *shape):
            s = (i % RING) * UNIT
            v = ring[:, s:s + int(np.prod(shape))]
            if len(shape) == 2:
                return v.rearrange("p (a b) -> p a b", a=shape[0])
            return v

        def wait_unit(eng, i):
            eng.wait_ge(unit_landed[i % RING], 16 * (i // RING + 1))

        last_tile = {}
        for j in range(N_CIN):
            last_tile[U_CIN + j] = f"glu_{2 * (j // 2) + 1}"

        def last_of(u0, name, per_unit_tile):
            for j in range(4):
                last_tile[u0 + j] = f"{name}_{j}" if per_unit_tile else f"{name}_{j // 2}_{TT - 1}"

        for l in range(2):
            last_of(U_KV[l], f"xk{l}", True)
            last_of(U_KV[l] + 4, f"xv{l}", False)
            last_of(U_XQ[l], f"xq{l}", True)
            last_of(U_XO[l], f"xw{l}", False)
        last_of(U_COUT, "cout", False)
        last_of(U_MO, "mw", False)
        last_tile.update({U_DOWN: f"dnA_{TT - 1}", U_DOWN + 1: f"dnA_{TT - 1}", U_DOWN + 2: f"dnB_{TT - 1}"})
        last_tile.update({U_UQ + n: f"uq_{n}_{TT - 1}" for n in range(N_UQ)})
        last_tile.update({U_UKV + n: f"ukv_{2 * n + 1}_{TT - 1}" for n in range(N_UKV)})

        def last_in_turn(l, u):
            return f"m{l}gu{u // 6}" if u % 6 < 4 else f"m{l}yd{u // 6}_{NH - 1}"

        for l in range(2):
            for u in range(GU):
                last_tile[U_MOE[l] + (TURNS - 1) * GU + u] = last_in_turn(l, u)

        block = ctx.enter_context(nc.Block())

        @block.sync
        def _(sp):
            def slot_free(i):
                if i >= RING:
                    last = last_tile[i - RING]
                    wait_filled(sp, last, TURNS - 1 if tiles.at[last]["per_turn"]["filled"] else 0)

            def load(i, src, *shape):
                slot_free(i)
                sp.dma_start(unit(i, *shape), src).then_inc(unit_landed[i % RING], 16)

            def by_channel(i, w, cols):
                load(i, w.rearrange("(p k) n -> p k n", k=KD)[:, :, cols:cols + 256], KD, 256)

            def k_by_p(i, w, f):
                for q in range(2):
                    src = w.rearrange("(k p) n -> p k n", p=P)[:, 4 * q:4 * q + 4, f * HALF:(f + 1) * HALF]
                    load(i + q, src, 4, HALF)

            def p_by_k(i, w, c0, n):
                for q in range(2):
                    src = w.rearrange("(p k) n -> p k n", k=KD)[:, 4 * q:4 * q + 4, c0:c0 + n]
                    load(i + q, src, 4, n)

            w_in = A["conv_w_in"][0]
            for j in range(4):
                by_channel(U_CIN + 2 * j, w_in, 256 * j)
                by_channel(U_CIN + 2 * j + 1, w_in, D + 256 * j)
            for l in range(2):
                for j in range(4):
                    by_channel(U_KV[l] + j, A["xa_wkv"][l], 256 * j)
                for f in range(NH):
                    p_by_k(U_KV[l] + 4 + 2 * f, A["xa_wkv"][l], D + f * HALF, HALF)
            for f in range(NH):
                k_by_p(U_COUT + 2 * f, A["conv_w_out"][0], f)

            def cross(l):
                for j in range(4):
                    by_channel(U_XQ[l] + j, A["xa_wq"][l], 256 * j)
                for f in range(NH):
                    k_by_p(U_XO[l] + 2 * f, A["xa_wo"][l], f)

            def pairs(s, half, first, turn=None, steps_back=0, before_loop=False):
                l = s.l
                for pair in (2 * half, 2 * half + 1):
                    srcs = []
                    for e in range(2):
                        ex = first + (2 * pair + e)
                        srcs += [A["moe_w_gate"][l, ex].rearrange("(p k) n -> p k n", k=KD),
                                 A["moe_w_up"][l, ex].rearrange("(p k) n -> p k n", k=KD)]
                    for e in range(2):
                        srcs.append(A["moe_w_down"][l, first + (2 * pair + e)].rearrange("(k p) n -> p k n", p=P))
                    for i, src in enumerate(srcs):
                        u = 6 * pair + i
                        slot = (s.unit0 + u) % RING
                        if before_loop:
                            slot_free(s.unit0 + u)
                        else:
                            x = s.tiles.at[last_in_turn(l, (u + RING) % GU)]
                            sp.wait_ge(s.filled, turn * TL_ALL + (x["filled"] - steps_back * TL_ALL))
                        shape = (KD, FF) if i < 4 else (FF // P, D)
                        sp.dma_start(unit(slot, *shape), src).then_inc(s.landed[slot], 16)

            def moe(l):
                a, b = sweeps[l]
                pairs(a, 0, 0, before_loop=True)
                with sp.Fori(0, TURNS - 1) as turn:
                    pairs(a, 1, turn * EG, turn)
                    pairs(a, 0, turn * EG + EG, turn)
                pairs(a, 1, (TURNS - 1) * EG, TURNS - 1)
                sp.wait_ge(routed, l + 1)
                n = sp.value_load(most[0:1, l:l + 1], min_val=0, max_val=T)
                with sp.If(n > SLOTS):
                    with sp.Fori(0, 3) as r:
                        with sp.Fori(0, TURNS) as turn:
                            pairs(b, 0, turn * EG, r * TURNS + turn, steps_back=1)
                            pairs(b, 1, turn * EG, r * TURNS + turn)
                    wait_filled(sp, f"m{l}yd3_{NH - 1}", 3 * TURNS - 1, b)

            cross(0)
            moe(0)
            p_by_k(U_DOWN, A["mla_w_down"][0], 0, HALF)
            load(U_DOWN + 2, A["mla_w_down"][0].rearrange("(p k) n -> p k n", k=KD)[:, :, HALF:DOWN], KD, DOWN - HALF)
            for n in range(3):
                load(U_UQ + n, A["mla_w_uq"][0].rearrange("(k p) n -> p k n", p=P)[:, :, n * HALF:(n + 1) * HALF], 3, HALF)
            for n in range(2):
                load(U_UKV + n, A["mla_w_ukv"][0].rearrange("(k p) n -> p k n", p=P)[:, :, n * D:(n + 1) * D], 2, D)
            for f in range(NH):
                k_by_p(U_MO + 2 * f, A["mla_w_o"][0], f)
            cross(1)
            moe(1)
            for t in range(TT):
                sp.wait_ge(normed, 14 + t + 1)
                sp.dma_start(out[0, t * P:(t + 1) * P, :], xhat[:, t, :]).then_inc(stored, 16)
            sp.wait_ge(stored, 16 * TT)

        @block.gpsimd
        def _(pool):
            n = 0

            def step(ins):
                nonlocal n
                n += 1
                ins.then_inc(pool_step, 1)
                pool.wait_ge(pool_step, n)

            step(nc.gpsimd.memset(kv1[0:NB_ROWS, 0:2 * D], 0.0))
            nc.gpsimd.memset(ident[:, :], 0.0).then_inc(consts_ready, 1)
            pool.wait_ge(consts_ready, 1)
            nc.gpsimd.affine_select(out=ident[:, :], in_=ident[:, :], compare_op=ALU.not_equal, fill=1.0,
                                    base=0, pattern=[[-1, P]], channel_multiplier=1).then_inc(consts_ready, 1)
            step(nc.gpsimd.memset(ones[:, :], 1.0))
            step(nc.gpsimd.affine_select(out=before[:, :], in_=ones[:, :], compare_op=ALU.is_gt, fill=0.0,
                                         base=0, pattern=[[1, P]], channel_multiplier=-1))
            step(nc.gpsimd.memset(mean_of[:, :], 1.0 / D))
            step(nc.gpsimd.memset(u_pad[:, :, 0:W - 1], 0.0))
            step(nc.gpsimd.iota(slot_no_i[:, :], pattern=[[1, SLOTS]], base=0, channel_multiplier=0))
            step(nc.gpsimd.tensor_copy(slot_no[:, :], slot_no_i[:, :]))
            step(nc.gpsimd.tensor_scalar(desc[:, :], slot_no[:, 0:EG], -1.0, float(EG), ALU.mult, ALU.add))
            step(nc.gpsimd.memset(causal[:, :], 0.0))
            for c in (0, 2):
                step(nc.gpsimd.affine_select(out=causal[:, c * P:(c + 1) * P], in_=causal[:, c * P:(c + 1) * P],
                                             compare_op=ALU.is_ge, fill=NEG, base=0, pattern=[[-1, P]],
                                             channel_multiplier=1))
            inv = 1.0 / (np.float32(10000.0) ** (np.arange(0, ROPE, 2, dtype=np.float32) / np.float32(ROPE)))
            for i in range(ROPE // 2):
                step(nc.gpsimd.memset(rope_t[:, 0, :, i:i + 1], float(np.float32(inv[i]))))
            nc.gpsimd.memset(stat[:, 63:64], EPS).then_inc(consts_ready, 1)
            pool.wait_ge(row_landed, 16)
            for t in range(TT):
                pool.wait_ge(normed, t + 1)
                nc.gpsimd.tensor_tensor(h[:, t, :], h[:, t, :], bcast_row[:, :], ALU.add).then_inc(bias_added, 1)

        @block.scalar
        def _(act):
            def copy(dst, src):
                return nc.scalar.activation(dst, src, ACT.Copy)

            act.dma_start(h[:, :, :], A["x"][0].rearrange("(t p) d -> p t d", p=P)).then_inc(x_landed, 16)
            act.wait_ge(pool_step, 1)
            rows = [(prm_a[R_MIX:R_MIX + 2, :], A["norm_mix"]), (prm_a[R_XA:R_XA + 2, :], A["norm_xa"]),
                    (prm_a[R_MEM:R_MEM + 2, :], A["norm_mem"]), (prm_a[R_FFN:R_FFN + 2, :], A["norm_ffn"]),
                    (prm_b[0:W, :], A["conv_w_dw"][0]),
                    (prm_b[R_BDW:R_BDW + 1, :], A["conv_b_dw"]),
                    (prm_b[R_LNG:R_LNG + 1, :], A["conv_ln_g"]),
                    (prm_b[R_LNB:R_LNB + 1, :], A["conv_ln_b"]),
                    (prm_b[R_BA:R_BG + 1, :], A["conv_b_in"][0].rearrange("(r n) -> r n", r=2)),
                    (prm_b[R_QN:R_QN + 1, 0:QR], A["mla_q_norm"]),
                    (prm_b[R_KVN:R_KVN + 1, 0:KVR], A["mla_kv_norm"])]
            for dst, src in rows:
                act.dma_start(dst, src).then_inc(prm_landed, 16)
            act.dma_start(mem_rows, A["mem"][0].rearrange("(t p) d -> p t d", p=P)).then_inc(mem_landed, 16)
            act.dma_start(bcast_row[:, :], A["conv_b_out"].partition_broadcast(P)).then_inc(row_landed, 16)
            act.dma_start(pos_i[:, :], A["positions"][0].rearrange("(t p) -> p t", p=P),
                          allow_slow_non_contiguous=True).then_inc(small_landed, 16)
            for l in range(2):
                act.dma_start(router[:, l, :, 0:G], A["moe_w_grp"][l].rearrange("(p k) n -> p k n", k=KD),
                              allow_slow_non_contiguous=True).then_inc(small_landed, 16)
                act.dma_start(router[:, l, :, G:], A["moe_w_exp"][l].rearrange("(p k) n -> p k n", k=KD),
                              allow_slow_non_contiguous=True).then_inc(small_landed, 16)
                act.dma_start(router_b[:, l, 0:G], A["moe_b_grp"][l:l + 1, :].partition_broadcast(P)).then_inc(small_landed, 16)
                act.dma_start(router_b[:, l, G:], A["moe_b_exp"][l:l + 1, :].partition_broadcast(P)).then_inc(small_landed, 16)

            n_steps = 0

            def root_mean_square(src, c, n, junk):
                nonlocal n_steps
                n_steps += 1
                nc.scalar.activation(junk, src, ACT.Square, accum_out=c).then_inc(act_step, 1)
                act.wait_ge(act_step, n_steps)
                return nc.scalar.activation(c, c, ACT.Sqrt, bias=stat[:, 63:64], scale=1.0 / n)

            def rms(i, src, t, junk):
                root_mean_square(src, stat[:, 2 * i + t + 1:2 * i + t + 2], D, junk).then_inc(rms_ready, 1)

            def gained(name, row):
                for j in (1, 3):
                    b = wait_filled(act, f"{name}_{j}")
                    for q in range(2):
                        k = 2 * j + q
                        ins = nc.scalar.activation(hT[:, k, :], b[:, q * T:(q + 1) * T], ACT.Copy,
                                                   scale=gain_of[:, k, row:row + 1])
                    evac(ins, f"{name}_{j}")

            act.wait_ge(x_landed, 16)
            act.wait_ge(consts_ready, 3)
            for t in range(TT):
                rms(0, h[:, t, :], t, xhat[:, t, :])
            act.wait_ge(mem_landed, 16)
            for t in range(TT):
                rms(1, mem_rows[:, t, :], t, kv0[:, t * D:(t + 1) * D])
            wait_evac(act, "prm")
            gained("n0", R_MIX)
            for j in (1, 3):
                b = wait_filled(act, f"mem_{j}")
                for q in range(2):
                    k = 2 * j + q
                    for l in range(2):
                        ins = nc.scalar.activation(memT[l][:, k, :], b[:, q * NMEM:(q + 1) * NMEM], ACT.Copy,
                                                   scale=gain_of[:, k, R_MEM + l:R_MEM + l + 1])
                evac(ins, f"mem_{j}")
            for j in range(KD):
                b = wait_filled(act, f"glu_{j}")
                if j >= 2:
                    wait_evac(act, f"glu_{j - 2}")
                nc.scalar.activation(sig[:, j % 2, :], b[:, T:2 * T], ACT.Sigmoid,
                                     bias=conv_of[:, j, R_BG:R_BG + 1]).then_inc(sig_ready, 1)
            for l in range(2):
                for j in range(4):
                    b = wait_filled(act, f"xk{l}_{j}")
                    evac(copy(xkT[l][:, 2 * j:2 * j + 2, :], b[:, :].rearrange("p (a b) -> p a b", a=2)), f"xk{l}_{j}")
                for f in range(NH):
                    for t in range(TT):
                        b = wait_filled(act, f"xv{l}_{f}_{t}")
                        evac(copy(xv[l][:, t, f * HALF:(f + 1) * HALF], b[:, :]), f"xv{l}_{f}_{t}")
            for q in range(2):
                act.wait_ge(centred, q + 1)
                nc.scalar.activation(conv_sq[:, 4 * q:4 * q + 4, :], conv[:, 4 * q:4 * q + 4, :],
                                     ACT.Square).then_inc(squared, 1)
            b = wait_filled(act, "var")
            evac(nc.scalar.activation(ln_rstd, b[:, 0:T], ACT.Sqrt, bias=stat[:, 63:64]), "var")
            for j in range(KD):
                act.wait_ge(ln_scaled, j // 4 + 1)
                nc.scalar.activation(hT[:, j, :], conv[:, j, :], ACT.Silu, bias=conv_of[:, j, R_LNB:R_LNB + 1],
                                     scale=conv_of[:, j, R_LNG:R_LNG + 1]).then_inc(conv_act, 1)

            def cross(l):
                i = 2 if l == 0 else 5
                prev = "cout" if l == 0 else "mw"
                for t in range(TT):
                    wait_evac(act, f"{prev}_{NH - 1}_{t}")
                    rms(i, h[:, t, :], t, xhat[:, t, :])
                gained(f"nx{l}", R_XA + l)
                for j in (1, 3):
                    b = wait_filled(act, f"xq{l}_{j}")
                    evac(copy(xqT[:, 2 * j:2 * j + 2, :], b[:, :].rearrange("p (a b) -> p a b", a=2)), f"xq{l}_{j}")
                for hd in range(XH):
                    act.wait_ge(x_max_ready, XH * l + hd + 1)
                    b = wait_filled(act, f"xs{l}_{hd}")
                    for t in range(TT):
                        c = 32 + 2 * hd + t
                        ins = nc.scalar.activation(xprob[:, hd, t, :], b[:, t * NMEM:(t + 1) * NMEM], ACT.Exp,
                                                   bias=stat[:, c:c + 1], scale=XSCALE,
                                                   accum_out=stat[:, c + 8:c + 9])
                    evac(ins, f"xs{l}_{hd}")
                for hd in range(XH):
                    b = wait_filled(act, f"xp{l}_{hd}")
                    evac(copy(xprobT[:, hd % 2, :], b[:, :]), f"xp{l}_{hd}")

            def route(l):
                i = 3 if l == 0 else 6
                for t in range(TT):
                    wait_evac(act, f"xw{l}_{NH - 1}_{t}")
                    rms(i, h[:, t, :], t, xhat[:, t, :])
                gained(f"nf{l}", R_FFN + l)
                act.wait_ge(route_diff, 2 * l + 1)
                nc.scalar.activation(rt[:, 8:16], rt[:, 0:8], ACT.Exp).then_inc(route_exp, 1)
                act.wait_ge(route_diff, 2 * l + 2)
                nc.scalar.activation(rt[:, 18:20], rt[:, 16:18], ACT.Exp).then_inc(route_exp, 1)

            def experts(s, turn):
                l = s.l

                def gate(j):
                    b = wait_filled(act, f"m{l}gu{j}", turn, s)
                    nc.scalar.activation(gated[:, j % 2, :], b[:, 0:FF], ACT.Silu).then_inc(s.gate_ready, 1)

                def puts(q):
                    b = wait_filled(act, f"m{l}st{q}", turn, s)
                    evac(copy(put[:, 2 * q:2 * q + 2, :, :].rearrange("p a t s -> p (a t s)"), b[:, :]), f"m{l}st{q}", s)

                def mid(j):
                    b = wait_filled(act, f"m{l}ht{j}", turn, s)
                    evac(copy(hmidT.rearrange("p a b -> p (a b)"), b[:, 0:2 * P]), f"m{l}ht{j}", s)

                def y(j):
                    b = wait_filled(act, f"m{l}yd{j}_1", turn, s)
                    evac(copy(yslot[:, j % 2, HALF:], b[:, :]), f"m{l}yd{j}_1", s)

                for k in range(1, KD, 2):
                    b = wait_filled(act, f"m{l}ga{k}", turn, s)
                    evac(nc.scalar.activation(xg[:, k, :], b[:, :], ACT.Copy,
                                              scale=gain_of[:, k, R_FFN + l:R_FFN + l + 1]), f"m{l}ga{k}", s)
                gate(0)
                gate(1)
                puts(0)
                mid(0)
                y(0)
                gate(2)
                mid(1)
                y(1)
                gate(3)
                puts(1)
                mid(2)
                y(2)
                mid(3)
                y(3)

            def moe(l):
                a, b = sweeps[l]
                with act.Fori(0, TURNS) as turn:
                    experts(a, turn)
                act.wait_ge(routed, l + 1)
                n = act.value_load(most[0:1, l:l + 1], min_val=0, max_val=T)
                with act.If(n > SLOTS):
                    wait_evac(act, f"m{l}yd3_1", TURNS - 1)
                    act.sem_inc(b.act, TL_ACT)
                    with act.Fori(0, 3) as r:
                        with act.Fori(0, TURNS) as turn:
                            experts(b, r * TURNS + turn)
                    wait_evac(act, f"m{l}sc1_{NH - 1}_{TT - 1}", 3 * TURNS - 1, b)

            cross(0)
            route(0)
            moe(0)

            for t in range(TT):
                wait_evac(act, f"m0sc1_{NH - 1}_{t}", TURNS - 1)
                rms(4, h[:, t, :], t, xhat[:, t, :])
            act.wait_ge(angles_ready, 1)
            for q in range(2):
                nc.scalar.activation(rope_t[:, 4 + q, :, :], rope_t[:, 2 + q, :, :], ACT.Sin).then_inc(sincos_ready, 1)
            gained("n4", R_MIX + 1)
            for t in range(TT):
                b = wait_filled(act, f"dnA_{t}")
                evac(copy(down[:, t, 0:HALF], b[:, :]), f"dnA_{t}")
            for t in range(TT):
                b = wait_filled(act, f"dnB_{t}")
                evac(copy(down[:, t, HALF:DOWN], b[:, 0:DOWN - HALF]), f"dnB_{t}")
            for t in range(TT):
                wait_evac(act, f"dnB_{t}")
                for q, (c0, c1) in enumerate(((0, QR), (QR, QR + KVR))):
                    root_mean_square(down[:, t, c0:c1], stat[:, 52 + 2 * t + q:53 + 2 * t + q], c1 - c0,
                                     squares_junk[:, 2 * t + q, 0:c1 - c0]).then_inc(down_rms_ready, 1)
            b = wait_filled(act, "cT_1")
            nc.scalar.activation(cT[:, 2, :], b[:, 0:T], ACT.Copy, scale=conv_of[:, 2, R_QN:R_QN + 1])
            evac(nc.scalar.activation(cT[:, 3, :], b[:, T:2 * T], ACT.Copy, scale=conv_of[:, 0, R_KVN:R_KVN + 1]), "cT_1")
            for n in range(3):
                for t in range(TT):
                    b = wait_filled(act, f"uq_{n}_{t}")
                    evac(copy(qtok[:, t, n * HALF:(n + 1) * HALF], b[:, :]), f"uq_{n}_{t}")

            def heads(name, dst):
                for j in range(1, H // 2, 2):
                    b = wait_filled(act, f"{name}_{j}")
                    evac(copy(dst[0:QKD, 2 * j:2 * j + 2, :], b[0:QKD, :].rearrange("p (a b) -> p a b", a=2)), f"{name}_{j}")

            heads("qT", qhT)
            for n in range(4):
                b = wait_filled(act, f"ukv_{n}_1")
                src = b[:, :].rearrange("p (h c) -> p h c", h=4)
                copy(ktok[:, 1, :].rearrange("p (h c) -> p h c", h=H)[:, 4 * n:4 * n + 4, 0:NOPE], src[:, :, 0:NOPE])
                evac(copy(vtok[:, 1, 4 * n * VD:4 * (n + 1) * VD].rearrange("p (h c) -> p h c", h=4), src[:, :, NOPE:]), f"ukv_{n}_1")
            heads("kT", khT)
            SPANS = [(0, P), (P, 3 * P)]

            def m_exp(hd):
                act.wait_ge(m_max_ready, hd + 1)
                for t in range(TT):
                    c = 32 + 4 * (hd % 2) + t
                    a0, a1 = SPANS[t]
                    ins = nc.scalar.activation(prob[:, hd % 2, a0:a1], score[:, hd % 2, a0:a1], ACT.Exp,
                                               bias=stat[:, c:c + 1], scale=MSCALE, accum_out=stat[:, c + 2:c + 3])
                ins.then_inc(m_exp_ready, 1)

            m_exp(0)
            for hd in range(H):
                if hd + 1 < H:
                    if hd >= 1:
                        wait_filled(act, f"mp_{hd - 1}")
                    m_exp(hd + 1)
                b = wait_filled(act, f"mp_{hd}")
                if hd >= 2:
                    wait_filled(act, f"mo_{hd // 2 - 1}")
                evac(copy(probT[:, hd % 2, :], b[:, 0:3 * P]), f"mp_{hd}")
                if hd % 2:
                    b = wait_filled(act, f"mo_{hd // 2}")
                    evac(copy(hT[:, hd // 2, :], b[:, 0:T]), f"mo_{hd // 2}")
            act.dma_start(bcast_row[:, :], A["final_norm"].rearrange("(a n) -> a n", a=1).partition_broadcast(P)).then_inc(row_landed, 16)
            cross(1)
            route(1)
            moe(1)
            for t in range(TT):
                wait_evac(act, f"m1sc1_{NH - 1}_{t}", TURNS - 1)
                rms(7, h[:, t, :], t, xhat[:, t, :])

        @block.vector
        def _(dve):
            v = nc.vector
            n_steps = 0

            def mark(ins):
                nonlocal n_steps
                n_steps += 1
                ins.then_inc(dve_step, 1)
                return n_steps

            def step(ins):
                dve.wait_ge(dve_step, mark(ins))

            def norm(i, src, dst):
                for t in range(TT):
                    c = stat[:, 2 * i + t + 1:2 * i + t + 2]
                    dve.wait_ge(rms_ready, 2 * i + t + 1)
                    step(v.reciprocal(c, c))
                    v.tensor_scalar(dst[:, t, :], src[:, t, :], c, None, ALU.mult).then_inc(normed, 1)

            def gained(name, row):
                for j in (0, 2):
                    b = wait_filled(dve, f"{name}_{j}")
                    for q in range(2):
                        k = 2 * j + q
                        ins = v.tensor_scalar(hT[:, k, :], b[:, q * T:(q + 1) * T], gain_of[:, k, row:row + 1], None, ALU.mult)
                    evac(ins, f"{name}_{j}")

            def add_residual(name):
                for f in range(NH):
                    for t in range(TT):
                        b = wait_filled(dve, f"{name}_{f}_{t}")
                        s = h[:, t, f * HALF:(f + 1) * HALF]
                        evac(v.tensor_tensor(s, s, b[:, :], ALU.add), f"{name}_{f}_{t}")

            b = wait_filled(dve, "prm")
            evac(v.tensor_copy(prmT[:, :], b[:, 0:KD * (NA_ROWS + NB_ROWS)]), "prm")
            norm(0, h, xhat)
            norm(1, mem_rows, mem_rows)
            wait_evac(dve, "prm")
            gained("n0", R_MIX)
            for j in (0, 2):
                b = wait_filled(dve, f"mem_{j}")
                for q in range(2):
                    k = 2 * j + q
                    for l in range(2):
                        ins = v.tensor_scalar(memT[l][:, k, :], b[:, q * NMEM:(q + 1) * NMEM],
                                              gain_of[:, k, R_MEM + l:R_MEM + l + 1], None, ALU.mult)
                evac(ins, f"mem_{j}")

            dve.wait_ge(small_landed, 16 * 9)
            dve.wait_ge(consts_ready, 3)
            ang, full, r, rc = (rope_t[:, q, :, :] for q in range(4))
            posf = stat[:, 50:50 + TT]
            step(v.tensor_copy(posf, pos_i[:, :]))
            step(v.tensor_tensor(full, ang, posf.unsqueeze(2).to_broadcast([P, TT, ROPE // 2]), ALU.mult))
            step(v.tensor_scalar(ang, full, float(1.0 / (2 * np.pi)), None, ALU.mult))
            step(v.tensor_copy(rope_i[:, :, :], ang))
            step(v.tensor_copy(ang, rope_i[:, :, :]))
            c1 = 6.28125
            c2 = float(np.float32(np.float64(2 * np.pi) - c1))
            c3 = float(np.float64(2 * np.pi) - c1 - np.float64(np.float32(c2)))
            src = full
            for c in (c1, c2, c3):
                step(v.scalar_tensor_tensor(out=r, in0=ang, scalar=-c, in1=src, op0=ALU.mult, op1=ALU.add))
                src = r

            def wrap(x):
                for cmp, lim, add in ((ALU.is_gt, float(np.pi), -2 * np.pi), (ALU.is_lt, -float(np.pi), 2 * np.pi)):
                    step(v.tensor_scalar(ang, x, lim, float(add), cmp, ALU.mult))
                    step(v.tensor_tensor(x, x, ang, ALU.add))
                return v.tensor_scalar(x, x, 3.1415925, -3.1415925, ALU.min, ALU.max)

            step(wrap(r))
            step(v.tensor_scalar(rc, r, float(np.pi / 2), None, ALU.add))
            wrap(rc).then_inc(angles_ready, 1)
            sin_t, cos_t = rope_t[:, 4, :, :], rope_t[:, 5, :, :]

            done_tap = {}
            for m in range(KD // 2):
                for j in (2 * m, 2 * m + 1):
                    b = wait_filled(dve, f"glu_{j}")
                    dve.wait_ge(sig_ready, j + 1)
                    evac(v.scalar_tensor_tensor(out=u_pad[:, j, W - 1:], in0=b[:, 0:T], scalar=conv_of[:, j, R_BA:R_BA + 1],
                                                in1=sig[:, j % 2, :], op0=ALU.add, op1=ALU.mult), f"glu_{j}")
                for tap in range(W):
                    for j in (2 * m, 2 * m + 1):
                        taps = u_pad[:, j, tap:tap + T]
                        w = conv_of[:, j, tap:tap + 1]
                        if tap == 0:
                            wait_evac(dve, f"glu_{j}")
                            ins = v.tensor_scalar(conv[:, j, :], taps, w, conv_of[:, j, R_BDW:R_BDW + 1], ALU.mult, ALU.add)
                        else:
                            dve.wait_ge(dve_step, done_tap[j])
                            ins = v.scalar_tensor_tensor(out=conv[:, j, :], in0=taps, scalar=w, in1=conv[:, j, :],
                                                         op0=ALU.mult, op1=ALU.add)
                        if tap < W - 1:
                            done_tap[j] = mark(ins)
                        else:
                            ins.then_inc(conv_ready, 1)

            b = wait_filled(dve, "mu")
            dve.wait_ge(conv_ready, KD)
            for q in range(2):
                s = conv[:, 4 * q:4 * q + 4, :]
                ins = v.tensor_tensor(s, s, b[:, 0:T].unsqueeze(1).to_broadcast([P, 4, T]), ALU.subtract)
                ins.then_inc(centred, 1)
            dve.wait_ge(centred, 2)
            evac(v.tensor_copy(stat[:, 60:61], b[:, 0:1]), "mu")
            wait_evac(dve, "var")
            step(v.reciprocal(ln_rstd, ln_rstd))
            for q in range(2):
                s = conv[:, 4 * q:4 * q + 4, :]
                v.tensor_tensor(s, s, ln_rstd.unsqueeze(1).to_broadcast([P, 4, T]), ALU.mult).then_inc(ln_scaled, 1)
            dve.wait_ge(bias_added, TT)
            add_residual("cout")

            def cross(l):
                i = 2 if l == 0 else 5
                norm(i, h, xhat)
                gained(f"nx{l}", R_XA + l)
                for j in (0, 2):
                    b = wait_filled(dve, f"xq{l}_{j}")
                    evac(v.tensor_copy(xqT[:, 2 * j:2 * j + 2, :], b[:, :].rearrange("p (a b) -> p a b", a=2)), f"xq{l}_{j}")
                for hd in range(XH):
                    b = wait_filled(dve, f"xs{l}_{hd}")
                    mx = stat[:, 32 + 2 * hd:34 + 2 * hd]
                    step(v.tensor_reduce(out=mx, in_=b[:, :].rearrange("p (t m) -> p t m", t=TT), axis=AX.X, op=ALU.max))
                    v.tensor_scalar(mx, mx, -XSCALE, None, ALU.mult).then_inc(x_max_ready, 1)
                for hd in range(XH):
                    wait_evac(dve, f"xs{l}_{hd}")
                    su = stat[:, 40 + 2 * hd:42 + 2 * hd]
                    step(v.reciprocal(su, su))
                    v.tensor_tensor(xprob[:, hd, :, :], xprob[:, hd, :, :],
                                    su.unsqueeze(2).to_broadcast([P, TT, NMEM]), ALU.mult).then_inc(x_prob_ready, 1)
                for hd in range(XH):
                    b = wait_filled(dve, f"xo{l}_{hd}")
                    evac(v.tensor_copy(hT[:, 2 * hd:2 * hd + 2, :], b[:, :].rearrange("p (a b) -> p a b", a=2)), f"xo{l}_{hd}")
                add_residual(f"xw{l}")

            gdiff, gexp = view(rt, 0, TT, G), view(rt, 8, TT, G)
            ediff, eexp = rt[:, 16:18], rt[:, 18:20]
            gmax, gsum, m1, m2, best, w1, w2 = (rt[:, 20 + 2 * q:22 + 2 * q] for q in range(7))
            logit = view(rt, 40, TT, G + E)
            group = view(rt, 112, TT, G)
            eq = view(rt, 120, TT, EG)
            mine = view(rt, 136, TT, EG)
            first, second, within, chosen = (view(rt, 152 + 16 * q, TT, EG) for q in range(4))
            masked = view(rt, 216, TT, G, EG)
            taken = view(rt, 280, TT, G, EG)
            weight = view(rt, 344, TT, G, EG)
            slot = view(rt, 408, TT, E)

            def over(x, n):
                return x.unsqueeze(2).to_broadcast([P, TT, n])

            def first_of(x, top, n, onehot):
                step(v.tensor_reduce(out=top, in_=x, axis=AX.X, op=ALU.max))
                e = eq[:, :, 0:n]
                step(v.tensor_tensor(e, x, over(top, n), ALU.is_equal))
                step(v.tensor_tensor(e, e, desc[:, EG - n:EG].unsqueeze(1).to_broadcast([P, TT, n]), ALU.mult))
                step(v.tensor_reduce(out=best, in_=e, axis=AX.X, op=ALU.max))
                step(v.tensor_tensor(onehot, e, over(best, n), ALU.is_equal))

            def route(l):
                i = 3 if l == 0 else 6
                norm(i, h, xhat)
                gained(f"nf{l}", R_FFN + l)
                b = wait_filled(dve, f"lg{l}")
                evac(v.tensor_tensor(logit, b[:, 0:TT * (G + E)].rearrange("p (t n) -> p t n", t=TT),
                                     router_b[:, l:l + 1, :].to_broadcast([P, TT, G + E]), ALU.add), f"lg{l}")
                wait_evac(dve, f"lg{l}")
                first_of(logit[:, :, 0:G], gmax, G, group)
                v.tensor_tensor(gdiff, logit[:, :, 0:G], over(gmax, G), ALU.subtract).then_inc(route_diff, 1)
                step(v.tensor_tensor(masked, logit[:, :, G:].rearrange("p t (g e) -> p t g e", g=G),
                                     group.unsqueeze(3).to_broadcast([P, TT, G, EG]), ALU.mult))
                step(v.tensor_reduce(out=mine, in_=masked.rearrange("p t g e -> p t e g"), axis=AX.X, op=ALU.add))
                first_of(mine, m1, EG, first)
                step(v.scalar_tensor_tensor(out=mine, in0=first, scalar=NEG, in1=mine, op0=ALU.mult, op1=ALU.add))
                first_of(mine, m2, EG, second)
                v.tensor_tensor(ediff, m2, m1, ALU.subtract).then_inc(route_diff, 1)
                step(v.tensor_tensor(chosen, first, second, ALU.add))
                v.tensor_tensor(taken, group.unsqueeze(3).to_broadcast([P, TT, G, EG]),
                                chosen.unsqueeze(2).to_broadcast([P, TT, G, EG]), ALU.mult).then_inc(assigned, 1)
                dve.wait_ge(route_exp, 2 * l + 1)
                step(v.tensor_reduce(out=gsum, in_=gexp, axis=AX.X, op=ALU.add))
                dve.wait_ge(route_exp, 2 * l + 2)
                step(v.tensor_scalar(w1, eexp, 1.0, None, ALU.add))
                step(v.tensor_tensor(w1, w1, gsum, ALU.mult))
                step(v.reciprocal(w1, w1))
                step(v.tensor_tensor(w2, w1, eexp, ALU.mult))
                step(v.tensor_tensor(first, first, over(w1, EG), ALU.mult))
                step(v.tensor_tensor(second, second, over(w2, EG), ALU.mult))
                step(v.tensor_tensor(within, first, second, ALU.add))
                step(v.tensor_tensor(weight, group.unsqueeze(3).to_broadcast([P, TT, G, EG]),
                                     within.unsqueeze(2).to_broadcast([P, TT, G, EG]), ALU.mult))
                dve.wait_ge(assigned, l + 1)
                b = wait_filled(dve, f"rk{l}")
                flat = taken.rearrange("p t g e -> p t (g e)")
                step(v.scalar_tensor_tensor(out=slot, in0=b[:, 0:TT * E].rearrange("p (t n) -> p t n", t=TT), scalar=1.0,
                                            in1=flat, op0=ALU.add, op1=ALU.mult))
                step(v.tensor_scalar(slot, slot, -1.0, None, ALU.add))
                step(v.tensor_reduce(out=rt[:, 38:39], in_=b[:, TT * E:(TT + 1) * E], axis=AX.X, op=ALU.max))
                mark(v.tensor_copy(most[:, l:l + 1], rt[:, 38:39]))
                dve.wait_ge(dve_step, n_steps)
                evac(v.tensor_copy(rt[:, 39:40], rt[:, 38:39]), f"rk{l}")
                wait_evac(dve, f"rk{l}")
                v.tensor_copy(rt[:, 39:40], rt[:, 38:39]).then_inc(routed, 1)

            def experts(s, turn, first_expert, repeat=None):
                l = s.l
                if repeat is not None:
                    dve.wait_ge(s.shifted, repeat + 1)
                wflat = weight.rearrange("p t g e -> p t (g e)")
                for t in range(TT):
                    p3 = pick[:, t, :].rearrange("p (e s) -> p e s", e=EG)
                    v.tensor_tensor(p3, slot_no[:, :].unsqueeze(1).to_broadcast([P, EG, SLOTS]),
                                    slot[:, t, bass.ds(first_expert, EG)].unsqueeze(2).to_broadcast([P, EG, SLOTS]),
                                    ALU.is_equal).then_inc(s.picked, 1)
                for k in range(0, KD, 2):
                    b = wait_filled(dve, f"m{l}ga{k}", turn, s)
                    evac(v.tensor_scalar(xg[:, k, :], b[:, :], gain_of[:, k, R_FFN + l:R_FFN + l + 1], None, ALU.mult),
                         f"m{l}ga{k}", s)
                wait_filled(dve, f"m{l}ga{KD - 1}", turn, s)
                for t in range(TT):
                    p3 = pick[:, t, :].rearrange("p (e s) -> p e s", e=EG)
                    v.tensor_tensor(p3, p3, wflat[:, t, bass.ds(first_expert, EG)].unsqueeze(2).to_broadcast([P, EG, SLOTS]),
                                    ALU.mult).then_inc(s.weighted, 1)

                def mid(j):
                    b = wait_filled(dve, f"m{l}gu{j}", turn, s)
                    s_value = turn * (EG // 2) + (j + 1)
                    dve.wait_ge(s.gate_ready, s_value)
                    evac(v.tensor_tensor(hmid[:, j % 2, :], gated[:, j % 2, :], b[:, FF:2 * FF], ALU.mult), f"m{l}gu{j}", s)

                def y(j):
                    b = wait_filled(dve, f"m{l}yd{j}_0", turn, s)
                    evac(v.tensor_copy(yslot[:, j % 2, 0:HALF], b[:, :]), f"m{l}yd{j}_0", s)

                def scatter(q):
                    for f in range(NH):
                        for t in range(TT):
                            name = f"m{l}sc{q}_{f}_{t}"
                            b = wait_filled(dve, name, turn, s)
                            c = h[:, t, f * HALF:(f + 1) * HALF]
                            dve.wait_ge(s.dve, evac_value(s, name, turn) - 1)
                            evac(v.tensor_tensor(c, c, b[:, :], ALU.add), name, s)

                mid(0)
                mid(1)
                y(0)
                mid(2)
                y(1)
                mid(3)
                scatter(0)
                y(2)
                y(3)
                scatter(1)

            def moe(l):
                a, b = sweeps[l]
                dve.wait_ge(routed, l + 1)
                with dve.Fori(0, TURNS) as turn:
                    experts(a, turn, turn * EG)
                n = dve.value_load(most[0:1, l:l + 1], min_val=0, max_val=T)
                with dve.If(n > SLOTS):
                    wait_evac(dve, f"m{l}sc1_{NH - 1}_{TT - 1}", TURNS - 1)
                    dve.sem_inc(b.dve, TL_DVE)
                    with dve.Fori(0, 3) as r:
                        v.tensor_scalar(slot, slot, -float(SLOTS), None, ALU.add).then_inc(b.shifted, 1)
                        with dve.Fori(0, TURNS) as turn:
                            experts(b, r * TURNS + turn, turn * EG, r)
                    wait_evac(dve, f"m{l}sc1_{NH - 1}_{TT - 1}", 3 * TURNS - 1, b)

            cross(0)
            route(0)
            moe(0)

            norm(4, h, xhat)
            gained("n4", R_MIX + 1)
            for t in range(TT):
                dve.wait_ge(down_rms_ready, 2 * (t + 1))
                c = stat[:, 52 + 2 * t:54 + 2 * t]
                step(v.reciprocal(c, c))
                for q, (c0, c1) in enumerate(((0, QR), (QR, QR + KVR))):
                    part = down[:, t, c0:c1]
                    ins = v.tensor_scalar(part, part, c[:, q:q + 1], None, ALU.mult)
                ins.then_inc(down_ready, 1)
            dve.wait_ge(sincos_ready, 2)
            kr = down[:, :, QR + KVR:DOWN]
            HR = ROPE // 2

            def rotate(x1, x2, cs, sn, tmp):
                a, b_, c_, d_ = tmp
                v.tensor_tensor(a, x1, cs, ALU.mult)
                v.tensor_tensor(b_, x2, sn, ALU.mult)
                v.tensor_tensor(c_, x2, cs, ALU.mult)
                step(v.tensor_tensor(d_, x1, sn, ALU.mult))
                v.tensor_tensor(x1, a, b_, ALU.subtract)
                return v.tensor_tensor(x2, c_, d_, ALU.add)

            step(rotate(kr[:, :, 0:HR], kr[:, :, HR:ROPE], cos_t, sin_t, [rope_tmp[:, q, :, 0, :] for q in range(4)]))
            for j in (0, 2):
                b = wait_filled(dve, f"cT_{j}")
                ins = v.tensor_scalar(cT[:, 2 * j, :], b[:, 0:T], conv_of[:, 0 if j == 0 else 1, (R_QN if j == 0 else R_KVN):(R_QN if j == 0 else R_KVN) + 1], None, ALU.mult)
                if j == 0:
                    ins = v.tensor_scalar(cT[:, 1, :], b[:, T:2 * T], conv_of[:, 1, R_QN:R_QN + 1], None, ALU.mult)
                evac(ins, f"cT_{j}")
            wait_evac(dve, "uq_2_1")
            qh = qtok.rearrange("p t (h c) -> p t h c", h=H)
            for t in range(TT):
                cs = cos_t[:, t, :].unsqueeze(1).to_broadcast([P, H, HR])
                sn = sin_t[:, t, :].unsqueeze(1).to_broadcast([P, H, HR])
                rotate(qh[:, t, :, NOPE:NOPE + HR], qh[:, t, :, NOPE + HR:QKD], cs, sn,
                       [rope_tmp[:, q, t, :, :] for q in range(4)]).then_inc(roped, 1)

            def heads(name, dst):
                for j in range(0, H // 2, 2):
                    b = wait_filled(dve, f"{name}_{j}")
                    evac(v.tensor_copy(dst[0:QKD, 2 * j:2 * j + 2, :], b[0:QKD, :].rearrange("p (a b) -> p a b", a=2)), f"{name}_{j}")

            heads("qT", qhT)
            kh = ktok.rearrange("p t (h c) -> p t h c", h=H)
            wait_filled(dve, f"qT_{H // 2 - 1}")
            for t in range(TT):
                v.tensor_copy(kh[:, t, :, NOPE:QKD], kr[:, t, :].unsqueeze(1).to_broadcast([P, H, ROPE])).then_inc(ktok_ready, 1)
            for n in range(4):
                b = wait_filled(dve, f"ukv_{n}_0")
                src = b[:, :].rearrange("p (h c) -> p h c", h=4)
                v.tensor_copy(kh[:, 0, 4 * n:4 * n + 4, 0:NOPE], src[:, :, 0:NOPE])
                evac(v.tensor_copy(vtok[:, 0, 4 * n * VD:4 * (n + 1) * VD].rearrange("p (h c) -> p h c", h=4), src[:, :, NOPE:]), f"ukv_{n}_0")
            heads("kT", khT)

            def m_max(hd):
                b = wait_filled(dve, f"ms_{hd}")
                sc = score[:, hd % 2, :]
                evac(v.tensor_tensor(sc, b[:, 0:3 * P], causal[:, :], ALU.add), f"ms_{hd}")
                wait_evac(dve, f"ms_{hd}")
                c = 32 + 4 * (hd % 2)
                v.tensor_reduce(out=stat[:, c:c + 1], in_=sc[:, 0:P], axis=AX.X, op=ALU.max)
                step(v.tensor_reduce(out=stat[:, c + 1:c + 2], in_=sc[:, P:3 * P], axis=AX.X, op=ALU.max))
                v.tensor_scalar(stat[:, c:c + 2], stat[:, c:c + 2], -MSCALE, None, ALU.mult).then_inc(m_max_ready, 1)

            m_max(0)
            for hd in range(H):
                if hd + 1 < H:
                    if hd >= 1:
                        dve.wait_ge(m_exp_ready, hd)
                        dve.wait_ge(m_prob_ready, hd)
                    m_max(hd + 1)
                dve.wait_ge(m_exp_ready, hd + 1)
                c = 34 + 4 * (hd % 2)
                step(v.reciprocal(stat[:, c:c + 2], stat[:, c:c + 2]))
                pr = prob[:, hd % 2, :]
                v.tensor_scalar(pr[:, 0:P], pr[:, 0:P], stat[:, c:c + 1], None, ALU.mult)
                v.tensor_scalar(pr[:, P:3 * P], pr[:, P:3 * P], stat[:, c + 1:c + 2], None, ALU.mult).then_inc(m_prob_ready, 1)
            add_residual("mw")
            cross(1)
            route(1)
            moe(1)
            dve.wait_ge(row_landed, 32)
            for t in range(TT):
                i = 7
                c = stat[:, 2 * i + t + 1:2 * i + t + 2]
                dve.wait_ge(rms_ready, 2 * i + t + 1)
                step(v.reciprocal(c, c))
                v.scalar_tensor_tensor(out=xhat[:, t, :], in0=h[:, t, :], scalar=c, in1=bcast_row[:, :],
                                       op0=ALU.mult, op1=ALU.mult).then_inc(normed, 1)

        @block.tensor
        def _(pe):
            mm = nc.tensor.matmul

            def fill(ins):
                ins.then_inc(bank_filled, 1)

            def turn_rows(name, rows):
                for j in range(4):
                    b = open_bank(pe, f"{name}_{j}")
                    for q in range(2):
                        for t in range(TT):
                            k = 2 * j + q
                            ins = nc.tensor.transpose(b[:, q * T + t * P:q * T + (t + 1) * P], rows[:, t, k::KD], ident[:, :])
                    fill(ins)

            def channel_major(name, u0, src):
                for j in range(4):
                    b = open_bank(pe, f"{name}_{j}")
                    wait_unit(pe, u0 + j)
                    w = unit(u0 + j, KD, 256)
                    for q in range(2):
                        for k in range(KD):
                            ins = mm(b[:, q * T:(q + 1) * T], lhsT=w[:, k, q * P:(q + 1) * P], rhs=src[:, k, :],
                                     start=(k == 0), stop=(k == KD - 1))
                    fill(ins)

            def token_major(name, u0, src, nk=KD, per=4, cols=HALF, parts=NH):
                for f in range(parts):
                    for t in range(TT):
                        b = open_bank(pe, f"{name}_{f}_{t}")
                        for k in range(nk):
                            u = u0 + f * (nk // per) + k // per
                            if t == 0 and k % per == 0:
                                wait_unit(pe, u)
                            ins = mm(b[:, 0:cols], lhsT=src[:, k, t * P:(t + 1) * P], rhs=unit(u, per, cols)[:, k % per, :],
                                     start=(k == 0), stop=(k == nk - 1))
                        fill(ins)

            pe.wait_ge(consts_ready, 2)
            pe.wait_ge(prm_landed, 16 * 11)
            b = open_bank(pe, "prm")
            for k in range(KD):
                nc.tensor.transpose(b[:, k * NA_ROWS:(k + 1) * NA_ROWS], prm_a[:, k::KD], ident[0:NA_ROWS, 0:NA_ROWS])
            o = KD * NA_ROWS
            for k in range(KD):
                ins = nc.tensor.transpose(b[:, o + k * NB_ROWS:o + (k + 1) * NB_ROWS], prm_b[:, k * P:(k + 1) * P],
                                          ident[0:NB_ROWS, 0:NB_ROWS])
            fill(ins)
            pe.wait_ge(normed, 2)
            turn_rows("n0", xhat)
            pe.wait_ge(normed, 4)
            turn_rows("mem", mem_rows)

            for j in (2, 3):
                wait_evac(pe, f"n0_{j}")
            for j in range(KD):
                b = open_bank(pe, f"glu_{j}")
                for part in range(2):
                    i = U_CIN + 2 * (j // 2) + part
                    if j % 2 == 0:
                        wait_unit(pe, i)
                    w = unit(i, KD, 256)
                    c = (j % 2) * P
                    for k in range(KD):
                        ins = mm(b[:, part * T:(part + 1) * T], lhsT=w[:, k, c:c + P], rhs=hT[:, k, :],
                                 start=(k == 0), stop=(k == KD - 1))
                fill(ins)
            for j in (2, 3):
                wait_evac(pe, f"mem_{j}")
            for l in range(2):
                channel_major(f"xk{l}", U_KV[l], memT[l])
                token_major(f"xv{l}", U_KV[l] + 4, memT[l])
            b = open_bank(pe, "mu")
            for k in range(KD):
                pe.wait_ge(conv_ready, k + 1)
                ins = mm(b[:, 0:T], lhsT=mean_of[:, :], rhs=conv[:, k, :], start=(k == 0), stop=(k == KD - 1))
            fill(ins)
            b = open_bank(pe, "var")
            for k in range(KD):
                pe.wait_ge(squared, k // 4 + 1)
                ins = mm(b[:, 0:T], lhsT=mean_of[:, :], rhs=conv_sq[:, k, :], start=(k == 0), stop=(k == KD - 1))
            fill(ins)
            pe.wait_ge(conv_act, KD)
            token_major("cout", U_COUT, hT)

            def cross(l):
                i = 2 if l == 0 else 5
                pe.wait_ge(normed, 2 * i + 2)
                turn_rows(f"nx{l}", xhat)
                for j in (2, 3):
                    wait_evac(pe, f"nx{l}_{j}")
                channel_major(f"xq{l}", U_XQ[l], hT)
                for j in (2, 3):
                    wait_evac(pe, f"xq{l}_{j}")
                for hd in range(XH):
                    b = open_bank(pe, f"xs{l}_{hd}")
                    for t in range(TT):
                        for c in range(2):
                            ins = mm(b[:, t * NMEM:(t + 1) * NMEM], lhsT=xqT[:, 2 * hd + c, t * P:(t + 1) * P],
                                     rhs=xkT[l][:, 2 * hd + c, :], start=(c == 0), stop=(c == 1))
                    fill(ins)

                def probs_turned(hd):
                    b = open_bank(pe, f"xp{l}_{hd}")
                    pe.wait_ge(x_prob_ready, XH * l + hd + 1)
                    for c in range(2):
                        for t in range(TT):
                            ins = nc.tensor.transpose(b[:, c * T + t * P:c * T + (t + 1) * P],
                                                      xprob[:, hd, t, c * P:(c + 1) * P], ident[:, :])
                    fill(ins)

                for hd in range(XH):
                    probs_turned(hd)
                    b = open_bank(pe, f"xo{l}_{hd}")
                    wait_evac(pe, f"xp{l}_{hd}")
                    for c in range(2):
                        for m in range(2):
                            ins = mm(b[:, c * T:(c + 1) * T], lhsT=xv[l][:, m, hd * XHD + c * P:hd * XHD + (c + 1) * P],
                                     rhs=xprobT[:, hd % 2, m * T:(m + 1) * T], start=(m == 0), stop=(m == 1))
                    fill(ins)
                wait_evac(pe, f"xo{l}_{XH - 1}")
                token_major(f"xw{l}", U_XO[l], hT)

            def route(l):
                i = 3 if l == 0 else 6
                pe.wait_ge(normed, 2 * i + 2)
                turn_rows(f"nf{l}", xhat)
                for j in (2, 3):
                    wait_evac(pe, f"nf{l}_{j}")
                pe.wait_ge(small_landed, 16 * 9)
                b = open_bank(pe, f"lg{l}")
                n = G + E
                for t in range(TT):
                    for k in range(KD):
                        ins = mm(b[:, t * n:(t + 1) * n], lhsT=hT[:, k, t * P:(t + 1) * P], rhs=router[:, l, k, :],
                                 start=(k == 0), stop=(k == KD - 1))
                fill(ins)
                pe.wait_ge(assigned, l + 1)
                taken = [rt[:, 280 + t * E:280 + (t + 1) * E] for t in range(TT)]
                b = open_bank(pe, f"rk{l}")
                mm(b[:, 0:E], lhsT=before[:, :], rhs=taken[0], start=True, stop=True)
                mm(b[:, E:2 * E], lhsT=ones[:, :], rhs=taken[0], start=True, stop=False)
                mm(b[:, E:2 * E], lhsT=before[:, :], rhs=taken[1], start=False, stop=True)
                mm(b[:, 2 * E:3 * E], lhsT=ones[:, :], rhs=taken[0], start=True, stop=False)
                ins = mm(b[:, 2 * E:3 * E], lhsT=ones[:, :], rhs=taken[1], start=False, stop=True)
                fill(ins)

            def experts(s, turn):
                l = s.l

                def ready(banks_of, copies_of=()):
                    return wait_in_turn(pe, s, turn, banks_of, copies_of)

                def filled(ins):
                    ins.then_inc(s.filled, 1)

                def landed(u):
                    i = s.unit0 + u
                    slot = i % RING
                    pe.wait_ge(s.landed[slot], turn * (16 * GU // RING) + 16 * (i // RING + 1 - s.first_use[slot]))
                    return slot

                pe.wait_ge(s.picked, turn * TT + TT)
                for k in range(KD):
                    b, = ready([f"ga{k}"])
                    for t in range(TT):
                        ins = mm(b[:, :], lhsT=xhat[:, t, k::KD], rhs=pick[:, t, :], start=(t == 0), stop=(t == TT - 1))
                    filled(ins)

                def gate_up(j):
                    b, = ready([f"gu{j}"], [f"ga{KD - 2}", f"ga{KD - 1}"] if j == 0 else [])
                    w = []
                    for e in range(2):
                        slot = landed(6 * j + 2 * e)
                        landed(6 * j + 2 * e + 1)
                        w.append(ring[:, slot * UNIT:(slot + 2) * UNIT].rearrange("p (g k n) -> p g k n", g=2, k=KD))
                    for k in range(KD):
                        for e in range(2):
                            c = (2 * j + e) * SLOTS
                            ins = mm(b[e * SLOTS:(e + 1) * SLOTS, :].rearrange("p (g n) -> p g n", g=2),
                                     lhsT=xg[:, k, c:c + SLOTS], rhs=w[e][:, :, k, :],
                                     start=(k == 0), stop=(k == KD - 1), skip_group_check=True)
                    filled(ins)

                def puts(q):
                    pe.wait_ge(s.weighted, turn * TT + TT)
                    b, = ready([f"st{q}"])
                    for jj in range(2):
                        for t in range(TT):
                            c = (2 * q + jj) * P
                            ins = nc.tensor.transpose(b[:, (jj * TT + t) * P:(jj * TT + t + 1) * P], pick[:, t, c:c + P], ident[:, :])
                    filled(ins)

                def mid(j):
                    b, = ready([f"ht{j}"], [f"gu{j}"])
                    for c in range(2):
                        ins = nc.tensor.transpose(b[:, c * P:(c + 1) * P], hmid[:, j % 2, c * P:(c + 1) * P], ident[:, :])
                    filled(ins)

                def downs(j):
                    bs = ready([f"yd{j}_{f}" for f in range(NH)], [f"ht{j}"])
                    w = [unit(landed(6 * j + 4 + e), FF // P, D) for e in range(2)]
                    for f in range(NH):
                        for c in range(FF // P):
                            for e in range(2):
                                ins = mm(bs[f][e * SLOTS:(e + 1) * SLOTS, :], lhsT=hmidT[:, c, e * SLOTS:(e + 1) * SLOTS],
                                         rhs=w[e][:, c, f * HALF:(f + 1) * HALF],
                                         start=(c == 0), stop=(c == FF // P - 1), skip_group_check=True)
                        filled(ins)

                def scatter(q):
                    copies = [f"yd{2 * q + 1}_{f}" for f in range(NH)] + [f"st{q}"]
                    for f in range(NH):
                        for t in range(TT):
                            b, = ready([f"sc{q}_{f}_{t}"], copies if f == t == 0 else [])
                            for jj in range(2):
                                ins = mm(b[:, :], lhsT=put[:, 2 * q + jj, t, :], rhs=yslot[:, jj, f * HALF:(f + 1) * HALF],
                                         start=(jj == 0), stop=(jj == 1))
                            filled(ins)

                gate_up(0)
                gate_up(1)
                puts(0)
                mid(0)
                downs(0)
                gate_up(2)
                mid(1)
                downs(1)
                gate_up(3)
                scatter(0)
                puts(1)
                mid(2)
                downs(2)
                mid(3)
                downs(3)
                scatter(1)

            def moe(l):
                a, b = sweeps[l]
                wait_evac(pe, f"rk{l}")
                wait_evac(pe, f"nf{l}_3")
                with pe.Fori(0, TURNS) as turn:
                    experts(a, turn)
                pe.wait_ge(routed, l + 1)
                n = pe.value_load(most[0:1, l:l + 1], min_val=0, max_val=T)
                with pe.If(n > SLOTS):
                    wait_filled(pe, f"m{l}sc1_{NH - 1}_{TT - 1}", TURNS - 1)
                    pe.sem_inc(b.filled, TL_ALL)
                    with pe.Fori(0, 3) as r:
                        with pe.Fori(0, TURNS) as turn:
                            experts(b, r * TURNS + turn)
                    wait_evac(pe, f"m{l}sc1_{NH - 1}_{TT - 1}", 3 * TURNS - 1, b)

            cross(0)
            route(0)
            moe(0)

            pe.wait_ge(normed, 10)
            turn_rows("n4", xhat)
            for j in (2, 3):
                wait_evac(pe, f"n4_{j}")
            for t in range(TT):
                b = open_bank(pe, f"dnA_{t}")
                for k in range(KD):
                    i = U_DOWN + k // 4
                    if t == 0 and k % 4 == 0:
                        wait_unit(pe, i)
                    ins = mm(b[:, :], lhsT=hT[:, k, t * P:(t + 1) * P], rhs=unit(i, 4, HALF)[:, k % 4, :],
                             start=(k == 0), stop=(k == KD - 1))
                fill(ins)
            wait_unit(pe, U_DOWN + 2)
            for t in range(TT):
                b = open_bank(pe, f"dnB_{t}")
                for k in range(KD):
                    ins = mm(b[:, 0:DOWN - HALF], lhsT=hT[:, k, t * P:(t + 1) * P],
                             rhs=unit(U_DOWN + 2, KD, DOWN - HALF)[:, k, :], start=(k == 0), stop=(k == KD - 1))
                fill(ins)
            pe.wait_ge(down_ready, TT)
            for j in range(3):
                b = open_bank(pe, f"cT_{j}")
                for c in (2 * j, 2 * j + 1)[:2 if j < 2 else 1]:
                    for t in range(TT):
                        o = (c % 2) * T + t * P
                        ins = nc.tensor.transpose(b[:, o:o + P], down[:, t, c * P:(c + 1) * P], ident[:, :])
                fill(ins)
            for j in range(2):
                wait_evac(pe, f"cT_{j}")
            for n in range(3):
                wait_unit(pe, U_UQ + n)
                for t in range(TT):
                    b = open_bank(pe, f"uq_{n}_{t}")
                    for k in range(3):
                        ins = mm(b[:, :], lhsT=cT[:, k, t * P:(t + 1) * P], rhs=unit(U_UQ + n, 3, HALF)[:, k, :],
                                 start=(k == 0), stop=(k == 2))
                    fill(ins)
            pe.wait_ge(roped, TT)

            def heads(name, rows):
                for j in range(H // 2):
                    b = open_bank(pe, f"{name}_{j}")
                    for q in range(2):
                        for t in range(TT):
                            c = (2 * j + q) * QKD
                            ins = nc.tensor.transpose(b[0:QKD, q * T + t * P:q * T + (t + 1) * P], rows[:, t, c:c + QKD], ident[:, :])
                    fill(ins)

            heads("qT", qtok)
            wait_evac(pe, "cT_2")
            for n in range(4):
                if n % 2 == 0:
                    wait_unit(pe, U_UKV + n // 2)
                for t in range(TT):
                    b = open_bank(pe, f"ukv_{n}_{t}")
                    for k in range(2):
                        c = (n % 2) * HALF
                        ins = mm(b[:, :], lhsT=cT[:, 3 + k, t * P:(t + 1) * P], rhs=unit(U_UKV + n // 2, 2, D)[:, k, c:c + HALF],
                                 start=(k == 0), stop=(k == 1))
                    fill(ins)
            pe.wait_ge(ktok_ready, TT)
            for t in range(TT):
                wait_evac(pe, f"ukv_3_{t}")
            heads("kT", ktok)
            for j in (H // 2 - 2, H // 2 - 1):
                wait_evac(pe, f"qT_{j}")
                wait_evac(pe, f"kT_{j}")

            def scores(hd):
                b = open_bank(pe, f"ms_{hd}")
                mm(b[:, 0:P], lhsT=qhT[0:QKD, hd, 0:P], rhs=khT[0:QKD, hd, 0:P], start=True, stop=True)
                ins = mm(b[:, P:3 * P], lhsT=qhT[0:QKD, hd, P:2 * P], rhs=khT[0:QKD, hd, :], start=True, stop=True)
                fill(ins)

            scores(0)
            scores(1)
            for hd in range(H):
                if hd + 2 < H:
                    scores(hd + 2)
                b = open_bank(pe, f"mp_{hd}")
                pe.wait_ge(m_prob_ready, hd + 1)
                for c in range(3):
                    ins = nc.tensor.transpose(b[:, c * P:(c + 1) * P], prob[:, hd % 2, c * P:(c + 1) * P], ident[:, :])
                fill(ins)
                if hd % 2:
                    b = open_bank(pe, f"mo_{hd // 2}")
                    for g in range(2):
                        hh = hd - 1 + g
                        wait_evac(pe, f"mp_{hh}")
                        o = b[g * VD:(g + 1) * VD, :]
                        mm(o[:, 0:T], lhsT=vtok[:, 0, hh * VD:(hh + 1) * VD], rhs=probT[:, g, 0:T],
                           start=True, stop=False, skip_group_check=True)
                        ins = mm(o[:, P:T], lhsT=vtok[:, 1, hh * VD:(hh + 1) * VD], rhs=probT[:, g, T:3 * P],
                                 start=False, stop=True, skip_group_check=True)
                    fill(ins)
            wait_evac(pe, f"mo_{H // 2 - 1}")
            token_major("mw", U_MO, hT)
            cross(1)
            route(1)
            moe(1)


_INS = ["x", "mem", "positions", "norm_mix", "conv_w_in", "conv_b_in", "conv_w_dw", "conv_b_dw", "conv_ln_g",
        "conv_ln_b", "conv_w_out", "conv_b_out", "mla_w_down", "mla_q_norm", "mla_w_uq", "mla_kv_norm",
        "mla_w_ukv", "mla_w_o", "norm_xa", "norm_mem", "xa_wq", "xa_wkv", "xa_wo", "norm_ffn", "moe_w_grp",
        "moe_b_grp", "moe_w_exp", "moe_b_exp", "moe_w_gate", "moe_w_up", "moe_w_down", "final_norm"]


def kernel(**inputs):
    import numpy as _np
    import concourse.bacc as _bacc
    from concourse import mybir as _mybir
    from concourse.bass_utils import run_bass_kernel_spmd as _run

    nc = _bacc.Bacc("TRN2", target_bir_lowering=False, num_devices=1)
    arrays, args = {}, {}
    for name in _INS:
        a = _np.ascontiguousarray(inputs[name])
        arrays[f"in_{name}_dram"] = a
        args[name] = nc.dram_tensor(f"in_{name}_dram", a.shape, _mybir.dt.from_np(a.dtype), kind="ExternalInput").ap()
    shape = tuple(inputs["x"].shape)
    out = nc.dram_tensor("out_0_dram", shape, _mybir.dt.from_np(_np.dtype("float32")), kind="ExternalOutput").ap()
    trunk(nc, args, out)
    r = _run(nc, [arrays], core_ids=[0])
    return r.results[0]["out_0_dram"]
```

```python
from contextlib import ExitStack

import numpy as np

import concourse.bass as bass
from concourse import mybir

F32 = mybir.dt.float32
I32 = mybir.dt.int32
ALU = mybir.AluOpType
ACT = mybir.ActivationFunctionType
AX = mybir.AxisListType

P = 128
EPS = 1e-6
NEG = -1e30
RING = 12
UNIT = 2048
SLOTS = 64
CAP = 40
NBANK = 8


class Tiles:

    def __init__(self):
        self.n = 0
        self.count = {"filled": 0, "dve": 0, "act": 0}
        self.at, self.order = {}, {}

    def add(self, name, owner):
        self.n += 1
        self.count["filled"] += 1
        self.count[owner] += 1
        self.at[name] = {"n": self.n - 1, "owner": owner, "filled": self.count["filled"], "freed": self.count[owner]}
        self.order[self.n - 1] = name


GROUP_PAIRS, GROUP_K, HALVES, TOKEN_TILES = 4, 8, 2, 2


def _down(j):
    return [(f"ht{j}", "act"), (f"yd{j}_0", "dve"), (f"yd{j}_1", "act")]


def _back(q):
    return [(f"sc{q}_{f}_{t}", "dve") for f in range(HALVES) for t in range(TOKEN_TILES)]


TURN_TILES = (
    [("st0", "act"), ("st1", "act"), ("gu1", "mid")] + _down(0) + [("gu2", "mid")] + _down(1) + [("gu3", "mid")]
    + _back(0) + _down(2) + [(f"ga{k}", ("ga_dve", "ga_act")[k % 2]) for k in range(GROUP_K)]
    + _down(3) + [("gu0", "mid")] + _back(1)
)
BANKS_A_TURN = -(-len(TURN_TILES) // NBANK) * NBANK
NEXT_TURNS = {f"ga{k}" for k in range(GROUP_K)} | {"gu0"}
PARTS = {"prologue": [x for x in TURN_TILES if x[0] in NEXT_TURNS], "turn": TURN_TILES,
         "epilogue": [x for x in TURN_TILES if x[0] not in NEXT_TURNS]}
OWNERS = ("dve", "act", "mid", "ga_dve", "ga_act")
TURN_UNITS = []
for _j in range(GROUP_PAIRS):
    if _j + 1 < GROUP_PAIRS:
        TURN_UNITS += [(w, _j + 1, e) for e in range(2) for w in ("gate", "up")]
    TURN_UNITS += [("down", _j, e) for e in range(2)]
FIRST_UNITS = [(w, 0, e) for e in range(2) for w in ("gate", "up")]
TURN_UNITS += FIRST_UNITS
EPILOGUE_UNITS = TURN_UNITS[:-len(FIRST_UNITS)]


class Place:

    def __init__(self, sweep, part, turn=None, repeat=None):
        self.s, self.part, self.turn, self.repeat = sweep, part, turn, repeat

    def nth(self, k, parts, base=0):
        p, b, e = parts
        turns = self.s.turns - 1
        a_turn = 0
        if self.part == "turn":
            k += p
            if isinstance(self.turn, int):
                k += self.turn * b
            else:
                a_turn = b
        elif self.part == "epilogue":
            k += p + turns * b
        return base + k, a_turn, 0 if self.repeat is None else p + turns * b + e

    def value(self, count):
        const, a_turn, a_repeat = count
        v = const
        if a_turn:
            v = self.turn * a_turn + v
        if a_repeat:
            v = self.repeat * a_repeat + v
        return v

    def tile(self, name):
        names = PARTS[self.part]
        i = [x[0] for x in names].index(name)
        return names[i][1], i, sum(x[1] == names[i][1] for x in names[:i + 1])

    def filled(self, name):
        return self.nth(self.tile(name)[1] + 1, self.s.parts_of["filled"], self.s.base["filled"])

    def freed(self, name, turns_ago=0):
        o, _, k = self.tile(name)
        parts = self.s.parts_of[o]
        return self.nth(k - turns_ago * parts[1], parts, self.s.base[o])

    def bank(self, name):
        i = [x[0] for x in TURN_TILES].index(name)
        return (self.s.bank0 + i) % NBANK

    def before(self, name):
        i = [x[0] for x in TURN_TILES].index(name) - NBANK
        if self.part == "turn":
            ago = 0
            while i < 0 or i >= len(TURN_TILES):
                if i < 0:
                    i, ago = i + BANKS_A_TURN, ago + 1
                else:
                    i -= NBANK
            last = TURN_TILES[i][0]
            return self.tile(last)[0], self.freed(last, ago)
        while i >= 0:
            if TURN_TILES[i][0] not in NEXT_TURNS:
                last = TURN_TILES[i][0]
                return self.tile(last)[0], self.freed(last)
            i -= NBANK
        i += BANKS_A_TURN
        while i >= len(TURN_TILES):
            i -= NBANK
        last_turn = Place(self.s, "turn", self.s.turns - 2, self.repeat)
        last = TURN_TILES[i][0]
        return last_turn.tile(last)[0], last_turn.freed(last)


def trunk(nc, A, out):
    _, T, D = A["x"].shape
    TT = T // P
    KD = D // P
    W = A["conv_w_dw"].shape[1]
    NMEM = A["mem"].shape[1]
    QR = A["mla_q_norm"].shape[1]
    KVR = A["mla_kv_norm"].shape[1]
    ROPE = A["mla_w_down"].shape[2] - QR - KVR
    DOWN = QR + KVR + ROPE
    NOPE = VD = 64
    QKD = NOPE + ROPE
    H = A["mla_w_uq"].shape[2] // QKD
    XH = 4
    XHD = D // XH
    E = A["moe_w_exp"].shape[2]
    G = A["moe_w_grp"].shape[2]
    EG = E // G
    FF = A["moe_w_gate"].shape[3]
    HALF = 512
    NH = D // HALF
    XSCALE = 1.0 / float(np.sqrt(XHD))
    MSCALE = 1.0 / float(np.sqrt(QKD))
    assert (T, D, NMEM, FF, EG, H, QKD) == (256, 1024, 256, 256, 8, 16, 96)
    assert (EG // 2, KD, NH, TT) == (GROUP_PAIRS, GROUP_K, HALVES, TOKEN_TILES)
    REPEATS = -(-T // CAP) - 1

    N_CIN, N_KV, N_COUT, N_XQ, N_XO = 8, 8, 4, 4, 4
    N_MLA_DOWN, N_UQ, N_UKV, N_MO = 3, 3, 2, 4
    U_CIN = 0
    U_KV = [N_CIN, N_CIN + N_KV]
    U_COUT = N_CIN + 2 * N_KV
    U_XQ0 = U_COUT + N_COUT
    U_XO0 = U_XQ0 + N_XQ
    U_MOE0 = U_XO0 + N_XO
    U_DOWN = U_MOE0 + 3 * E
    U_UQ = U_DOWN + N_MLA_DOWN
    U_UKV = U_UQ + N_UQ
    U_MO = U_UKV + N_UKV
    U_XQ1 = U_MO + N_MO
    U_XO1 = U_XQ1 + N_XQ
    U_MOE1 = U_XO1 + N_XO
    U_XQ, U_XO, U_MOE = [U_XQ0, U_XQ1], [U_XO0, U_XO1], [U_MOE0, U_MOE1]
    GU = 3 * EG
    TURNS = G

    tiles = Tiles()
    alt = ("dve", "act")
    tiles.add("prm", "dve")
    for j in range(4):
        tiles.add(f"n0_{j}", alt[j % 2])
    for j in range(4):
        tiles.add(f"mem_{j}", alt[j % 2])
    for j in range(KD):
        tiles.add(f"glu_{j}", "dve")
    for l in range(2):
        for j in range(4):
            tiles.add(f"xk{l}_{j}", "act")
        for f in range(NH):
            for t in range(TT):
                tiles.add(f"xv{l}_{f}_{t}", "act")
    tiles.add("mu", "dve")
    tiles.add("var", "act")

    def add_out(name):
        for f in range(NH):
            for t in range(TT):
                tiles.add(f"{name}_{f}_{t}", "dve")

    ALL_TILES = {o: tuple(sum(x[1] == o for x in PARTS[p]) for p in ("prologue", "turn", "epilogue")) for o in OWNERS}
    ALL_TILES["filled"] = tuple(len(PARTS[p]) for p in ("prologue", "turn", "epilogue"))
    in_a_sweep = {o: n[0] + n[1] * (TURNS - 1) + n[2] for o, n in ALL_TILES.items()}
    before_moe = []

    add_out("cout")
    for l in range(2):
        if l == 1:
            for j in range(4):
                tiles.add(f"n4_{j}", alt[j % 2])
            for t in range(TT):
                tiles.add(f"dnA_{t}", "act")
            for t in range(TT):
                tiles.add(f"dnB_{t}", "act")
            for j in range(3):
                tiles.add(f"cT_{j}", alt[j % 2])
            for n in range(3):
                for t in range(TT):
                    tiles.add(f"uq_{n}_{t}", "act")
            for j in range(H // 2):
                tiles.add(f"qT_{j}", alt[j % 2])
            for n in range(4):
                for t in range(TT):
                    tiles.add(f"ukv_{n}_{t}", alt[t % 2])
            for j in range(H // 2):
                tiles.add(f"kT_{j}", alt[j % 2])
            tiles.add("ms_0", "dve")
            tiles.add("ms_1", "dve")
            for hd in range(H):
                if hd + 2 < H:
                    tiles.add(f"ms_{hd + 2}", "dve")
                tiles.add(f"mp_{hd}", "act")
                if hd % 2:
                    tiles.add(f"mo_{hd // 2}", "act")
            add_out("mw")
        for j in range(4):
            tiles.add(f"nx{l}_{j}", alt[j % 2])
        for j in range(4):
            tiles.add(f"xq{l}_{j}", alt[j % 2])
        for hd in range(XH):
            tiles.add(f"xs{l}_{hd}", "act")
        for hd in range(XH):
            tiles.add(f"xp{l}_{hd}", "act")
            tiles.add(f"xo{l}_{hd}", "dve")
        add_out(f"xw{l}")
        for j in range(4):
            tiles.add(f"nf{l}_{j}", alt[j % 2])
        tiles.add(f"lg{l}", "dve")
        tiles.add(f"rk{l}", "dve")
        before_moe.append(dict(tiles.count, mid=0, ga_dve=0, ga_act=0))
        for o in ("filled", "dve", "act"):
            tiles.count[o] += in_a_sweep[o]

    ctx = ExitStack()
    with ctx:
        def sb(name, shape, dt=F32):
            return ctx.enter_context(nc.sbuf_tensor(name, shape, dt))

        def sem(name):
            return ctx.enter_context(nc.semaphore(name))

        banks = [ctx.enter_context(nc.psum_tensor(f"bank{i}", [P, 512], F32)) for i in range(NBANK)]

        ring = sb("ring", [P, RING * UNIT])
        h = sb("h", [P, TT, D])
        xhat = sb("xhat", [P, TT, D])
        hT = sb("hT", [P, KD, T])
        kv0 = sb("kv0", [P, 4096])
        kv1 = sb("kv1", [P, 4096])
        scratch = sb("scratch", [P, 9856])
        bcast_row = sb("bcast_row", [P, D])
        ident = sb("ident", [P, P])
        before = sb("before", [P, P])
        ones = sb("ones", [P, P])
        mean_of = sb("mean_of", [P, P])
        slot_no = sb("slot_no", [P, SLOTS])
        slot_no_i = sb("slot_no_i", [P, SLOTS], I32)
        desc = sb("desc", [P, EG])
        causal = sb("causal", [P, 3 * P])
        router = sb("router", [P, 2, KD, G + E])
        router_b = sb("router_b", [P, 2, G + E])
        NA_ROWS, NB_ROWS = 8, W + 7
        prmT = sb("prmT", [P, KD * (NA_ROWS + NB_ROWS)])
        stat = sb("stat", [P, 64])
        rt = sb("rt", [P, 1024])
        pos_i = sb("pos_i", [P, TT], I32)
        rope_t = sb("rope_t", [P, 6, TT, ROPE // 2])
        rope_i = sb("rope_i", [P, TT, ROPE // 2], I32)
        most = sb("most", [P, 2], I32)

        gain_of = prmT[:, 0:KD * NA_ROWS].rearrange("p (k r) -> p k r", k=KD)
        conv_of = prmT[:, KD * NA_ROWS:].rearrange("p (k r) -> p k r", k=KD)
        R_MIX, R_XA, R_MEM, R_FFN = 0, 2, 4, 6
        R_BDW, R_LNG, R_LNB, R_BA, R_BG, R_QN, R_KVN = range(W, W + 7)
        prm_a = kv1[0:NA_ROWS, 0:D]
        prm_b = kv1[0:NB_ROWS, D:2 * D]

        def view(t, at, *shape):
            n = int(np.prod(shape))
            v = t[:, at:at + n]
            if len(shape) == 2:
                return v.rearrange("p (a b) -> p a b", a=shape[0])
            if len(shape) == 3:
                return v.rearrange("p (a b c) -> p a b c", a=shape[0], b=shape[1])
            return v

        xkT = [view(kv0, 0, KD, NMEM), view(kv1, 0, KD, NMEM)]
        xv = [view(kv0, 2048, 2, D), view(kv1, 2048, 2, D)]
        PADDED = W - 1 + T
        u_pad = view(scratch, 0, KD, PADDED)
        conv = view(scratch, 2304, KD, T)
        mem_rows = view(scratch, 4352, 2, D)
        conv_sq = view(scratch, 4352, KD, T)
        memT = [view(scratch, 6400, KD, NMEM), xhat[:, :, :].rearrange("p a b -> p (a b)").rearrange("p (k m) -> p k m", k=KD)]
        sig = view(scratch, 8448, 2, T)
        ln_rstd = view(scratch, 8960, T)
        xqT = view(scratch, 0, KD, T)
        xprob = view(scratch, 2048, XH, TT, NMEM)
        xprobT = view(scratch, 4096, 2, 2 * T)
        qtok = view(scratch, 0, TT, H * QKD)
        ktok = qtok
        qhT = view(scratch, 3072, H, T)
        khT = view(kv0, 0, H, T)
        vtok = xhat
        down = view(scratch, 7168, TT, DOWN)
        cT = view(scratch, 8512, 5, T)
        rope_tmp = scratch[:, 3072:3072 + 4 * TT * H * (ROPE // 2)].rearrange(
            "p (n t h r) -> p n t h r", n=4, t=TT, h=H)
        squares_junk = view(scratch, 5120, 2 * TT, 384)
        score = view(scratch, 7168, 2, 3 * P)
        prob = view(scratch, 7168 + 768, 2, 3 * P)
        probT = view(scratch, 7168 + 1536, 2, 3 * P)
        xg = scratch[:, 0:KD * EG * SLOTS].rearrange("p (k e c) -> p k e c", k=KD, e=EG)
        pick = view(scratch, 4096, TT, EG * SLOTS)
        yslot = view(scratch, 5120, 2, D)
        put = view(scratch, 7168, 4, TT, P)
        hmid = view(scratch, 8192, 2, FF)
        gated = view(scratch, 8704, 2, FF)
        hmidT = view(scratch, 9216, 2, P)

        bank_filled, dve_freed, act_freed = sem("bank_filled"), sem("dve_freed"), sem("act_freed")
        unit_landed = [sem(f"unit_landed{i}") for i in range(RING)]
        x_landed, mem_landed, prm_landed, small_landed, row_landed = (
            sem("x_landed"), sem("mem_landed"), sem("prm_landed"), sem("small_landed"), sem("row_landed"))
        pool_step, consts_ready, bias_added = sem("pool_step"), sem("consts_ready"), sem("bias_added")
        rms_ready, normed = sem("rms_ready"), sem("normed")
        dve_step, act_step = sem("dve_step"), sem("act_step")
        sig_ready, conv_ready, centred, squared, ln_scaled, conv_act = (
            sem("sig_ready"), sem("conv_ready"), sem("centred"), sem("squared"), sem("ln_scaled"), sem("conv_act"))
        angles_ready, sincos_ready = sem("angles_ready"), sem("sincos_ready")
        x_max_ready, x_exp_ready, x_prob_ready = sem("x_max_ready"), sem("x_exp_ready"), sem("x_prob_ready")
        down_rms_ready = sem("down_rms_ready")
        down_ready, roped, ktok_ready = sem("down_ready"), sem("roped"), sem("ktok_ready")
        m_max_ready, m_exp_ready, m_prob_ready = sem("m_max_ready"), sem("m_exp_ready"), sem("m_prob_ready")
        route_diff, route_exp, assigned, routed = (
            sem("route_diff"), sem("route_exp"), sem("assigned"), sem("routed"))
        stored = sem("stored")

        class Sweep:
            pass

        sweeps = []
        for l in range(2):
            a, b = Sweep(), Sweep()
            own = {x: sem(f"{x}_freed{l}") for x in ("mid", "ga_dve", "ga_act")}
            a.sem = {"filled": bank_filled, "dve": dve_freed, "act": act_freed, **own}
            a.base = before_moe[l]
            a.landed, a.unit0, a.first_use = unit_landed, U_MOE[l], [0] * RING
            b.sem = {x: sem(f"more_{x}{l}") for x in ("filled",) + OWNERS}
            b.base = {"filled": ALL_TILES["filled"][1], "dve": ALL_TILES["dve"][1], "act": ALL_TILES["act"][1],
                      "mid": 0, "ga_dve": 0, "ga_act": 0}
            b.landed = [sem(f"more_landed{l}_{i}") for i in range(RING)]
            b.unit0 = U_MOE[l] % RING
            b.first_use = [1 if i < b.unit0 else 0 for i in range(RING)]
            b.shifted = sem(f"slots_shifted{l}")
            for s, tag in ((a, ""), (b, "more_")):
                s.l, s.turns, s.parts_of, s.bank0 = l, TURNS, ALL_TILES, 0
                s.picked, s.weighted, s.gate_ready = sem(f"{tag}picked{l}"), sem(f"{tag}weighted{l}"), sem(f"{tag}gate_ready{l}")
            sweeps.append((a, b))

        def wait_filled(eng, name):
            eng.wait_ge(bank_filled, tiles.at[name]["filled"])
            return banks[tiles.at[name]["n"] % NBANK]

        def wait_evac(eng, name):
            x = tiles.at[name]
            eng.wait_ge(dve_freed if x["owner"] == "dve" else act_freed, x["freed"])

        def evac(ins, name):
            ins.then_inc(dve_freed if tiles.at[name]["owner"] == "dve" else act_freed, 1)

        def open_bank(pe, name):
            n = tiles.at[name]["n"]
            if n >= NBANK:
                wait_evac(pe, tiles.order[n - NBANK])
            return banks[n % NBANK]

        def filled_at(eng, pl, name):
            eng.wait_ge(pl.s.sem["filled"], pl.value(pl.filled(name)))
            return banks[pl.bank(name)]

        def copied_at(ins, pl, name):
            ins.then_inc(pl.s.sem[pl.tile(name)[0]], 1)

        def ready_at(pe, pl, banks_of=(), copies_of=()):
            need = []
            if pl.part != "prologue":
                need += [pl.before(x) for x in banks_of]
            need += [(pl.tile(x)[0], pl.freed(x)) for x in copies_of]
            for o in OWNERS:
                mine = [count for owner, count in need if owner == o]
                if mine:
                    pe.wait_ge(pl.s.sem[o], pl.value(max(mine)))
            return [banks[pl.bank(x)] for x in banks_of]

        def unit(i, *shape):
            s = (i % RING) * UNIT
            v = ring[:, s:s + int(np.prod(shape))]
            if len(shape) == 2:
                return v.rearrange("p (a b) -> p a b", a=shape[0])
            return v

        def wait_unit(eng, i):
            eng.wait_ge(unit_landed[i % RING], 16 * (i // RING + 1))

        last_tile = {}
        for j in range(N_CIN):
            last_tile[U_CIN + j] = f"glu_{2 * (j // 2) + 1}"

        def last_of(u0, name, per_unit_tile):
            for j in range(4):
                last_tile[u0 + j] = f"{name}_{j}" if per_unit_tile else f"{name}_{j // 2}_{TT - 1}"

        for l in range(2):
            last_of(U_KV[l], f"xk{l}", True)
            last_of(U_KV[l] + 4, f"xv{l}", False)
            last_of(U_XQ[l], f"xq{l}", True)
            last_of(U_XO[l], f"xw{l}", False)
        last_of(U_COUT, "cout", False)
        last_of(U_MO, "mw", False)
        last_tile.update({U_DOWN: f"dnA_{TT - 1}", U_DOWN + 1: f"dnA_{TT - 1}", U_DOWN + 2: f"dnB_{TT - 1}"})
        last_tile.update({U_UQ + n: f"uq_{n}_{TT - 1}" for n in range(N_UQ)})
        last_tile.update({U_UKV + n: f"ukv_{2 * n + 1}_{TT - 1}" for n in range(N_UKV)})

        def last_of_unit(u):
            kind, pair, _ = TURN_UNITS[u]
            return f"yd{pair}_{NH - 1}" if kind == "down" else f"gu{pair}"

        for l in range(2):
            for u in range(len(FIRST_UNITS)):
                last_tile[U_MOE[l] + u] = Place(sweeps[l][0], "prologue").filled("gu0")[0]
            for u in range(len(EPILOGUE_UNITS)):
                last_tile[U_MOE[l] + len(FIRST_UNITS) + (TURNS - 1) * GU + u] = Place(sweeps[l][0], "epilogue").filled(last_of_unit(u))[0]

        block = ctx.enter_context(nc.Block())

        @block.sync
        def _(sp):
            def slot_free(i):
                if i >= RING:
                    last = last_tile[i - RING]
                    if isinstance(last, int):
                        sp.wait_ge(bank_filled, last)
                    else:
                        wait_filled(sp, last)

            def load(i, src, *shape):
                slot_free(i)
                sp.dma_start(unit(i, *shape), src).then_inc(unit_landed[i % RING], 16)

            def by_channel(i, w, cols):
                load(i, w.rearrange("(p k) n -> p k n", k=KD)[:, :, cols:cols + 256], KD, 256)

            def k_by_p(i, w, f):
                for q in range(2):
                    src = w.rearrange("(k p) n -> p k n", p=P)[:, 4 * q:4 * q + 4, f * HALF:(f + 1) * HALF]
                    load(i + q, src, 4, HALF)

            def p_by_k(i, w, c0, n):
                for q in range(2):
                    src = w.rearrange("(p k) n -> p k n", k=KD)[:, 4 * q:4 * q + 4, c0:c0 + n]
                    load(i + q, src, 4, n)

            w_in = A["conv_w_in"][0]
            for j in range(4):
                by_channel(U_CIN + 2 * j, w_in, 256 * j)
                by_channel(U_CIN + 2 * j + 1, w_in, D + 256 * j)
                if j == 0:
                    sp.wait_ge(x_landed, 16)
                    sp.wait_ge(prm_landed, 16 * 11)
                    sp.wait_ge(mem_landed, 16)
            for l in range(2):
                for j in range(4):
                    by_channel(U_KV[l] + j, A["xa_wkv"][l], 256 * j)
                for f in range(NH):
                    p_by_k(U_KV[l] + 4 + 2 * f, A["xa_wkv"][l], D + f * HALF, HALF)
            for f in range(NH):
                k_by_p(U_COUT + 2 * f, A["conv_w_out"][0], f)

            def cross(l):
                for j in range(4):
                    by_channel(U_XQ[l] + j, A["xa_wq"][l], 256 * j)
                for f in range(NH):
                    k_by_p(U_XO[l] + 2 * f, A["xa_wo"][l], f)

            def load_expert(s, what, group, slot):
                kind, pair, e = what
                ex = group * EG + (2 * pair + e)
                if kind == "down":
                    src, shape = A["moe_w_down"][s.l, ex].rearrange("(k p) n -> p k n", p=P), (FF // P, D)
                else:
                    src, shape = A[f"moe_w_{kind}"][s.l, ex].rearrange("(p k) n -> p k n", k=KD), (KD, FF)
                sp.dma_start(unit(slot, *shape), src).then_inc(s.landed[slot % RING], 16)

            def sweep(s, repeat=None):
                n1, first = len(FIRST_UNITS), s.unit0
                if repeat is not None:
                    sp.wait_ge(s.sem["filled"], repeat * in_a_sweep["filled"] + s.base["filled"])
                for i, what in enumerate(FIRST_UNITS + TURN_UNITS[:RING]):
                    if repeat is None:
                        slot_free(first + i)
                    elif i >= RING:
                        pl = Place(s, "prologue", repeat=repeat)
                        sp.wait_ge(s.sem["filled"], pl.value(pl.filled("gu0")))
                    load_expert(s, what, 0, first + i)
                with sp.Fori(0, TURNS - 1) as turn:
                    pl = Place(s, "turn", turn, repeat)
                    for u in range(RING, GU):
                        sp.wait_ge(s.sem["filled"], pl.value(pl.filled(last_of_unit(u - RING))))
                        if u < GU - n1:
                            load_expert(s, TURN_UNITS[u], turn, first + n1 + u)
                        else:
                            load_expert(s, TURN_UNITS[u], turn + 1, first + n1 + u)
                    for u in range(RING):
                        sp.wait_ge(s.sem["filled"], pl.value(pl.filled(last_of_unit(u + RING))))
                        load_expert(s, TURN_UNITS[u], turn + 1, first + n1 + u)
                pl = Place(s, "epilogue", repeat=repeat)
                for u in range(RING, len(EPILOGUE_UNITS)):
                    sp.wait_ge(s.sem["filled"], pl.value(pl.filled(last_of_unit(u - RING))))
                    load_expert(s, TURN_UNITS[u], TURNS - 1, first + n1 + u)

            def moe(l):
                a, b = sweeps[l]
                sweep(a)
                sp.wait_ge(routed, l + 1)
                n = sp.value_load(most[0:1, l:l + 1], min_val=0, max_val=T)
                with sp.If(n > CAP):
                    with sp.Fori(0, REPEATS) as repeat:
                        sweep(b, repeat)
                    sp.wait_ge(b.sem["filled"], b.base["filled"] + REPEATS * in_a_sweep["filled"])

            cross(0)
            moe(0)
            p_by_k(U_DOWN, A["mla_w_down"][0], 0, HALF)
            load(U_DOWN + 2, A["mla_w_down"][0].rearrange("(p k) n -> p k n", k=KD)[:, :, HALF:DOWN], KD, DOWN - HALF)
            for n in range(3):
                load(U_UQ + n, A["mla_w_uq"][0].rearrange("(k p) n -> p k n", p=P)[:, :, n * HALF:(n + 1) * HALF], 3, HALF)
            for n in range(2):
                load(U_UKV + n, A["mla_w_ukv"][0].rearrange("(k p) n -> p k n", p=P)[:, :, n * D:(n + 1) * D], 2, D)
            for f in range(NH):
                k_by_p(U_MO + 2 * f, A["mla_w_o"][0], f)
            cross(1)
            moe(1)
            for t in range(TT):
                sp.wait_ge(normed, 14 + t + 1)
                sp.dma_start(out[0, t * P:(t + 1) * P, :], xhat[:, t, :]).then_inc(stored, 16)
            sp.wait_ge(stored, 16 * TT)

        @block.gpsimd
        def _(pool):
            n = 0

            def step(ins):
                nonlocal n
                n += 1
                ins.then_inc(pool_step, 1)
                pool.wait_ge(pool_step, n)

            step(nc.gpsimd.memset(kv1[0:NB_ROWS, 0:2 * D], 0.0))
            nc.gpsimd.memset(ident[:, :], 0.0).then_inc(consts_ready, 1)
            pool.wait_ge(consts_ready, 1)
            nc.gpsimd.affine_select(out=ident[:, :], in_=ident[:, :], compare_op=ALU.not_equal, fill=1.0,
                                    base=0, pattern=[[-1, P]], channel_multiplier=1).then_inc(consts_ready, 1)
            step(nc.gpsimd.memset(ones[:, :], 1.0))
            step(nc.gpsimd.affine_select(out=before[:, :], in_=ones[:, :], compare_op=ALU.is_gt, fill=0.0,
                                         base=0, pattern=[[1, P]], channel_multiplier=-1))
            step(nc.gpsimd.memset(mean_of[:, :], 1.0 / D))
            step(nc.gpsimd.memset(u_pad[:, :, 0:W - 1], 0.0))
            step(nc.gpsimd.iota(slot_no_i[:, :], pattern=[[1, SLOTS]], base=0, channel_multiplier=0))
            step(nc.gpsimd.tensor_copy(slot_no[:, :], slot_no_i[:, :]))
            step(nc.gpsimd.memset(slot_no[:, CAP:], 1e6))
            step(nc.gpsimd.tensor_scalar(desc[:, :], slot_no[:, 0:EG], -1.0, float(EG), ALU.mult, ALU.add))
            step(nc.gpsimd.memset(causal[:, :], 0.0))
            for c in (0, 2):
                step(nc.gpsimd.affine_select(out=causal[:, c * P:(c + 1) * P], in_=causal[:, c * P:(c + 1) * P],
                                             compare_op=ALU.is_ge, fill=NEG, base=0, pattern=[[-1, P]],
                                             channel_multiplier=1))
            inv = 1.0 / (np.float32(10000.0) ** (np.arange(0, ROPE, 2, dtype=np.float32) / np.float32(ROPE)))
            for i in range(ROPE // 2):
                step(nc.gpsimd.memset(rope_t[:, 0, :, i:i + 1], float(np.float32(inv[i]))))
            nc.gpsimd.memset(stat[:, 63:64], EPS).then_inc(consts_ready, 1)
            pool.wait_ge(row_landed, 16)
            for t in range(TT):
                pool.wait_ge(normed, t + 1)
                nc.gpsimd.tensor_tensor(h[:, t, :], h[:, t, :], bcast_row[:, :], ALU.add).then_inc(bias_added, 1)

        @block.scalar
        def _(act):
            def copy(dst, src):
                return nc.scalar.activation(dst, src, ACT.Copy)

            act.dma_start(h[:, :, :], A["x"][0].rearrange("(t p) d -> p t d", p=P)).then_inc(x_landed, 16)
            act.wait_ge(pool_step, 1)
            rows = [(prm_a[R_MIX:R_MIX + 2, :], A["norm_mix"]), (prm_a[R_XA:R_XA + 2, :], A["norm_xa"]),
                    (prm_a[R_MEM:R_MEM + 2, :], A["norm_mem"]), (prm_a[R_FFN:R_FFN + 2, :], A["norm_ffn"]),
                    (prm_b[0:W, :], A["conv_w_dw"][0]),
                    (prm_b[R_BDW:R_BDW + 1, :], A["conv_b_dw"]),
                    (prm_b[R_LNG:R_LNG + 1, :], A["conv_ln_g"]),
                    (prm_b[R_LNB:R_LNB + 1, :], A["conv_ln_b"]),
                    (prm_b[R_BA:R_BG + 1, :], A["conv_b_in"][0].rearrange("(r n) -> r n", r=2)),
                    (prm_b[R_QN:R_QN + 1, 0:QR], A["mla_q_norm"]),
                    (prm_b[R_KVN:R_KVN + 1, 0:KVR], A["mla_kv_norm"])]
            for dst, src in rows:
                act.dma_start(dst, src).then_inc(prm_landed, 16)
            act.dma_start(mem_rows, A["mem"][0].rearrange("(t p) d -> p t d", p=P)).then_inc(mem_landed, 16)
            act.dma_start(bcast_row[:, :], A["conv_b_out"].partition_broadcast(P)).then_inc(row_landed, 16)
            act.dma_start(pos_i[:, :], A["positions"][0].rearrange("(t p) -> p t", p=P),
                          allow_slow_non_contiguous=True).then_inc(small_landed, 16)
            for l in range(2):
                act.dma_start(router[:, l, :, 0:G], A["moe_w_grp"][l].rearrange("(p k) n -> p k n", k=KD),
                              allow_slow_non_contiguous=True).then_inc(small_landed, 16)
                act.dma_start(router[:, l, :, G:], A["moe_w_exp"][l].rearrange("(p k) n -> p k n", k=KD),
                              allow_slow_non_contiguous=True).then_inc(small_landed, 16)
                act.dma_start(router_b[:, l, 0:G], A["moe_b_grp"][l:l + 1, :].partition_broadcast(P)).then_inc(small_landed, 16)
                act.dma_start(router_b[:, l, G:], A["moe_b_exp"][l:l + 1, :].partition_broadcast(P)).then_inc(small_landed, 16)

            n_steps = 0

            def root_mean_square(src, c, n, junk):
                nonlocal n_steps
                n_steps += 1
                nc.scalar.activation(junk, src, ACT.Square, accum_out=c).then_inc(act_step, 1)
                act.wait_ge(act_step, n_steps)
                return nc.scalar.activation(c, c, ACT.Sqrt, bias=stat[:, 63:64], scale=1.0 / n)

            def rms(i, src, t, junk):
                root_mean_square(src, stat[:, 2 * i + t + 1:2 * i + t + 2], D, junk).then_inc(rms_ready, 1)

            def gained(name, row):
                for j in (1, 3):
                    b = wait_filled(act, f"{name}_{j}")
                    for q in range(2):
                        k = 2 * j + q
                        ins = nc.scalar.activation(hT[:, k, :], b[:, q * T:(q + 1) * T], ACT.Copy,
                                                   scale=gain_of[:, k, row:row + 1])
                    evac(ins, f"{name}_{j}")

            act.wait_ge(x_landed, 16)
            act.wait_ge(consts_ready, 3)
            for t in range(TT):
                rms(0, h[:, t, :], t, xhat[:, t, :])
            act.wait_ge(mem_landed, 16)
            for t in range(TT):
                rms(1, mem_rows[:, t, :], t, kv0[:, t * D:(t + 1) * D])
            wait_evac(act, "prm")
            gained("n0", R_MIX)
            for j in (1, 3):
                b = wait_filled(act, f"mem_{j}")
                for q in range(2):
                    k = 2 * j + q
                    for l in range(2):
                        ins = nc.scalar.activation(memT[l][:, k, :], b[:, q * NMEM:(q + 1) * NMEM], ACT.Copy,
                                                   scale=gain_of[:, k, R_MEM + l:R_MEM + l + 1])
                evac(ins, f"mem_{j}")
            for j in range(KD):
                b = wait_filled(act, f"glu_{j}")
                if j >= 2:
                    wait_evac(act, f"glu_{j - 2}")
                nc.scalar.activation(sig[:, j % 2, :], b[:, T:2 * T], ACT.Sigmoid,
                                     bias=conv_of[:, j, R_BG:R_BG + 1]).then_inc(sig_ready, 1)
            for l in range(2):
                for j in range(4):
                    b = wait_filled(act, f"xk{l}_{j}")
                    evac(copy(xkT[l][:, 2 * j:2 * j + 2, :], b[:, :].rearrange("p (a b) -> p a b", a=2)), f"xk{l}_{j}")
                for f in range(NH):
                    for t in range(TT):
                        b = wait_filled(act, f"xv{l}_{f}_{t}")
                        evac(copy(xv[l][:, t, f * HALF:(f + 1) * HALF], b[:, :]), f"xv{l}_{f}_{t}")
            for q in range(2):
                act.wait_ge(centred, q + 1)
                nc.scalar.activation(conv_sq[:, 4 * q:4 * q + 4, :], conv[:, 4 * q:4 * q + 4, :],
                                     ACT.Square).then_inc(squared, 1)
            b = wait_filled(act, "var")
            evac(nc.scalar.activation(ln_rstd, b[:, 0:T], ACT.Sqrt, bias=stat[:, 63:64]), "var")
            for j in range(KD):
                act.wait_ge(ln_scaled, j // 4 + 1)
                nc.scalar.activation(hT[:, j, :], conv[:, j, :], ACT.Silu, bias=conv_of[:, j, R_LNB:R_LNB + 1],
                                     scale=conv_of[:, j, R_LNG:R_LNG + 1]).then_inc(conv_act, 1)

            def cross(l):
                i = 2 if l == 0 else 5
                prev = "cout" if l == 0 else "mw"
                for t in range(TT):
                    wait_evac(act, f"{prev}_{NH - 1}_{t}")
                    rms(i, h[:, t, :], t, xhat[:, t, :])
                gained(f"nx{l}", R_XA + l)
                for j in (1, 3):
                    b = wait_filled(act, f"xq{l}_{j}")
                    evac(copy(xqT[:, 2 * j:2 * j + 2, :], b[:, :].rearrange("p (a b) -> p a b", a=2)), f"xq{l}_{j}")
                for hd in range(XH):
                    act.wait_ge(x_max_ready, XH * l + hd + 1)
                    b = wait_filled(act, f"xs{l}_{hd}")
                    for t in range(TT):
                        c = 32 + 2 * hd + t
                        ins = nc.scalar.activation(xprob[:, hd, t, :], b[:, t * NMEM:(t + 1) * NMEM], ACT.Exp,
                                                   bias=stat[:, c:c + 1], scale=XSCALE,
                                                   accum_out=stat[:, c + 8:c + 9])
                    evac(ins, f"xs{l}_{hd}")
                for hd in range(XH):
                    b = wait_filled(act, f"xp{l}_{hd}")
                    evac(copy(xprobT[:, hd % 2, :], b[:, :]), f"xp{l}_{hd}")

            def route(l):
                i = 3 if l == 0 else 6
                for t in range(TT):
                    wait_evac(act, f"xw{l}_{NH - 1}_{t}")
                    rms(i, h[:, t, :], t, xhat[:, t, :])
                gained(f"nf{l}", R_FFN + l)
                act.wait_ge(route_diff, 2 * l + 1)
                nc.scalar.activation(rt[:, 8:16], rt[:, 0:8], ACT.Exp).then_inc(route_exp, 1)
                act.wait_ge(route_diff, 2 * l + 2)
                nc.scalar.activation(rt[:, 18:20], rt[:, 16:18], ACT.Exp).then_inc(route_exp, 1)

            def run_part(pl):
                l = pl.s.l
                gates = (1, EG // 2, EG // 2 - 1)

                def gathered():
                    for k in range(1, KD, 2):
                        b = filled_at(act, pl, f"ga{k}")
                        copied_at(nc.scalar.activation(xg[:, k, :, 0:CAP], b[:, 0:EG * CAP].rearrange("p (e c) -> p e c", e=EG),
                                                       ACT.Copy, scale=gain_of[:, k, R_FFN + l:R_FFN + l + 1]), pl, f"ga{k}")

                def gate(j):
                    b = filled_at(act, pl, f"gu{j}")
                    nc.scalar.activation(gated[:, j % 2, :], b[:, 0:FF], ACT.Silu).then_inc(pl.s.gate_ready, 1)

                def puts(q):
                    b = filled_at(act, pl, f"st{q}")
                    copied_at(copy(put[:, 2 * q:2 * q + 2, :, :].rearrange("p a t s -> p (a t s)"), b[:, :]), pl, f"st{q}")

                def mid(j):
                    b = filled_at(act, pl, f"ht{j}")
                    copied_at(copy(hmidT.rearrange("p a b -> p (a b)"), b[:, 0:2 * P]), pl, f"ht{j}")

                def y(j):
                    b = filled_at(act, pl, f"yd{j}_1")
                    copied_at(copy(yslot[:, j % 2, HALF:], b[:, :]), pl, f"yd{j}_1")

                if pl.part != "prologue":
                    puts(0)
                    puts(1)
                    for j in range(3):
                        gate(j + 1)
                        mid(j)
                        y(j)
                if pl.part != "epilogue":
                    gathered()
                if pl.part != "prologue":
                    mid(3)
                    y(3)
                if pl.part != "epilogue":
                    gate(0)

            def sweep(s, repeat=None):
                run_part(Place(s, "prologue", repeat=repeat))
                with act.Fori(0, TURNS - 1) as turn:
                    run_part(Place(s, "turn", turn, repeat))
                run_part(Place(s, "epilogue", repeat=repeat))

            def moe(l):
                a, b = sweeps[l]
                sweep(a)
                act.wait_ge(routed, l + 1)
                n = act.value_load(most[0:1, l:l + 1], min_val=0, max_val=T)
                with act.If(n > CAP):
                    act.wait_ge(act_freed, Place(a, "epilogue").freed("yd3_1")[0])
                    act.sem_inc(b.sem["act"], b.base["act"])
                    with act.Fori(0, REPEATS) as repeat:
                        sweep(b, repeat)
                    act.wait_ge(b.sem["dve"], b.base["dve"] + REPEATS * in_a_sweep["dve"])

            cross(0)
            route(0)
            moe(0)

            for t in range(TT):
                act.wait_ge(dve_freed, Place(sweeps[0][0], "epilogue").freed(f"sc1_{NH - 1}_{t}")[0])
                rms(4, h[:, t, :], t, xhat[:, t, :])
            act.wait_ge(angles_ready, 1)
            for q in range(2):
                nc.scalar.activation(rope_t[:, 4 + q, :, :], rope_t[:, 2 + q, :, :], ACT.Sin).then_inc(sincos_ready, 1)
            gained("n4", R_MIX + 1)
            for t in range(TT):
                b = wait_filled(act, f"dnA_{t}")
                evac(copy(down[:, t, 0:HALF], b[:, :]), f"dnA_{t}")
            for t in range(TT):
                b = wait_filled(act, f"dnB_{t}")
                evac(copy(down[:, t, HALF:DOWN], b[:, 0:DOWN - HALF]), f"dnB_{t}")
            for t in range(TT):
                wait_evac(act, f"dnB_{t}")
                for q, (c0, c1) in enumerate(((0, QR), (QR, QR + KVR))):
                    root_mean_square(down[:, t, c0:c1], stat[:, 52 + 2 * t + q:53 + 2 * t + q], c1 - c0,
                                     squares_junk[:, 2 * t + q, 0:c1 - c0]).then_inc(down_rms_ready, 1)
            b = wait_filled(act, "cT_1")
            nc.scalar.activation(cT[:, 2, :], b[:, 0:T], ACT.Copy, scale=conv_of[:, 2, R_QN:R_QN + 1])
            evac(nc.scalar.activation(cT[:, 3, :], b[:, T:2 * T], ACT.Copy, scale=conv_of[:, 0, R_KVN:R_KVN + 1]), "cT_1")
            for n in range(3):
                for t in range(TT):
                    b = wait_filled(act, f"uq_{n}_{t}")
                    evac(copy(qtok[:, t, n * HALF:(n + 1) * HALF], b[:, :]), f"uq_{n}_{t}")

            def heads(name, dst):
                for j in range(1, H // 2, 2):
                    b = wait_filled(act, f"{name}_{j}")
                    evac(copy(dst[0:QKD, 2 * j:2 * j + 2, :], b[0:QKD, :].rearrange("p (a b) -> p a b", a=2)), f"{name}_{j}")

            heads("qT", qhT)
            for n in range(4):
                b = wait_filled(act, f"ukv_{n}_1")
                src = b[:, :].rearrange("p (h c) -> p h c", h=4)
                copy(ktok[:, 1, :].rearrange("p (h c) -> p h c", h=H)[:, 4 * n:4 * n + 4, 0:NOPE], src[:, :, 0:NOPE])
                evac(copy(vtok[:, 1, 4 * n * VD:4 * (n + 1) * VD].rearrange("p (h c) -> p h c", h=4), src[:, :, NOPE:]), f"ukv_{n}_1")
            heads("kT", khT)
            SPANS = [(0, P), (P, 3 * P)]

            def m_exp(hd):
                act.wait_ge(m_max_ready, hd + 1)
                for t in range(TT):
                    c = 32 + 4 * (hd % 2) + t
                    a0, a1 = SPANS[t]
                    ins = nc.scalar.activation(prob[:, hd % 2, a0:a1], score[:, hd % 2, a0:a1], ACT.Exp,
                                               bias=stat[:, c:c + 1], scale=MSCALE, accum_out=stat[:, c + 2:c + 3])
                ins.then_inc(m_exp_ready, 1)

            m_exp(0)
            for hd in range(H):
                if hd + 1 < H:
                    if hd >= 1:
                        wait_filled(act, f"mp_{hd - 1}")
                    m_exp(hd + 1)
                b = wait_filled(act, f"mp_{hd}")
                if hd >= 2:
                    wait_filled(act, f"mo_{hd // 2 - 1}")
                evac(copy(probT[:, hd % 2, :], b[:, 0:3 * P]), f"mp_{hd}")
                if hd % 2:
                    b = wait_filled(act, f"mo_{hd // 2}")
                    evac(copy(hT[:, hd // 2, :], b[:, 0:T]), f"mo_{hd // 2}")
            act.dma_start(bcast_row[:, :], A["final_norm"].rearrange("(a n) -> a n", a=1).partition_broadcast(P)).then_inc(row_landed, 16)
            cross(1)
            route(1)
            moe(1)
            for t in range(TT):
                act.wait_ge(dve_freed, Place(sweeps[1][0], "epilogue").freed(f"sc1_{NH - 1}_{t}")[0])
                rms(7, h[:, t, :], t, xhat[:, t, :])

        @block.vector
        def _(dve):
            v = nc.vector
            n_steps = 0

            def mark(ins):
                nonlocal n_steps
                n_steps += 1
                ins.then_inc(dve_step, 1)
                return n_steps

            def step(ins):
                dve.wait_ge(dve_step, mark(ins))

            def norm(i, src, dst):
                for t in range(TT):
                    c = stat[:, 2 * i + t + 1:2 * i + t + 2]
                    dve.wait_ge(rms_ready, 2 * i + t + 1)
                    step(v.reciprocal(c, c))
                    v.tensor_scalar(dst[:, t, :], src[:, t, :], c, None, ALU.mult).then_inc(normed, 1)

            def gained(name, row):
                for j in (0, 2):
                    b = wait_filled(dve, f"{name}_{j}")
                    for q in range(2):
                        k = 2 * j + q
                        ins = v.tensor_scalar(hT[:, k, :], b[:, q * T:(q + 1) * T], gain_of[:, k, row:row + 1], None, ALU.mult)
                    evac(ins, f"{name}_{j}")

            def add_residual(name):
                for f in range(NH):
                    for t in range(TT):
                        b = wait_filled(dve, f"{name}_{f}_{t}")
                        s = h[:, t, f * HALF:(f + 1) * HALF]
                        evac(v.tensor_tensor(s, s, b[:, :], ALU.add), f"{name}_{f}_{t}")

            b = wait_filled(dve, "prm")
            evac(v.tensor_copy(prmT[:, :], b[:, 0:KD * (NA_ROWS + NB_ROWS)]), "prm")
            norm(0, h, xhat)
            norm(1, mem_rows, mem_rows)
            wait_evac(dve, "prm")
            gained("n0", R_MIX)
            for j in (0, 2):
                b = wait_filled(dve, f"mem_{j}")
                for q in range(2):
                    k = 2 * j + q
                    for l in range(2):
                        ins = v.tensor_scalar(memT[l][:, k, :], b[:, q * NMEM:(q + 1) * NMEM],
                                              gain_of[:, k, R_MEM + l:R_MEM + l + 1], None, ALU.mult)
                evac(ins, f"mem_{j}")

            dve.wait_ge(small_landed, 16 * 9)
            dve.wait_ge(consts_ready, 3)
            ang, full, r, rc = (rope_t[:, q, :, :] for q in range(4))
            posf = stat[:, 50:50 + TT]
            step(v.tensor_copy(posf, pos_i[:, :]))
            step(v.tensor_tensor(full, ang, posf.unsqueeze(2).to_broadcast([P, TT, ROPE // 2]), ALU.mult))
            step(v.tensor_scalar(ang, full, float(1.0 / (2 * np.pi)), None, ALU.mult))
            step(v.tensor_copy(rope_i[:, :, :], ang))
            step(v.tensor_copy(ang, rope_i[:, :, :]))
            c1 = 6.28125
            c2 = float(np.float32(np.float64(2 * np.pi) - c1))
            c3 = float(np.float64(2 * np.pi) - c1 - np.float64(np.float32(c2)))
            src = full
            for c in (c1, c2, c3):
                step(v.scalar_tensor_tensor(out=r, in0=ang, scalar=-c, in1=src, op0=ALU.mult, op1=ALU.add))
                src = r

            def wrap(x):
                for cmp, lim, add in ((ALU.is_gt, float(np.pi), -2 * np.pi), (ALU.is_lt, -float(np.pi), 2 * np.pi)):
                    step(v.tensor_scalar(ang, x, lim, float(add), cmp, ALU.mult))
                    step(v.tensor_tensor(x, x, ang, ALU.add))
                return v.tensor_scalar(x, x, 3.1415925, -3.1415925, ALU.min, ALU.max)

            step(wrap(r))
            step(v.tensor_scalar(rc, r, float(np.pi / 2), None, ALU.add))
            wrap(rc).then_inc(angles_ready, 1)
            sin_t, cos_t = rope_t[:, 4, :, :], rope_t[:, 5, :, :]

            done_tap = {}
            for m in range(KD // 2):
                for j in (2 * m, 2 * m + 1):
                    b = wait_filled(dve, f"glu_{j}")
                    dve.wait_ge(sig_ready, j + 1)
                    evac(v.scalar_tensor_tensor(out=u_pad[:, j, W - 1:], in0=b[:, 0:T], scalar=conv_of[:, j, R_BA:R_BA + 1],
                                                in1=sig[:, j % 2, :], op0=ALU.add, op1=ALU.mult), f"glu_{j}")
                for tap in range(W):
                    for j in (2 * m, 2 * m + 1):
                        taps = u_pad[:, j, tap:tap + T]
                        w = conv_of[:, j, tap:tap + 1]
                        if tap == 0:
                            wait_evac(dve, f"glu_{j}")
                            ins = v.tensor_scalar(conv[:, j, :], taps, w, conv_of[:, j, R_BDW:R_BDW + 1], ALU.mult, ALU.add)
                        else:
                            dve.wait_ge(dve_step, done_tap[j])
                            ins = v.scalar_tensor_tensor(out=conv[:, j, :], in0=taps, scalar=w, in1=conv[:, j, :],
                                                         op0=ALU.mult, op1=ALU.add)
                        if tap < W - 1:
                            done_tap[j] = mark(ins)
                        else:
                            ins.then_inc(conv_ready, 1)

            b = wait_filled(dve, "mu")
            dve.wait_ge(conv_ready, KD)
            for q in range(2):
                s = conv[:, 4 * q:4 * q + 4, :]
                ins = v.tensor_tensor(s, s, b[:, 0:T].unsqueeze(1).to_broadcast([P, 4, T]), ALU.subtract)
                ins.then_inc(centred, 1)
            dve.wait_ge(centred, 2)
            evac(v.tensor_copy(stat[:, 60:61], b[:, 0:1]), "mu")
            wait_evac(dve, "var")
            step(v.reciprocal(ln_rstd, ln_rstd))
            for q in range(2):
                s = conv[:, 4 * q:4 * q + 4, :]
                v.tensor_tensor(s, s, ln_rstd.unsqueeze(1).to_broadcast([P, 4, T]), ALU.mult).then_inc(ln_scaled, 1)
            dve.wait_ge(bias_added, TT)
            add_residual("cout")

            def cross(l):
                i = 2 if l == 0 else 5
                norm(i, h, xhat)
                gained(f"nx{l}", R_XA + l)
                for j in (0, 2):
                    b = wait_filled(dve, f"xq{l}_{j}")
                    evac(v.tensor_copy(xqT[:, 2 * j:2 * j + 2, :], b[:, :].rearrange("p (a b) -> p a b", a=2)), f"xq{l}_{j}")
                for hd in range(XH):
                    b = wait_filled(dve, f"xs{l}_{hd}")
                    mx = stat[:, 32 + 2 * hd:34 + 2 * hd]
                    step(v.tensor_reduce(out=mx, in_=b[:, :].rearrange("p (t m) -> p t m", t=TT), axis=AX.X, op=ALU.max))
                    v.tensor_scalar(mx, mx, -XSCALE, None, ALU.mult).then_inc(x_max_ready, 1)
                for hd in range(XH):
                    wait_evac(dve, f"xs{l}_{hd}")
                    su = stat[:, 40 + 2 * hd:42 + 2 * hd]
                    step(v.reciprocal(su, su))
                    v.tensor_tensor(xprob[:, hd, :, :], xprob[:, hd, :, :],
                                    su.unsqueeze(2).to_broadcast([P, TT, NMEM]), ALU.mult).then_inc(x_prob_ready, 1)
                for hd in range(XH):
                    b = wait_filled(dve, f"xo{l}_{hd}")
                    evac(v.tensor_copy(hT[:, 2 * hd:2 * hd + 2, :], b[:, :].rearrange("p (a b) -> p a b", a=2)), f"xo{l}_{hd}")
                add_residual(f"xw{l}")

            gdiff, gexp = view(rt, 0, TT, G), view(rt, 8, TT, G)
            ediff, eexp = rt[:, 16:18], rt[:, 18:20]
            gmax, gsum, m1, m2, best, w1, w2 = (rt[:, 20 + 2 * q:22 + 2 * q] for q in range(7))
            logit = view(rt, 40, TT, G + E)
            group = view(rt, 112, TT, G)
            eq = view(rt, 120, TT, EG)
            mine = view(rt, 136, TT, EG)
            first, second, within, chosen = (view(rt, 152 + 16 * q, TT, EG) for q in range(4))
            masked = view(rt, 216, TT, G, EG)
            taken = view(rt, 280, TT, G, EG)
            weight = view(rt, 344, TT, G, EG)
            slot = view(rt, 408, TT, E)

            def over(x, n):
                return x.unsqueeze(2).to_broadcast([P, TT, n])

            def first_of(x, top, n, onehot):
                step(v.tensor_reduce(out=top, in_=x, axis=AX.X, op=ALU.max))
                e = eq[:, :, 0:n]
                step(v.tensor_tensor(e, x, over(top, n), ALU.is_equal))
                step(v.tensor_tensor(e, e, desc[:, EG - n:EG].unsqueeze(1).to_broadcast([P, TT, n]), ALU.mult))
                step(v.tensor_reduce(out=best, in_=e, axis=AX.X, op=ALU.max))
                step(v.tensor_tensor(onehot, e, over(best, n), ALU.is_equal))

            def route(l):
                i = 3 if l == 0 else 6
                norm(i, h, xhat)
                gained(f"nf{l}", R_FFN + l)
                b = wait_filled(dve, f"lg{l}")
                evac(v.tensor_tensor(logit, b[:, 0:TT * (G + E)].rearrange("p (t n) -> p t n", t=TT),
                                     router_b[:, l:l + 1, :].to_broadcast([P, TT, G + E]), ALU.add), f"lg{l}")
                wait_evac(dve, f"lg{l}")
                v.memset(xg[:, :, :, CAP:], 0.0)
                first_of(logit[:, :, 0:G], gmax, G, group)
                v.tensor_tensor(gdiff, logit[:, :, 0:G], over(gmax, G), ALU.subtract).then_inc(route_diff, 1)
                step(v.tensor_tensor(masked, logit[:, :, G:].rearrange("p t (g e) -> p t g e", g=G),
                                     group.unsqueeze(3).to_broadcast([P, TT, G, EG]), ALU.mult))
                step(v.tensor_reduce(out=mine, in_=masked.rearrange("p t g e -> p t e g"), axis=AX.X, op=ALU.add))
                first_of(mine, m1, EG, first)
                step(v.scalar_tensor_tensor(out=mine, in0=first, scalar=NEG, in1=mine, op0=ALU.mult, op1=ALU.add))
                first_of(mine, m2, EG, second)
                v.tensor_tensor(ediff, m2, m1, ALU.subtract).then_inc(route_diff, 1)
                step(v.tensor_tensor(chosen, first, second, ALU.add))
                v.tensor_tensor(taken, group.unsqueeze(3).to_broadcast([P, TT, G, EG]),
                                chosen.unsqueeze(2).to_broadcast([P, TT, G, EG]), ALU.mult).then_inc(assigned, 1)
                dve.wait_ge(route_exp, 2 * l + 1)
                step(v.tensor_reduce(out=gsum, in_=gexp, axis=AX.X, op=ALU.add))
                dve.wait_ge(route_exp, 2 * l + 2)
                step(v.tensor_scalar(w1, eexp, 1.0, None, ALU.add))
                step(v.tensor_tensor(w1, w1, gsum, ALU.mult))
                step(v.reciprocal(w1, w1))
                step(v.tensor_tensor(w2, w1, eexp, ALU.mult))
                step(v.tensor_tensor(first, first, over(w1, EG), ALU.mult))
                step(v.tensor_tensor(second, second, over(w2, EG), ALU.mult))
                step(v.tensor_tensor(within, first, second, ALU.add))
                step(v.tensor_tensor(weight, group.unsqueeze(3).to_broadcast([P, TT, G, EG]),
                                     within.unsqueeze(2).to_broadcast([P, TT, G, EG]), ALU.mult))
                dve.wait_ge(assigned, l + 1)
                b = wait_filled(dve, f"rk{l}")
                flat = taken.rearrange("p t g e -> p t (g e)")
                step(v.scalar_tensor_tensor(out=slot, in0=b[:, 0:TT * E].rearrange("p (t n) -> p t n", t=TT), scalar=1.0,
                                            in1=flat, op0=ALU.add, op1=ALU.mult))
                step(v.tensor_scalar(slot, slot, -1.0, None, ALU.add))
                step(v.tensor_reduce(out=rt[:, 38:39], in_=b[:, TT * E:(TT + 1) * E], axis=AX.X, op=ALU.max))
                mark(v.tensor_copy(most[:, l:l + 1], rt[:, 38:39]))
                dve.wait_ge(dve_step, n_steps)
                evac(v.tensor_copy(rt[:, 39:40], rt[:, 38:39]), f"rk{l}")
                wait_evac(dve, f"rk{l}")
                v.tensor_copy(rt[:, 39:40], rt[:, 38:39]).then_inc(routed, 1)

            def run_part(pl):
                l, s = pl.s.l, pl.s
                wflat = weight.rearrange("p t g e -> p t (g e)")
                group = 0 if pl.part == "prologue" else None if pl.part == "epilogue" else pl.turn + 1

                def pick_tokens():
                    for t in range(TT):
                        p3 = pick[:, t, :].rearrange("p (e s) -> p e s", e=EG)
                        v.tensor_tensor(p3, slot_no[:, :].unsqueeze(1).to_broadcast([P, EG, SLOTS]),
                                        slot[:, t, bass.ds(group * EG, EG)].unsqueeze(2).to_broadcast([P, EG, SLOTS]),
                                        ALU.is_equal).then_inc(s.picked, 1)

                def gathered():
                    for k in range(0, KD, 2):
                        b = filled_at(dve, pl, f"ga{k}")
                        copied_at(v.tensor_scalar(xg[:, k, :, 0:CAP], b[:, 0:EG * CAP].rearrange("p (e c) -> p e c", e=EG),
                                                  gain_of[:, k, R_FFN + l:R_FFN + l + 1], None, ALU.mult), pl, f"ga{k}")
                    filled_at(dve, pl, f"ga{KD - 1}")
                    for t in range(TT):
                        p3 = pick[:, t, :].rearrange("p (e s) -> p e s", e=EG)
                        v.tensor_tensor(p3, p3, wflat[:, t, bass.ds(group * EG, EG)].unsqueeze(2).to_broadcast([P, EG, SLOTS]),
                                        ALU.mult).then_inc(s.weighted, 1)

                def mid(j):
                    b = filled_at(dve, pl, f"gu{j}")
                    k = j if j else (1 if pl.part == "prologue" else EG // 2)
                    dve.wait_ge(s.gate_ready, pl.value(pl.nth(k, (1, EG // 2, EG // 2 - 1))))
                    copied_at(v.tensor_tensor(hmid[:, j % 2, :], gated[:, j % 2, :], b[:, FF:2 * FF], ALU.mult), pl, f"gu{j}")

                def y(j):
                    b = filled_at(dve, pl, f"yd{j}_0")
                    copied_at(v.tensor_copy(yslot[:, j % 2, 0:HALF], b[:, :]), pl, f"yd{j}_0")

                def scatter(q):
                    for f in range(NH):
                        for t in range(TT):
                            name = f"sc{q}_{f}_{t}"
                            b = filled_at(dve, pl, name)
                            c = h[:, t, f * HALF:(f + 1) * HALF]
                            const, a_turn, a_repeat = pl.freed(name)
                            dve.wait_ge(s.sem["dve"], pl.value((const - 1, a_turn, a_repeat)))
                            copied_at(v.tensor_tensor(c, c, b[:, :], ALU.add), pl, name)

                if pl.part == "prologue":
                    pick_tokens()
                    gathered()
                    mid(0)
                    return
                mid(1)
                if pl.part == "turn":
                    filled_at(dve, pl, "st1")
                    pick_tokens()
                y(0)
                mid(2)
                y(1)
                mid(3)
                scatter(0)
                y(2)
                if pl.part == "turn":
                    gathered()
                y(3)
                if pl.part == "turn":
                    mid(0)
                scatter(1)

            def sweep(s, repeat=None):
                if repeat is not None:
                    v.tensor_scalar(slot, slot, -float(CAP), None, ALU.add).then_inc(s.shifted, 1)
                    dve.wait_ge(s.shifted, repeat + 1)
                run_part(Place(s, "prologue", repeat=repeat))
                with dve.Fori(0, TURNS - 1) as turn:
                    run_part(Place(s, "turn", turn, repeat))
                run_part(Place(s, "epilogue", repeat=repeat))

            def moe(l):
                a, b = sweeps[l]
                dve.wait_ge(routed, l + 1)
                sweep(a)
                n = dve.value_load(most[0:1, l:l + 1], min_val=0, max_val=T)
                with dve.If(n > CAP):
                    dve.wait_ge(dve_freed, Place(a, "epilogue").freed(f"sc1_{NH - 1}_{TT - 1}")[0])
                    dve.sem_inc(b.sem["dve"], b.base["dve"])
                    with dve.Fori(0, REPEATS) as repeat:
                        sweep(b, repeat)
                    dve.wait_ge(b.sem["dve"], b.base["dve"] + REPEATS * in_a_sweep["dve"])

            cross(0)
            route(0)
            moe(0)

            norm(4, h, xhat)
            gained("n4", R_MIX + 1)
            for t in range(TT):
                dve.wait_ge(down_rms_ready, 2 * (t + 1))
                c = stat[:, 52 + 2 * t:54 + 2 * t]
                step(v.reciprocal(c, c))
                for q, (c0, c1) in enumerate(((0, QR), (QR, QR + KVR))):
                    part = down[:, t, c0:c1]
                    ins = v.tensor_scalar(part, part, c[:, q:q + 1], None, ALU.mult)
                ins.then_inc(down_ready, 1)
            dve.wait_ge(sincos_ready, 2)
            kr = down[:, :, QR + KVR:DOWN]
            HR = ROPE // 2

            def rotate(x1, x2, cs, sn, tmp):
                a, b_, c_, d_ = tmp
                v.tensor_tensor(a, x1, cs, ALU.mult)
                v.tensor_tensor(b_, x2, sn, ALU.mult)
                v.tensor_tensor(c_, x2, cs, ALU.mult)
                step(v.tensor_tensor(d_, x1, sn, ALU.mult))
                v.tensor_tensor(x1, a, b_, ALU.subtract)
                return v.tensor_tensor(x2, c_, d_, ALU.add)

            step(rotate(kr[:, :, 0:HR], kr[:, :, HR:ROPE], cos_t, sin_t, [rope_tmp[:, q, :, 0, :] for q in range(4)]))
            for j in (0, 2):
                b = wait_filled(dve, f"cT_{j}")
                ins = v.tensor_scalar(cT[:, 2 * j, :], b[:, 0:T], conv_of[:, 0 if j == 0 else 1, (R_QN if j == 0 else R_KVN):(R_QN if j == 0 else R_KVN) + 1], None, ALU.mult)
                if j == 0:
                    ins = v.tensor_scalar(cT[:, 1, :], b[:, T:2 * T], conv_of[:, 1, R_QN:R_QN + 1], None, ALU.mult)
                evac(ins, f"cT_{j}")
            wait_evac(dve, "uq_2_1")
            qh = qtok.rearrange("p t (h c) -> p t h c", h=H)
            for t in range(TT):
                cs = cos_t[:, t, :].unsqueeze(1).to_broadcast([P, H, HR])
                sn = sin_t[:, t, :].unsqueeze(1).to_broadcast([P, H, HR])
                rotate(qh[:, t, :, NOPE:NOPE + HR], qh[:, t, :, NOPE + HR:QKD], cs, sn,
                       [rope_tmp[:, q, t, :, :] for q in range(4)]).then_inc(roped, 1)

            def heads(name, dst):
                for j in range(0, H // 2, 2):
                    b = wait_filled(dve, f"{name}_{j}")
                    evac(v.tensor_copy(dst[0:QKD, 2 * j:2 * j + 2, :], b[0:QKD, :].rearrange("p (a b) -> p a b", a=2)), f"{name}_{j}")

            heads("qT", qhT)
            kh = ktok.rearrange("p t (h c) -> p t h c", h=H)
            wait_filled(dve, f"qT_{H // 2 - 1}")
            for t in range(TT):
                v.tensor_copy(kh[:, t, :, NOPE:QKD], kr[:, t, :].unsqueeze(1).to_broadcast([P, H, ROPE])).then_inc(ktok_ready, 1)
            for n in range(4):
                b = wait_filled(dve, f"ukv_{n}_0")
                src = b[:, :].rearrange("p (h c) -> p h c", h=4)
                v.tensor_copy(kh[:, 0, 4 * n:4 * n + 4, 0:NOPE], src[:, :, 0:NOPE])
                evac(v.tensor_copy(vtok[:, 0, 4 * n * VD:4 * (n + 1) * VD].rearrange("p (h c) -> p h c", h=4), src[:, :, NOPE:]), f"ukv_{n}_0")
            heads("kT", khT)

            def m_max(hd):
                b = wait_filled(dve, f"ms_{hd}")
                sc = score[:, hd % 2, :]
                evac(v.tensor_tensor(sc, b[:, 0:3 * P], causal[:, :], ALU.add), f"ms_{hd}")
                wait_evac(dve, f"ms_{hd}")
                c = 32 + 4 * (hd % 2)
                v.tensor_reduce(out=stat[:, c:c + 1], in_=sc[:, 0:P], axis=AX.X, op=ALU.max)
                step(v.tensor_reduce(out=stat[:, c + 1:c + 2], in_=sc[:, P:3 * P], axis=AX.X, op=ALU.max))
                v.tensor_scalar(stat[:, c:c + 2], stat[:, c:c + 2], -MSCALE, None, ALU.mult).then_inc(m_max_ready, 1)

            m_max(0)
            for hd in range(H):
                if hd + 1 < H:
                    if hd >= 1:
                        dve.wait_ge(m_exp_ready, hd)
                        dve.wait_ge(m_prob_ready, hd)
                    m_max(hd + 1)
                dve.wait_ge(m_exp_ready, hd + 1)
                c = 34 + 4 * (hd % 2)
                step(v.reciprocal(stat[:, c:c + 2], stat[:, c:c + 2]))
                pr = prob[:, hd % 2, :]
                v.tensor_scalar(pr[:, 0:P], pr[:, 0:P], stat[:, c:c + 1], None, ALU.mult)
                v.tensor_scalar(pr[:, P:3 * P], pr[:, P:3 * P], stat[:, c + 1:c + 2], None, ALU.mult).then_inc(m_prob_ready, 1)
            add_residual("mw")
            cross(1)
            route(1)
            moe(1)
            dve.wait_ge(row_landed, 32)
            for t in range(TT):
                i = 7
                c = stat[:, 2 * i + t + 1:2 * i + t + 2]
                dve.wait_ge(rms_ready, 2 * i + t + 1)
                step(v.reciprocal(c, c))
                v.scalar_tensor_tensor(out=xhat[:, t, :], in0=h[:, t, :], scalar=c, in1=bcast_row[:, :],
                                       op0=ALU.mult, op1=ALU.mult).then_inc(normed, 1)

        @block.tensor
        def _(pe):
            mm = nc.tensor.matmul

            def fill(ins):
                ins.then_inc(bank_filled, 1)

            def turn_rows(name, rows):
                for j in range(4):
                    b = open_bank(pe, f"{name}_{j}")
                    for q in range(2):
                        for t in range(TT):
                            k = 2 * j + q
                            ins = nc.tensor.transpose(b[:, q * T + t * P:q * T + (t + 1) * P], rows[:, t, k::KD], ident[:, :])
                    fill(ins)

            def channel_major(name, u0, src):
                for j in range(4):
                    b = open_bank(pe, f"{name}_{j}")
                    wait_unit(pe, u0 + j)
                    w = unit(u0 + j, KD, 256)
                    for q in range(2):
                        for k in range(KD):
                            ins = mm(b[:, q * T:(q + 1) * T], lhsT=w[:, k, q * P:(q + 1) * P], rhs=src[:, k, :],
                                     start=(k == 0), stop=(k == KD - 1))
                    fill(ins)

            def token_major(name, u0, src, nk=KD, per=4, cols=HALF, parts=NH):
                for f in range(parts):
                    for t in range(TT):
                        b = open_bank(pe, f"{name}_{f}_{t}")
                        for k in range(nk):
                            u = u0 + f * (nk // per) + k // per
                            if t == 0 and k % per == 0:
                                wait_unit(pe, u)
                            ins = mm(b[:, 0:cols], lhsT=src[:, k, t * P:(t + 1) * P], rhs=unit(u, per, cols)[:, k % per, :],
                                     start=(k == 0), stop=(k == nk - 1))
                        fill(ins)

            pe.wait_ge(consts_ready, 2)
            pe.wait_ge(prm_landed, 16 * 11)
            b = open_bank(pe, "prm")
            for k in range(KD):
                nc.tensor.transpose(b[:, k * NA_ROWS:(k + 1) * NA_ROWS], prm_a[:, k::KD], ident[0:NA_ROWS, 0:NA_ROWS])
            o = KD * NA_ROWS
            for k in range(KD):
                ins = nc.tensor.transpose(b[:, o + k * NB_ROWS:o + (k + 1) * NB_ROWS], prm_b[:, k * P:(k + 1) * P],
                                          ident[0:NB_ROWS, 0:NB_ROWS])
            fill(ins)
            pe.wait_ge(normed, 2)
            turn_rows("n0", xhat)
            pe.wait_ge(normed, 4)
            turn_rows("mem", mem_rows)

            for j in (2, 3):
                wait_evac(pe, f"n0_{j}")
            for j in range(KD):
                b = open_bank(pe, f"glu_{j}")
                for part in range(2):
                    i = U_CIN + 2 * (j // 2) + part
                    if j % 2 == 0:
                        wait_unit(pe, i)
                    w = unit(i, KD, 256)
                    c = (j % 2) * P
                    for k in range(KD):
                        ins = mm(b[:, part * T:(part + 1) * T], lhsT=w[:, k, c:c + P], rhs=hT[:, k, :],
                                 start=(k == 0), stop=(k == KD - 1))
                fill(ins)
            for j in (2, 3):
                wait_evac(pe, f"mem_{j}")
            for l in range(2):
                channel_major(f"xk{l}", U_KV[l], memT[l])
                token_major(f"xv{l}", U_KV[l] + 4, memT[l])
            b = open_bank(pe, "mu")
            for k in range(KD):
                pe.wait_ge(conv_ready, k + 1)
                ins = mm(b[:, 0:T], lhsT=mean_of[:, :], rhs=conv[:, k, :], start=(k == 0), stop=(k == KD - 1))
            fill(ins)
            b = open_bank(pe, "var")
            for k in range(KD):
                pe.wait_ge(squared, k // 4 + 1)
                ins = mm(b[:, 0:T], lhsT=mean_of[:, :], rhs=conv_sq[:, k, :], start=(k == 0), stop=(k == KD - 1))
            fill(ins)
            pe.wait_ge(conv_act, KD)
            token_major("cout", U_COUT, hT)

            def cross(l):
                i = 2 if l == 0 else 5
                pe.wait_ge(normed, 2 * i + 2)
                turn_rows(f"nx{l}", xhat)
                for j in (2, 3):
                    wait_evac(pe, f"nx{l}_{j}")
                channel_major(f"xq{l}", U_XQ[l], hT)
                for j in (2, 3):
                    wait_evac(pe, f"xq{l}_{j}")
                for hd in range(XH):
                    b = open_bank(pe, f"xs{l}_{hd}")
                    for t in range(TT):
                        for c in range(2):
                            ins = mm(b[:, t * NMEM:(t + 1) * NMEM], lhsT=xqT[:, 2 * hd + c, t * P:(t + 1) * P],
                                     rhs=xkT[l][:, 2 * hd + c, :], start=(c == 0), stop=(c == 1))
                    fill(ins)

                def probs_turned(hd):
                    b = open_bank(pe, f"xp{l}_{hd}")
                    pe.wait_ge(x_prob_ready, XH * l + hd + 1)
                    for c in range(2):
                        for t in range(TT):
                            ins = nc.tensor.transpose(b[:, c * T + t * P:c * T + (t + 1) * P],
                                                      xprob[:, hd, t, c * P:(c + 1) * P], ident[:, :])
                    fill(ins)

                for hd in range(XH):
                    probs_turned(hd)
                    b = open_bank(pe, f"xo{l}_{hd}")
                    wait_evac(pe, f"xp{l}_{hd}")
                    for c in range(2):
                        for m in range(2):
                            ins = mm(b[:, c * T:(c + 1) * T], lhsT=xv[l][:, m, hd * XHD + c * P:hd * XHD + (c + 1) * P],
                                     rhs=xprobT[:, hd % 2, m * T:(m + 1) * T], start=(m == 0), stop=(m == 1))
                    fill(ins)
                wait_evac(pe, f"xo{l}_{XH - 1}")
                token_major(f"xw{l}", U_XO[l], hT)

            def route(l):
                i = 3 if l == 0 else 6
                pe.wait_ge(normed, 2 * i + 2)
                turn_rows(f"nf{l}", xhat)
                for j in (2, 3):
                    wait_evac(pe, f"nf{l}_{j}")
                pe.wait_ge(small_landed, 16 * 9)
                b = open_bank(pe, f"lg{l}")
                n = G + E
                for t in range(TT):
                    for k in range(KD):
                        ins = mm(b[:, t * n:(t + 1) * n], lhsT=hT[:, k, t * P:(t + 1) * P], rhs=router[:, l, k, :],
                                 start=(k == 0), stop=(k == KD - 1))
                fill(ins)
                pe.wait_ge(assigned, l + 1)
                taken = [rt[:, 280 + t * E:280 + (t + 1) * E] for t in range(TT)]
                b = open_bank(pe, f"rk{l}")
                mm(b[:, 0:E], lhsT=before[:, :], rhs=taken[0], start=True, stop=True)
                mm(b[:, E:2 * E], lhsT=ones[:, :], rhs=taken[0], start=True, stop=False)
                mm(b[:, E:2 * E], lhsT=before[:, :], rhs=taken[1], start=False, stop=True)
                mm(b[:, 2 * E:3 * E], lhsT=ones[:, :], rhs=taken[0], start=True, stop=False)
                ins = mm(b[:, 2 * E:3 * E], lhsT=ones[:, :], rhs=taken[1], start=False, stop=True)
                fill(ins)

            def run_part(pl):
                s = pl.s
                at = {"prologue": 0, "turn": len(FIRST_UNITS), "epilogue": len(FIRST_UNITS) + (TURNS - 1) * GU}[pl.part]

                def filled(ins):
                    ins.then_inc(s.sem["filled"], 1)

                def landed(what):
                    u = (FIRST_UNITS if pl.part == "prologue" else TURN_UNITS).index(what)
                    i = s.unit0 + at + u
                    slot = i % RING
                    a_turn = 16 * GU // RING if pl.part == "turn" else 0
                    a_repeat = 0 if pl.repeat is None else 16 * 3 * E // RING
                    pe.wait_ge(s.landed[slot], pl.value((16 * (i // RING + 1 - s.first_use[slot]), a_turn, a_repeat)))
                    return slot

                def gather():
                    k1 = TT
                    pe.wait_ge(s.picked, pl.value(pl.nth(k1, (TT, TT, 0))))
                    for k in range(KD):
                        b, = ready_at(pe, pl, [f"ga{k}"])
                        for t in range(TT):
                            ins = mm(b[:, 0:EG * CAP].rearrange("p (e c) -> p e c", e=EG), lhsT=xhat[:, t, k::KD],
                                     rhs=pick[:, t, :].rearrange("p (e s) -> p e s", e=EG)[:, :, 0:CAP],
                                     start=(t == 0), stop=(t == TT - 1))
                        filled(ins)

                def gate_up(j):
                    b, = ready_at(pe, pl, [f"gu{j}"], [f"ga{KD - 2}", f"ga{KD - 1}"] if j == 0 else [])
                    w = []
                    for e in range(2):
                        slot = landed(("gate", j, e))
                        landed(("up", j, e))
                        w.append(ring[:, slot * UNIT:(slot + 2) * UNIT].rearrange("p (g k n) -> p g k n", g=2, k=KD))
                    for k in range(KD):
                        for e in range(2):
                            ins = mm(b[e * SLOTS:(e + 1) * SLOTS, :].rearrange("p (g n) -> p g n", g=2),
                                     lhsT=xg[:, k, 2 * j + e, :], rhs=w[e][:, :, k, :],
                                     start=(k == 0), stop=(k == KD - 1), skip_group_check=True)
                    filled(ins)

                def puts(q):
                    b, = ready_at(pe, pl, [f"st{q}"])
                    if q == 0:
                        pe.wait_ge(s.weighted, pl.value(pl.nth(0, (TT, TT, 0))))
                    for jj in range(2):
                        for t in range(TT):
                            c = (2 * q + jj) * P
                            ins = nc.tensor.transpose(b[:, (jj * TT + t) * P:(jj * TT + t + 1) * P], pick[:, t, c:c + P], ident[:, :])
                    filled(ins)

                def mid(j):
                    if j:
                        b, = ready_at(pe, pl, [f"ht{j}"], [f"gu{j}"])
                    else:
                        b, = ready_at(pe, pl, ["ht0"])
                        pe.wait_ge(s.sem["mid"], pl.value(pl.nth(0, s.parts_of["mid"], s.base["mid"])))
                    for c in range(2):
                        ins = nc.tensor.transpose(b[:, c * P:(c + 1) * P], hmid[:, j % 2, c * P:(c + 1) * P], ident[:, :])
                    filled(ins)

                def downs(j):
                    bs = ready_at(pe, pl, [f"yd{j}_{f}" for f in range(NH)], [f"ht{j}"])
                    w = [unit(landed(("down", j, e)), FF // P, D) for e in range(2)]
                    for f in range(NH):
                        for c in range(FF // P):
                            for e in range(2):
                                ins = mm(bs[f][e * SLOTS:(e + 1) * SLOTS, :], lhsT=hmidT[:, c, e * SLOTS:(e + 1) * SLOTS],
                                         rhs=w[e][:, c, f * HALF:(f + 1) * HALF],
                                         start=(c == 0), stop=(c == FF // P - 1), skip_group_check=True)
                        filled(ins)

                def scatter(q):
                    copies = [f"yd{2 * q + 1}_{f}" for f in range(NH)]
                    for f in range(NH):
                        for t in range(TT):
                            b, = ready_at(pe, pl, [f"sc{q}_{f}_{t}"], copies if f == t == 0 else [])
                            for jj in range(2):
                                ins = mm(b[:, :], lhsT=put[:, 2 * q + jj, t, :], rhs=yslot[:, jj, f * HALF:(f + 1) * HALF],
                                         start=(jj == 0), stop=(jj == 1))
                            filled(ins)

                if pl.part == "prologue":
                    gather()
                    gate_up(0)
                    return
                puts(0)
                puts(1)
                gate_up(1)
                mid(0)
                downs(0)
                gate_up(2)
                mid(1)
                downs(1)
                gate_up(3)
                scatter(0)
                mid(2)
                downs(2)
                if pl.part == "turn":
                    gather()
                mid(3)
                downs(3)
                if pl.part == "turn":
                    gate_up(0)
                scatter(1)
                if pl.part == "epilogue":
                    for o, last in (("dve", f"sc1_{NH - 1}_{TT - 1}"), ("act", "yd3_1")):
                        pe.wait_ge(s.sem[o], pl.value(pl.freed(last)))
                        pe.nop()

            def sweep(s, repeat=None):
                run_part(Place(s, "prologue", repeat=repeat))
                with pe.Fori(0, TURNS - 1) as turn:
                    run_part(Place(s, "turn", turn, repeat))
                run_part(Place(s, "epilogue", repeat=repeat))

            def moe(l):
                a, b = sweeps[l]
                wait_evac(pe, f"rk{l}")
                wait_evac(pe, f"nf{l}_3")
                sweep(a)
                pe.wait_ge(routed, l + 1)
                n = pe.value_load(most[0:1, l:l + 1], min_val=0, max_val=T)
                with pe.If(n > CAP):
                    pe.sem_inc(b.sem["filled"], b.base["filled"])
                    with pe.Fori(0, REPEATS) as repeat:
                        sweep(b, repeat)

            cross(0)
            route(0)
            moe(0)

            pe.wait_ge(normed, 10)
            turn_rows("n4", xhat)
            for j in (2, 3):
                wait_evac(pe, f"n4_{j}")
            for t in range(TT):
                b = open_bank(pe, f"dnA_{t}")
                for k in range(KD):
                    i = U_DOWN + k // 4
                    if t == 0 and k % 4 == 0:
                        wait_unit(pe, i)
                    ins = mm(b[:, :], lhsT=hT[:, k, t * P:(t + 1) * P], rhs=unit(i, 4, HALF)[:, k % 4, :],
                             start=(k == 0), stop=(k == KD - 1))
                fill(ins)
            wait_unit(pe, U_DOWN + 2)
            for t in range(TT):
                b = open_bank(pe, f"dnB_{t}")
                for k in range(KD):
                    ins = mm(b[:, 0:DOWN - HALF], lhsT=hT[:, k, t * P:(t + 1) * P],
                             rhs=unit(U_DOWN + 2, KD, DOWN - HALF)[:, k, :], start=(k == 0), stop=(k == KD - 1))
                fill(ins)
            pe.wait_ge(down_ready, TT)
            for j in range(3):
                b = open_bank(pe, f"cT_{j}")
                for c in (2 * j, 2 * j + 1)[:2 if j < 2 else 1]:
                    for t in range(TT):
                        o = (c % 2) * T + t * P
                        ins = nc.tensor.transpose(b[:, o:o + P], down[:, t, c * P:(c + 1) * P], ident[:, :])
                fill(ins)
            for j in range(2):
                wait_evac(pe, f"cT_{j}")
            for n in range(3):
                wait_unit(pe, U_UQ + n)
                for t in range(TT):
                    b = open_bank(pe, f"uq_{n}_{t}")
                    for k in range(3):
                        ins = mm(b[:, :], lhsT=cT[:, k, t * P:(t + 1) * P], rhs=unit(U_UQ + n, 3, HALF)[:, k, :],
                                 start=(k == 0), stop=(k == 2))
                    fill(ins)
            pe.wait_ge(roped, TT)

            def heads(name, rows):
                for j in range(H // 2):
                    b = open_bank(pe, f"{name}_{j}")
                    for q in range(2):
                        for t in range(TT):
                            c = (2 * j + q) * QKD
                            ins = nc.tensor.transpose(b[0:QKD, q * T + t * P:q * T + (t + 1) * P], rows[:, t, c:c + QKD], ident[:, :])
                    fill(ins)

            heads("qT", qtok)
            wait_evac(pe, "cT_2")
            for n in range(4):
                if n % 2 == 0:
                    wait_unit(pe, U_UKV + n // 2)
                for t in range(TT):
                    b = open_bank(pe, f"ukv_{n}_{t}")
                    for k in range(2):
                        c = (n % 2) * HALF
                        ins = mm(b[:, :], lhsT=cT[:, 3 + k, t * P:(t + 1) * P], rhs=unit(U_UKV + n // 2, 2, D)[:, k, c:c + HALF],
                                 start=(k == 0), stop=(k == 1))
                    fill(ins)
            pe.wait_ge(ktok_ready, TT)
            for t in range(TT):
                wait_evac(pe, f"ukv_3_{t}")
            heads("kT", ktok)
            for j in (H // 2 - 2, H // 2 - 1):
                wait_evac(pe, f"qT_{j}")
                wait_evac(pe, f"kT_{j}")

            def scores(hd):
                b = open_bank(pe, f"ms_{hd}")
                mm(b[:, 0:P], lhsT=qhT[0:QKD, hd, 0:P], rhs=khT[0:QKD, hd, 0:P], start=True, stop=True)
                ins = mm(b[:, P:3 * P], lhsT=qhT[0:QKD, hd, P:2 * P], rhs=khT[0:QKD, hd, :], start=True, stop=True)
                fill(ins)

            scores(0)
            scores(1)
            for hd in range(H):
                if hd + 2 < H:
                    scores(hd + 2)
                b = open_bank(pe, f"mp_{hd}")
                pe.wait_ge(m_prob_ready, hd + 1)
                for c in range(3):
                    ins = nc.tensor.transpose(b[:, c * P:(c + 1) * P], prob[:, hd % 2, c * P:(c + 1) * P], ident[:, :])
                fill(ins)
                if hd % 2:
                    b = open_bank(pe, f"mo_{hd // 2}")
                    for g in range(2):
                        hh = hd - 1 + g
                        wait_evac(pe, f"mp_{hh}")
                        o = b[g * VD:(g + 1) * VD, :]
                        mm(o[:, 0:T], lhsT=vtok[:, 0, hh * VD:(hh + 1) * VD], rhs=probT[:, g, 0:T],
                           start=True, stop=False, skip_group_check=True)
                        ins = mm(o[:, P:T], lhsT=vtok[:, 1, hh * VD:(hh + 1) * VD], rhs=probT[:, g, T:3 * P],
                                 start=False, stop=True, skip_group_check=True)
                    fill(ins)
            wait_evac(pe, f"mo_{H // 2 - 1}")
            token_major("mw", U_MO, hT)
            cross(1)
            route(1)
            moe(1)


_INS = ["x", "mem", "positions", "norm_mix", "conv_w_in", "conv_b_in", "conv_w_dw", "conv_b_dw", "conv_ln_g",
        "conv_ln_b", "conv_w_out", "conv_b_out", "mla_w_down", "mla_q_norm", "mla_w_uq", "mla_kv_norm",
        "mla_w_ukv", "mla_w_o", "norm_xa", "norm_mem", "xa_wq", "xa_wkv", "xa_wo", "norm_ffn", "moe_w_grp",
        "moe_b_grp", "moe_w_exp", "moe_b_exp", "moe_w_gate", "moe_w_up", "moe_w_down", "final_norm"]


def kernel(**inputs):
    import numpy as _np
    import concourse.bacc as _bacc
    from concourse import mybir as _mybir
    from concourse.bass_utils import run_bass_kernel_spmd as _run

    nc = _bacc.Bacc("TRN2", target_bir_lowering=False, num_devices=1)
    arrays, args = {}, {}
    for name in _INS:
        a = _np.ascontiguousarray(inputs[name])
        arrays[f"in_{name}_dram"] = a
        args[name] = nc.dram_tensor(f"in_{name}_dram", a.shape, _mybir.dt.from_np(a.dtype), kind="ExternalInput").ap()
    shape = tuple(inputs["x"].shape)
    out = nc.dram_tensor("out_0_dram", shape, _mybir.dt.from_np(_np.dtype("float32")), kind="ExternalOutput").ap()
    trunk(nc, args, out)
    r = _run(nc, [arrays], core_ids=[0])
    return r.results[0]["out_0_dram"]
```

```python
from contextlib import ExitStack

import numpy as np

import concourse.bass as bass
from concourse import mybir

F32 = mybir.dt.float32
I32 = mybir.dt.int32
ALU = mybir.AluOpType
ACT = mybir.ActivationFunctionType
AX = mybir.AxisListType

P = 128
EPS = 1e-6
NEG = -1e30
RING = 12
UNIT = 2048
SLOTS = 32
QUAD = 4
NBANK = 8


class Tiles:

    def __init__(self):
        self.n = 0
        self.count = {"filled": 0, "dve": 0, "act": 0}
        self.at, self.order = {}, {}

    def add(self, name, owner):
        self.n += 1
        self.count["filled"] += 1
        self.count[owner] += 1
        self.at[name] = {"n": self.n - 1, "owner": owner, "filled": self.count["filled"], "freed": self.count[owner]}
        self.order[self.n - 1] = name


QUADS, HALVES, TOKEN_TILES = 2, 2, 2


def _down(q):
    return [(f"ht{q}", "act"), (f"yd{q}_0", "dve"), (f"yd{q}_1", "act")]


def _back(q):
    return [(f"sc{q}_{f}_{t}", "dve") for f in range(HALVES) for t in range(TOKEN_TILES)]


def _gather(q):
    return [(f"ga{q}_0", "ga_dve"), (f"ga{q}_1", "ga_act")]


TURN_TILES = (
    [("st", "act"), ("gu1", "mid")] + _down(0) + _back(0)
    + _gather(0) + _down(1) + [("gu0", "mid")] + _gather(1) + _back(1)
)
BANKS_A_TURN = -(-len(TURN_TILES) // NBANK) * NBANK
NEXT_TURNS = {"ga0_0", "ga0_1", "gu0", "ga1_0", "ga1_1"}
PARTS = {"prologue": [x for x in TURN_TILES if x[0] in NEXT_TURNS], "turn": TURN_TILES,
         "epilogue": [x for x in TURN_TILES if x[0] not in NEXT_TURNS]}
OWNERS = ("dve", "act", "mid", "ga_dve", "ga_act")


def _gate_up(q):
    return [(w, q, pair, half) for half in range(2) for pair in range(QUAD // 2) for w in ("gate", "up")]


FIRST_UNITS = _gate_up(0)
TURN_UNITS = _gate_up(1) + [("down", q, e, 0) for q in range(QUADS) for e in range(QUAD)] + FIRST_UNITS
EPILOGUE_UNITS = TURN_UNITS[:-len(FIRST_UNITS)]


class Place:

    def __init__(self, sweep, part, turn=None, repeat=None):
        self.s, self.part, self.turn, self.repeat = sweep, part, turn, repeat

    def nth(self, k, parts, base=0):
        p, b, e = parts
        turns = self.s.turns - 1
        a_turn = 0
        if self.part == "turn":
            k += p
            if isinstance(self.turn, int):
                k += self.turn * b
            else:
                a_turn = b
        elif self.part == "epilogue":
            k += p + turns * b
        return base + k, a_turn, 0 if self.repeat is None else p + turns * b + e

    def value(self, count):
        const, a_turn, a_repeat = count
        v = const
        assert const > 0
        if a_turn:
            v = self.turn * a_turn + v
        if a_repeat:
            v = self.repeat * a_repeat + v
        return v

    def tile(self, name):
        names = PARTS[self.part]
        i = [x[0] for x in names].index(name)
        return names[i][1], i, sum(x[1] == names[i][1] for x in names[:i + 1])

    def filled(self, name):
        return self.nth(self.tile(name)[1] + 1, self.s.parts_of["filled"], self.s.base["filled"])

    def freed(self, name, turns_ago=0):
        o, _, k = self.tile(name)
        parts = self.s.parts_of[o]
        return self.nth(k - turns_ago * parts[1], parts, self.s.base[o])

    def bank(self, name):
        i = [x[0] for x in TURN_TILES].index(name)
        return (self.s.bank0 + i) % NBANK

    def before(self, name):
        i = [x[0] for x in TURN_TILES].index(name) - NBANK
        if self.part == "turn":
            ago = 0
            while i < 0 or i >= len(TURN_TILES):
                if i < 0:
                    i, ago = i + BANKS_A_TURN, ago + 1
                else:
                    i -= NBANK
            last = TURN_TILES[i][0]
            return self.tile(last)[0], self.freed(last, ago)
        while i >= 0:
            if TURN_TILES[i][0] not in NEXT_TURNS:
                last = TURN_TILES[i][0]
                return self.tile(last)[0], self.freed(last)
            i -= NBANK
        i += BANKS_A_TURN
        while i >= len(TURN_TILES):
            i -= NBANK
        last_turn = Place(self.s, "turn", self.s.turns - 2, self.repeat)
        last = TURN_TILES[i][0]
        return last_turn.tile(last)[0], last_turn.freed(last)


def trunk(nc, A, out):
    _, T, D = A["x"].shape
    TT = T // P
    KD = D // P
    W = A["conv_w_dw"].shape[1]
    NMEM = A["mem"].shape[1]
    QR = A["mla_q_norm"].shape[1]
    KVR = A["mla_kv_norm"].shape[1]
    ROPE = A["mla_w_down"].shape[2] - QR - KVR
    DOWN = QR + KVR + ROPE
    NOPE = VD = 64
    QKD = NOPE + ROPE
    H = A["mla_w_uq"].shape[2] // QKD
    AHEAD = 4
    XH = 4
    XHD = D // XH
    E = A["moe_w_exp"].shape[2]
    G = A["moe_w_grp"].shape[2]
    EG = E // G
    FF = A["moe_w_gate"].shape[3]
    HALF = 512
    NH = D // HALF
    XSCALE = 1.0 / float(np.sqrt(XHD))
    MSCALE = 1.0 / float(np.sqrt(QKD))
    assert (T, D, NMEM, FF, EG, H, QKD) == (256, 1024, 256, 256, 8, 16, 96)
    assert (EG // QUAD, NH, TT) == (QUADS, HALVES, TOKEN_TILES)
    REPEATS = -(-T // SLOTS) - 1

    N_CIN, N_KV, N_COUT, N_XQ, N_XO = 8, 8, 4, 4, 4
    N_MLA_DOWN, N_UQ, N_UKV, N_MO = 3, 3, 2, 4
    U_CIN = 0
    LATE_KEYS = 2
    U_XK0 = N_CIN
    U_XK1 = U_XK0 + N_KV
    U_COUT = U_XK1 + N_KV // 2 - LATE_KEYS
    U_XV1 = [U_COUT + N_COUT]
    U_XQ0 = U_XV1[0] + 2
    U_XO0 = U_XQ0 + N_XQ
    U_XV1.append(U_XO0 + N_XO)
    U_MOE0 = U_XV1[1] + 2
    U_XV = [[U_XK0 + 4, U_XK0 + 6], U_XV1]
    U_LATE = U_MOE0 + len(FIRST_UNITS)
    U_XK = [[U_XK0 + j for j in range(4)], [U_LATE + j if j < LATE_KEYS else U_XK1 + j - LATE_KEYS for j in range(4)]]
    U_DOWN = U_MOE0 + 3 * E + LATE_KEYS
    U_UQ = U_DOWN + N_MLA_DOWN
    U_UKV = U_UQ + N_UQ
    U_MO = U_UKV + N_UKV
    U_XQ1 = U_MO + N_MO
    U_XO1 = U_XQ1 + N_XQ
    U_MOE1 = U_XO1 + N_XO
    U_XQ, U_XO, U_MOE = [U_XQ0, U_XQ1], [U_XO0, U_XO1], [U_MOE0, U_MOE1]
    GU = 3 * EG
    TURNS = G

    tiles = Tiles()
    alt = ("dve", "act")
    tiles.add("prm", "dve")
    for j in range(4):
        tiles.add(f"n0_{j}", alt[j % 2])
    tiles.add("glu_0", "dve")
    for j in range(4):
        tiles.add(f"mem_{j}", alt[j % 2])
    for j in range(1, KD):
        tiles.add(f"glu_{j}", "dve")
    for j in range(4):
        tiles.add(f"xk0_{j}", "act")
    for f in range(NH):
        for t in range(TT):
            tiles.add(f"xv0_{f}_{t}", "act")
    tiles.add("mu", "dve")
    tiles.add("xk1_2", "act")
    tiles.add("var", "act")
    tiles.add("xk1_3", "act")

    def add_out(name):
        for f in range(NH):
            for t in range(TT):
                tiles.add(f"{name}_{f}_{t}", "dve")

    ALL_TILES = {o: tuple(sum(x[1] == o for x in PARTS[p]) for p in ("prologue", "turn", "epilogue")) for o in OWNERS}
    ALL_TILES["filled"] = tuple(len(PARTS[p]) for p in ("prologue", "turn", "epilogue"))
    in_a_sweep = {o: n[0] + n[1] * (TURNS - 1) + n[2] for o, n in ALL_TILES.items()}
    before_moe = []

    add_out("cout")
    for l in range(2):
        if l == 1:
            for j in range(4):
                tiles.add(f"n4_{j}", alt[j % 2])
            for t in range(TT):
                tiles.add(f"dnA_{t}", "act")
                tiles.add(f"dnB_{t}", "act")
            for j in range(3):
                tiles.add(f"cT_{j}", alt[j % 2])
            for t in range(TT):
                for n in range(3):
                    tiles.add(f"uq_{n}_{t}", "act")
            for n in range(4):
                for t in range(TT):
                    tiles.add(f"ukv_{n}_{t}", alt[t % 2])
            for j in range(H // 2):
                tiles.add(f"qT_{j}", alt[j % 2])
            for j in range(H // 2):
                tiles.add(f"kT_{j}", alt[j % 2])
            for hd in range(AHEAD):
                tiles.add(f"ms_{hd}", "dve")
            for hd in range(H):
                if hd + AHEAD < H:
                    tiles.add(f"ms_{hd + AHEAD}", "dve")
                tiles.add(f"mp_{hd}", "act")
                if hd % 2:
                    tiles.add(f"mo_{hd // 2}", "act")
            add_out("mw")
        if l == 0:
            tiles.add("xv1_0_0", "act")
        for j in range(4):
            tiles.add(f"nx{l}_{j}", alt[j % 2])
        for j in range(4):
            tiles.add(f"xq{l}_{j}", alt[j % 2])
        for hd in range(XH):
            tiles.add(f"xs{l}_{hd}", "act")
        if l == 0:
            tiles.add("xv1_0_1", "act")
        tiles.add(f"xp{l}_0", "act")
        for hd in range(XH):
            if hd + 1 < XH:
                tiles.add(f"xp{l}_{hd + 1}", "act")
            tiles.add(f"xo{l}_{hd}", "dve")
        add_out(f"xw{l}")
        if l == 0:
            tiles.add("xv1_1_0", "act")
        for j in range(4):
            tiles.add(f"nf{l}_{j}", alt[j % 2])
        tiles.add(f"lg{l}", "dve")
        if l == 0:
            tiles.add("xv1_1_1", "act")
        tiles.add(f"rk{l}", "dve")
        before_moe.append(dict(tiles.count, mid=0, ga_dve=0, ga_act=0))
        for o in ("filled", "dve", "act"):
            tiles.count[o] += in_a_sweep[o]

    ctx = ExitStack()
    with ctx:
        def sb(name, shape, dt=F32):
            return ctx.enter_context(nc.sbuf_tensor(name, shape, dt))

        def sem(name):
            return ctx.enter_context(nc.semaphore(name))

        banks = [ctx.enter_context(nc.psum_tensor(f"bank{i}", [P, 512], F32)) for i in range(NBANK)]

        ring = sb("ring", [P, RING * UNIT])
        h = sb("h", [P, TT, D])
        xhat = sb("xhat", [P, TT, D])
        hT = sb("hT", [P, KD, T])
        kv0 = sb("kv0", [P, 4096])
        kv1 = sb("kv1", [P, 4096])
        scratch = sb("scratch", [P, 9984])
        bcast_row = sb("bcast_row", [P, D])
        ident = sb("ident", [P, P])
        before = sb("before", [P, P])
        ones = sb("ones", [P, P])
        mean_of = sb("mean_of", [P, P])
        slot_no = sb("slot_no", [P, SLOTS])
        slot_no_i = sb("slot_no_i", [P, SLOTS], I32)
        desc = sb("desc", [P, EG])
        causal = sb("causal", [P, 3 * P])
        router = sb("router", [P, 2, KD, G + E])
        router_b = sb("router_b", [P, 2, G + E])
        NA_ROWS, NB_ROWS = 8, W + 7
        prmT = sb("prmT", [P, KD * (NA_ROWS + NB_ROWS)])
        stat = sb("stat", [P, 64])
        rt = sb("rt", [P, 512])
        pos_i = sb("pos_i", [P, TT], I32)
        rope_t = sb("rope_t", [P, 6, TT, ROPE // 2])
        rope_i = sb("rope_i", [P, TT, ROPE // 2], I32)
        most = sb("most", [P, 2], I32)

        gain_of = prmT[:, 0:KD * NA_ROWS].rearrange("p (k r) -> p k r", k=KD)
        conv_of = prmT[:, KD * NA_ROWS:].rearrange("p (k r) -> p k r", k=KD)
        R_MIX, R_XA, R_MEM, R_FFN = 0, 2, 4, 6
        R_BDW, R_LNG, R_LNB, R_BA, R_BG, R_QN, R_KVN = range(W, W + 7)
        prm_a = kv1[0:NA_ROWS, 0:D]
        prm_b = kv1[0:NB_ROWS, D:2 * D]

        def view(t, at, *shape):
            n = int(np.prod(shape))
            v = t[:, at:at + n]
            if len(shape) == 2:
                return v.rearrange("p (a b) -> p a b", a=shape[0])
            if len(shape) == 3:
                return v.rearrange("p (a b c) -> p a b c", a=shape[0], b=shape[1])
            return v

        xkT = [view(kv0, 0, KD, NMEM), view(kv1, 0, KD, NMEM)]
        xv = [view(kv0, 2048, 2, D), view(kv1, 2048, 2, D)]
        PADDED = W - 1 + T
        u_pad = view(scratch, 0, KD, PADDED)
        conv = view(scratch, 2304, KD, T)
        mem_rows = view(scratch, 4352, 2, D)
        conv_sq = view(scratch, 4352, KD, T)
        memT = [xhat[:, :, :].rearrange("p a b -> p (a b)").rearrange("p (k m) -> p k m", k=KD), view(scratch, 6400, KD, NMEM)]
        sig = view(scratch, 8448, 2, T)
        ln_rstd = view(scratch, 8960, T)
        ln_sum = view(scratch, 9216, T)
        pooled_tap = view(scratch, 9472, T)
        POOLED = 1
        xqT = view(scratch, 0, KD, T)
        xprob = view(scratch, 2048, XH, TT, NMEM)
        xprobT = view(scratch, 4096, 2, 2 * T)
        qtok = view(scratch, 0, TT, H * QKD)
        ktok = [hT[:, :, :].rearrange("p k t -> p (k t)")[:, 0:H * QKD], view(scratch, 7168, H * QKD)]
        qhT = view(scratch, 3072, H, T)
        khT = view(kv0, 0, H, T)
        vtok = xhat
        down = view(scratch, 7168, TT, DOWN)
        cT = view(scratch, 8704, 5, T)
        rope_tmp = scratch[:, 3072:3072 + 4 * TT * H * (ROPE // 2)].rearrange(
            "p (n t h r) -> p n t h r", n=4, t=TT, h=H)
        shared_key = view(rt, 0, TT, ROPE)
        squares_junk = view(scratch, 5120, 2 * TT, 384)
        DEPTH = 4
        score = view(scratch, 0, DEPTH, 3 * P)
        prob = view(scratch, DEPTH * 3 * P, DEPTH, 3 * P)
        probT = view(scratch, 7168, 2, 3 * P)
        xg = scratch[:, 0:KD * EG * SLOTS].rearrange("p (k e c) -> p k e c", k=KD, e=EG)
        pick = view(scratch, 2048, TT, EG * SLOTS)
        yslot = view(scratch, 2560, QUADS, D)
        put = view(scratch, 4608, QUADS, TT, P)
        hmid = view(scratch, 5120, QUADS, FF)
        gated = view(scratch, 5632, QUADS, FF)
        hmidT = view(scratch, 6144, FF // P, P)

        bank_filled, dve_freed, act_freed = sem("bank_filled"), sem("dve_freed"), sem("act_freed")
        unit_landed = [sem(f"unit_landed{i}") for i in range(RING)]
        rows_cleared, mem_landed, pos_landed, prm_landed, small_landed, row_landed = (
            sem("rows_cleared"),
            sem("mem_landed"), sem("pos_landed"), sem("prm_landed"), sem("small_landed"), sem("row_landed"))
        x_landed = [sem(f"x_landed{t}") for t in range(TT)]
        pool_step, consts_ready, bias_added = sem("pool_step"), sem("consts_ready"), sem("bias_added")
        rms_ready, normed = sem("rms_ready"), sem("normed")
        dve_step, act_step = sem("dve_step"), sem("act_step")
        sig_ready, conv_ready, centred, squared, ln_scaled, swished = (
            sem("sig_ready"), sem("conv_ready"), sem("centred"), sem("squared"), sem("ln_scaled"), sem("swished"))
        angles_ready, sincos_ready = sem("angles_ready"), sem("sincos_ready")
        x_max_ready, x_exp_ready, x_prob_ready = sem("x_max_ready"), sem("x_exp_ready"), sem("x_prob_ready")
        down_rms_ready = sem("down_rms_ready")
        down_ready, roped, ktok_ready = sem("down_ready"), sem("roped"), sem("ktok_ready")
        m_max_ready, m_exp_ready, m_prob_ready = sem("m_max_ready"), sem("m_exp_ready"), sem("m_prob_ready")
        m_sum_ready, m_part_ready = sem("m_sum_ready"), sem("m_part_ready")
        route_diff, route_exp, assigned, routed = (
            sem("route_diff"), sem("route_exp"), sem("assigned"), sem("routed"))
        pooled_ready = sem("pooled_ready")
        summed, late_filled, late_kept = sem("summed"), sem("late_filled"), sem("late_kept")
        stored = sem("stored")

        class Sweep:
            pass

        sweeps = []
        for l in range(2):
            a, b = Sweep(), Sweep()
            own = {x: sem(f"{x}_freed{l}") for x in ("mid", "ga_dve", "ga_act")}
            a.sem = {"filled": bank_filled, "dve": dve_freed, "act": act_freed, **own}
            a.base = before_moe[l]
            a.landed, a.unit0, a.first_use = unit_landed, U_MOE[l], [0] * RING
            a.late, b.late = LATE_KEYS if l == 0 else 0, 0
            b.sem = {x: sem(f"more_{x}{l}") for x in ("filled",) + OWNERS}
            b.base = {"filled": ALL_TILES["filled"][1], "dve": ALL_TILES["dve"][1], "act": ALL_TILES["act"][1],
                      "mid": 0, "ga_dve": 0, "ga_act": 0}
            b.landed = [sem(f"more_landed{l}_{i}") for i in range(RING)]
            b.unit0 = U_MOE[l] % RING
            b.first_use = [1 if i < b.unit0 else 0 for i in range(RING)]
            b.shifted = sem(f"slots_shifted{l}")
            for s, tag in ((a, ""), (b, "more_")):
                s.l, s.turns, s.parts_of, s.bank0 = l, TURNS, ALL_TILES, 0
                s.half_used = sem(f"{tag}half_used{l}")
                s.picked, s.weighted, s.gate_ready = sem(f"{tag}picked{l}"), sem(f"{tag}weighted{l}"), sem(f"{tag}gate_ready{l}")
            sweeps.append((a, b))

        def wait_filled(eng, name):
            eng.wait_ge(bank_filled, tiles.at[name]["filled"])
            return banks[tiles.at[name]["n"] % NBANK]

        def wait_evac(eng, name):
            x = tiles.at[name]
            eng.wait_ge(dve_freed if x["owner"] == "dve" else act_freed, x["freed"])

        def evac(ins, name):
            ins.then_inc(dve_freed if tiles.at[name]["owner"] == "dve" else act_freed, 1)

        def open_bank(pe, name):
            n = tiles.at[name]["n"]
            if n >= NBANK:
                wait_evac(pe, tiles.order[n - NBANK])
            return banks[n % NBANK]

        def filled_at(eng, pl, name):
            eng.wait_ge(pl.s.sem["filled"], pl.value(pl.filled(name)))
            return banks[pl.bank(name)]

        def copied_at(ins, pl, name):
            ins.then_inc(pl.s.sem[pl.tile(name)[0]], 1)

        def ready_at(pe, pl, banks_of=(), copies_of=()):
            need = []
            if pl.part != "prologue":
                need += [pl.before(x) for x in banks_of]
            need += [(pl.tile(x)[0], pl.freed(x)) for x in copies_of]
            for o in OWNERS:
                mine = [count for owner, count in need if owner == o]
                if mine:
                    pe.wait_ge(pl.s.sem[o], pl.value(max(mine)))
            return [banks[pl.bank(x)] for x in banks_of]

        def unit(i, *shape):
            s = (i % RING) * UNIT
            v = ring[:, s:s + int(np.prod(shape))]
            if len(shape) == 2:
                return v.rearrange("p (a b) -> p a b", a=shape[0])
            return v

        def wait_unit(eng, i):
            eng.wait_ge(unit_landed[i % RING], 16 * (i // RING + 1))

        last_tile = {}
        for j in range(N_CIN):
            last_tile[U_CIN + j] = f"glu_{2 * (j // 2) + 1}"

        def last_of(u0, name, per_unit_tile):
            for j in range(4):
                last_tile[u0 + j] = f"{name}_{j}" if per_unit_tile else f"{name}_{j // 2}_{TT - 1}"

        for l in range(2):
            for j in range(4):
                last_tile[U_XK[l][j]] = (late_filled, j + 1) if l == 1 and j < LATE_KEYS else f"xk{l}_{j}"
            for f in range(NH):
                for q in range(2):
                    last_tile[U_XV[l][f] + q] = f"xv{l}_{f}_{TT - 1}"
            last_of(U_XQ[l], f"xq{l}", True)
            last_of(U_XO[l], f"xw{l}", False)
        last_of(U_COUT, "cout", False)
        last_of(U_MO, "mw", False)
        last_tile.update({U_DOWN: f"dnA_{TT - 1}", U_DOWN + 1: f"dnA_{TT - 1}", U_DOWN + 2: f"dnB_{TT - 1}"})
        last_tile.update({U_UQ + n: f"uq_{n}_{TT - 1}" for n in range(N_UQ)})
        last_tile.update({U_UKV + n: f"ukv_{2 * n + 1}_{TT - 1}" for n in range(N_UKV)})

        def unit_used(pl, what):
            kind, quad, _, half = what
            if kind == "down":
                return pl.s.sem["filled"], pl.filled(f"yd{quad}_{NH - 1}")
            if half:
                return pl.s.sem["filled"], pl.filled(f"gu{quad}")
            k = 1 if quad or pl.part == "prologue" else QUADS
            return pl.s.half_used, pl.nth(k, (1, QUADS, QUADS - 1))

        for l in range(2):
            behind = len(FIRST_UNITS) + sweeps[l][0].late
            for part, units, u0 in (("prologue", FIRST_UNITS, 0), ("epilogue", EPILOGUE_UNITS, behind + (TURNS - 1) * GU)):
                for u, what in enumerate(units):
                    used, count = unit_used(Place(sweeps[l][0], part), what)
                    last_tile[U_MOE[l] + u0 + u] = used, count[0]

        LATE_BANK = 3

        block = ctx.enter_context(nc.Block())

        @block.sync
        def _(sp):
            def slot_free(i):
                if i >= RING:
                    last = last_tile[i - RING]
                    if isinstance(last, tuple):
                        sp.wait_ge(*last)
                    else:
                        wait_filled(sp, last)

            def load(i, src, *shape):
                slot_free(i)
                sp.dma_start(unit(i, *shape), src).then_inc(unit_landed[i % RING], 16)

            def by_channel(i, w, cols):
                load(i, w.rearrange("(p k) n -> p k n", k=KD)[:, :, cols:cols + 256], KD, 256)

            def k_by_p(i, w, f):
                for q in range(2):
                    src = w.rearrange("(k p) n -> p k n", p=P)[:, 4 * q:4 * q + 4, f * HALF:(f + 1) * HALF]
                    load(i + q, src, 4, HALF)

            def p_by_k(i, w, c0, n):
                for q in range(2):
                    src = w.rearrange("(p k) n -> p k n", k=KD)[:, 4 * q:4 * q + 4, c0:c0 + n]
                    load(i + q, src, 4, n)

            for t in range(TT):
                sp.dma_start(h[:, t, :], A["x"][0, t * P:(t + 1) * P, :]).then_inc(x_landed[t], 16)
            w_in = A["conv_w_in"][0]
            for j in range(4):
                if j == 0:
                    sp.wait_ge(rows_cleared, 1)
                    for dst, src in (
                            (prm_b[R_BDW:R_BDW + 1, :], A["conv_b_dw"]),
                            (prm_b[R_LNG:R_LNG + 1, :], A["conv_ln_g"]),
                            (prm_b[R_LNB:R_LNB + 1, :], A["conv_ln_b"]),
                            (prm_b[R_BA:R_BG + 1, :], A["conv_b_in"][0].rearrange("(r n) -> r n", r=2)),
                            (prm_b[R_QN:R_QN + 1, 0:QR], A["mla_q_norm"]),
                            (prm_b[R_KVN:R_KVN + 1, 0:KVR], A["mla_kv_norm"])):
                        sp.dma_start(dst, src).then_inc(prm_landed, 16)
                by_channel(U_CIN + 2 * j, w_in, 256 * j)
                by_channel(U_CIN + 2 * j + 1, w_in, D + 256 * j)
                if j == 0:
                    sp.dma_start(mem_rows, A["mem"][0].rearrange("(t p) d -> p t d", p=P)).then_inc(mem_landed, 16)
                if j == 1:
                    sp.dma_start(bcast_row[:, :], A["conv_b_out"].partition_broadcast(P)).then_inc(row_landed, 16)
                    sp.dma_start(pos_i[:, :], A["positions"][0].rearrange("(t p) -> p t", p=P),
                                 allow_slow_non_contiguous=True).then_inc(pos_landed, 16)
                if j >= 2:
                    l = j - 2
                    sp.dma_start(router[:, l, :, 0:G], A["moe_w_grp"][l].rearrange("(p k) n -> p k n", k=KD),
                                 allow_slow_non_contiguous=True).then_inc(small_landed, 16)
                    sp.dma_start(router[:, l, :, G:], A["moe_w_exp"][l].rearrange("(p k) n -> p k n", k=KD),
                                 allow_slow_non_contiguous=True).then_inc(small_landed, 16)
                    sp.dma_start(router_b[:, l, 0:G], A["moe_b_grp"][l:l + 1, :].partition_broadcast(P)).then_inc(small_landed, 16)
                    sp.dma_start(router_b[:, l, G:], A["moe_b_exp"][l:l + 1, :].partition_broadcast(P)).then_inc(small_landed, 16)

            def keys(l):
                for j in range(4):
                    if l == 0 or j >= LATE_KEYS:
                        by_channel(U_XK[l][j], A["xa_wkv"][l], 256 * j)

            def values(l, f):
                p_by_k(U_XV[l][f], A["xa_wkv"][l], D + f * HALF, HALF)

            keys(0)
            for f in range(NH):
                values(0, f)
            keys(1)
            for f in range(NH):
                k_by_p(U_COUT + 2 * f, A["conv_w_out"][0], f)

            def cross(l):
                if l == 0:
                    values(1, 0)
                for j in range(4):
                    by_channel(U_XQ[l] + j, A["xa_wq"][l], 256 * j)
                for f in range(NH):
                    k_by_p(U_XO[l] + 2 * f, A["xa_wo"][l], f)
                if l == 0:
                    values(1, 1)

            def load_expert(s, what, group, slot):
                kind, quad, which, half = what
                if kind == "down":
                    ex = group * EG + (quad * QUAD + which)
                    src, dst = A["moe_w_down"][s.l, ex].rearrange("(k p) n -> p k n", p=P), unit(slot, FF // P, D)
                else:
                    ex = group * EG + (quad * QUAD + 2 * which)
                    src = A[f"moe_w_{kind}"][s.l, bass.ds(ex, 2)].rearrange("e (p k) n -> p e k n", k=KD)
                    src = src[:, :, half * KD // 2:(half + 1) * KD // 2, :]
                    dst = unit(slot, UNIT).rearrange("p (e k n) -> p e k n", e=2, k=KD // 2)
                sp.dma_start(dst, src).then_inc(s.landed[slot % RING], 16)

            def sweep(s, repeat=None):
                n1, first = len(FIRST_UNITS) + s.late, s.unit0
                if repeat is not None:
                    sp.wait_ge(s.sem["filled"], repeat * in_a_sweep["filled"] + s.base["filled"])
                late = [("key", j) for j in range(s.late)]
                for i, what in enumerate(FIRST_UNITS + late + TURN_UNITS[:RING]):
                    if what[0] == "key":
                        by_channel(U_XK[1][what[1]], A["xa_wkv"][1], 256 * what[1])
                        continue
                    if repeat is None:
                        slot_free(first + i)
                    elif i >= RING:
                        pl = Place(s, "prologue", repeat=repeat)
                        used, count = unit_used(pl, FIRST_UNITS[i - RING])
                        sp.wait_ge(used, pl.value(count))
                    load_expert(s, what, 0, first + i)
                with sp.Fori(0, TURNS - 1) as turn:
                    pl = Place(s, "turn", turn, repeat)
                    for u in range(RING, GU):
                        used, count = unit_used(pl, TURN_UNITS[u - RING])
                        sp.wait_ge(used, pl.value(count))
                        if u < GU - len(FIRST_UNITS):
                            load_expert(s, TURN_UNITS[u], turn, first + n1 + u)
                        else:
                            load_expert(s, TURN_UNITS[u], turn + 1, first + n1 + u)
                    for u in range(RING):
                        used, count = unit_used(pl, TURN_UNITS[u + RING])
                        sp.wait_ge(used, pl.value(count))
                        load_expert(s, TURN_UNITS[u], turn + 1, first + n1 + u)
                pl = Place(s, "epilogue", repeat=repeat)
                for u in range(RING, len(EPILOGUE_UNITS)):
                    used, count = unit_used(pl, TURN_UNITS[u - RING])
                    sp.wait_ge(used, pl.value(count))
                    load_expert(s, TURN_UNITS[u], TURNS - 1, first + n1 + u)

            def moe(l):
                a, b = sweeps[l]
                sweep(a)
                sp.wait_ge(routed, l + 1)
                n = sp.value_load(most[0:1, l:l + 1], min_val=0, max_val=T)
                with sp.If(n > SLOTS):
                    with sp.Fori(0, REPEATS) as repeat:
                        sweep(b, repeat)
                    sp.wait_ge(b.sem["filled"], b.base["filled"] + REPEATS * in_a_sweep["filled"])

            cross(0)
            moe(0)
            p_by_k(U_DOWN, A["mla_w_down"][0], 0, HALF)
            load(U_DOWN + 2, A["mla_w_down"][0].rearrange("(p k) n -> p k n", k=KD)[:, :, HALF:DOWN], KD, DOWN - HALF)
            for n in range(3):
                load(U_UQ + n, A["mla_w_uq"][0].rearrange("(k p) n -> p k n", p=P)[:, :, n * HALF:(n + 1) * HALF], 3, HALF)
            for n in range(2):
                load(U_UKV + n, A["mla_w_ukv"][0].rearrange("(k p) n -> p k n", p=P)[:, :, n * D:(n + 1) * D], 2, D)
            for f in range(NH):
                k_by_p(U_MO + 2 * f, A["mla_w_o"][0], f)
            cross(1)
            moe(1)
            for t in range(TT):
                sp.wait_ge(normed, 14 + t + 1)
                sp.dma_start(out[0, t * P:(t + 1) * P, :], xhat[:, t, :]).then_inc(stored, 16)
            sp.wait_ge(stored, 16 * TT)

        @block.gpsimd
        def _(pool):
            n = 0

            def step(ins):
                nonlocal n
                n += 1
                ins.then_inc(pool_step, 1)
                pool.wait_ge(pool_step, n)

            nc.gpsimd.memset(prm_b[32:NB_ROWS, :], 0.0).then_inc(rows_cleared, 1)
            pool.wait_ge(rows_cleared, 1)
            nc.gpsimd.memset(ident[:, :], 0.0).then_inc(consts_ready, 1)
            pool.wait_ge(consts_ready, 1)
            nc.gpsimd.affine_select(out=ident[:, :], in_=ident[:, :], compare_op=ALU.not_equal, fill=1.0,
                                    base=0, pattern=[[-1, P]], channel_multiplier=1).then_inc(consts_ready, 1)
            pool.wait_ge(consts_ready, 2)
            nc.gpsimd.memset(stat[:, 63:64], EPS).then_inc(consts_ready, 1)
            pool.wait_ge(consts_ready, 3)
            step(nc.gpsimd.memset(ones[:, :], 1.0))
            step(nc.gpsimd.affine_select(out=before[:, :], in_=ones[:, :], compare_op=ALU.is_gt, fill=0.0,
                                         base=0, pattern=[[1, P]], channel_multiplier=-1))
            step(nc.gpsimd.memset(mean_of[:, :], 1.0 / D))
            step(nc.gpsimd.memset(u_pad[:, :, 0:W - 1], 0.0))
            step(nc.gpsimd.iota(slot_no_i[:, :], pattern=[[1, SLOTS]], base=0, channel_multiplier=0))
            step(nc.gpsimd.tensor_copy(slot_no[:, :], slot_no_i[:, :]))
            step(nc.gpsimd.tensor_scalar(desc[:, :], slot_no[:, 0:EG], -1.0, float(EG), ALU.mult, ALU.add))
            step(nc.gpsimd.memset(causal[:, :], 0.0))
            for c in (0, 2):
                step(nc.gpsimd.affine_select(out=causal[:, c * P:(c + 1) * P], in_=causal[:, c * P:(c + 1) * P],
                                             compare_op=ALU.is_ge, fill=NEG, base=0, pattern=[[-1, P]],
                                             channel_multiplier=1))
            inv = 1.0 / (np.float32(10000.0) ** (np.arange(0, ROPE, 2, dtype=np.float32) / np.float32(ROPE)))
            for i in range(ROPE // 2):
                step(nc.gpsimd.memset(rope_t[:, 0, :, i:i + 1], float(np.float32(inv[i]))))
            nc.gpsimd.memset(stat[:, 61:62], 0.0).then_inc(consts_ready, 1)
            wait_evac(pool, f"glu_{POOLED}")
            for tap in range(W):
                taps, w = u_pad[:, POOLED, tap:tap + T], conv_of[:, POOLED, tap:tap + 1]
                if tap == 0:
                    step(nc.gpsimd.tensor_scalar(conv[:, POOLED, :], taps, w, conv_of[:, POOLED, R_BDW:R_BDW + 1], ALU.mult, ALU.add))
                else:
                    step(nc.gpsimd.tensor_scalar(pooled_tap, taps, w, None, ALU.mult))
                    ins = nc.gpsimd.tensor_tensor(conv[:, POOLED, :], conv[:, POOLED, :], pooled_tap, ALU.add)
                    if tap < W - 1:
                        step(ins)
            ins.then_inc(pooled_ready, 1)
            pool.wait_ge(pooled_ready, 1)
            pool.wait_ge(row_landed, 16)
            for t in range(TT):
                pool.wait_ge(normed, t + 1)
                nc.gpsimd.tensor_tensor(h[:, t, :], h[:, t, :], bcast_row[:, :], ALU.add).then_inc(bias_added, 1)

            for hd in range(H):
                pool.wait_ge(m_sum_ready, hd + 1)
                c = 34 + 4 * (hd % DEPTH)
                pr = prob[:, hd % DEPTH, :]
                nc.gpsimd.tensor_scalar(pr[:, 0:P], pr[:, 0:P], stat[:, c:c + 1], None, ALU.mult).then_inc(m_part_ready, 1)
                pool.wait_ge(m_part_ready, hd + 1)
                nc.gpsimd.tensor_scalar(pr[:, P:3 * P], pr[:, P:3 * P], stat[:, c + 1:c + 2], None,
                                        ALU.mult).then_inc(m_prob_ready, 1)

        @block.scalar
        def _(act):
            def copy(dst, src):
                return nc.scalar.activation(dst, src, ACT.Copy)

            for dst, src in ((prm_a[R_MIX:R_MIX + 2, :], A["norm_mix"]), (prm_a[R_XA:R_XA + 2, :], A["norm_xa"]),
                             (prm_a[R_MEM:R_MEM + 2, :], A["norm_mem"]), (prm_a[R_FFN:R_FFN + 2, :], A["norm_ffn"])):
                act.dma_start(dst, src).then_inc(prm_landed, 16)
            act.wait_ge(rows_cleared, 1)
            act.dma_start(prm_b[0:W, :], A["conv_w_dw"][0]).then_inc(prm_landed, 16)
            n_steps = 0

            def root_mean_square(src, c, n, junk):
                nonlocal n_steps
                n_steps += 1
                nc.scalar.activation(junk, src, ACT.Square, accum_out=c).then_inc(act_step, 1)
                act.wait_ge(act_step, n_steps)
                return nc.scalar.activation(c, c, ACT.Sqrt, bias=stat[:, 63:64], scale=1.0 / n)

            def load_table(function):
                nonlocal n_steps
                n_steps += 1
                nc.scalar.activation(stat[:, 62:63], stat[:, 63:64], function).then_inc(act_step, 1)
                act.wait_ge(act_step, n_steps)

            def rms(i, src, t, junk):
                root_mean_square(src, stat[:, 2 * i + t + 1:2 * i + t + 2], D, junk).then_inc(rms_ready, 1)

            def gained(name, row):
                for j in (1, 3):
                    b = wait_filled(act, f"{name}_{j}")
                    for q in range(2):
                        k = 2 * j + q
                        ins = nc.scalar.activation(hT[:, k, :], b[:, q * T:(q + 1) * T], ACT.Copy,
                                                   scale=gain_of[:, k, row:row + 1])
                    evac(ins, f"{name}_{j}")

            act.wait_ge(consts_ready, 3)
            load_table(ACT.Sqrt)
            for t in range(TT):
                act.wait_ge(x_landed[t], 16)
                rms(0, h[:, t, :], t, xhat[:, t, :])
            wait_evac(act, "prm")
            gained("n0", R_MIX)
            act.wait_ge(mem_landed, 16)
            for t in range(TT):
                rms(1, mem_rows[:, t, :], t, kv0[:, t * D:(t + 1) * D])

            def sigmoid(j):
                b = wait_filled(act, f"glu_{j}")
                if j >= 2:
                    wait_evac(act, f"glu_{j - 2}")
                nc.scalar.activation(sig[:, j % 2, :], b[:, T:2 * T], ACT.Sigmoid,
                                     bias=conv_of[:, j, R_BG:R_BG + 1]).then_inc(sig_ready, 1)

            sigmoid(0)
            for j in (1, 3):
                b = wait_filled(act, f"mem_{j}")
                for q in range(2):
                    k = 2 * j + q
                    for l in range(2):
                        ins = nc.scalar.activation(memT[l][:, k, :], b[:, q * NMEM:(q + 1) * NMEM], ACT.Copy,
                                                   scale=gain_of[:, k, R_MEM + l:R_MEM + l + 1])
                evac(ins, f"mem_{j}")
            for j in range(1, KD):
                sigmoid(j)

            def keys(l, j):
                b = wait_filled(act, f"xk{l}_{j}")
                evac(copy(xkT[l][:, 2 * j:2 * j + 2, :], b[:, :].rearrange("p (a b) -> p a b", a=2)), f"xk{l}_{j}")

            def values(l, f, t):
                b = wait_filled(act, f"xv{l}_{f}_{t}")
                evac(copy(xv[l][:, t, f * HALF:(f + 1) * HALF], b[:, :]), f"xv{l}_{f}_{t}")

            for j in range(4):
                keys(0, j)
            for f in range(NH):
                for t in range(TT):
                    values(0, f, t)
            for q in range(2):
                if q == 0:
                    act.wait_ge(centred, 1)
                else:
                    wait_evac(act, "mu")
                nc.scalar.activation(conv_sq[:, 4 * q:4 * q + 4, :], conv[:, 4 * q:4 * q + 4, :],
                                     ACT.Square).then_inc(squared, 1)
            keys(1, 2)
            b = wait_filled(act, "var")
            evac(nc.scalar.activation(ln_rstd, b[:, 0:T], ACT.Sqrt, bias=stat[:, 63:64]), "var")
            for j in range(KD):
                act.wait_ge(ln_scaled, j // 4 + 1)
                nc.scalar.activation(hT[:, j, :], conv[:, j, :], ACT.Silu, bias=conv_of[:, j, R_LNB:R_LNB + 1],
                                     scale=conv_of[:, j, R_LNG:R_LNG + 1]).then_inc(swished, 1)
            keys(1, 3)

            def cross(l):
                i = 2 if l == 0 else 5
                prev = "cout" if l == 0 else "mw"
                for t in range(TT):
                    wait_evac(act, f"{prev}_{NH - 1}_{t}")
                    rms(i, h[:, t, :], t, xhat[:, t, :])
                load_table(ACT.Exp)
                if l == 0:
                    values(1, 0, 0)
                gained(f"nx{l}", R_XA + l)
                for j in (1, 3):
                    b = wait_filled(act, f"xq{l}_{j}")
                    evac(copy(xqT[:, 2 * j:2 * j + 2, :], b[:, :].rearrange("p (a b) -> p a b", a=2)), f"xq{l}_{j}")
                for hd in range(XH):
                    act.wait_ge(x_max_ready, XH * l + hd + 1)
                    b = wait_filled(act, f"xs{l}_{hd}")
                    for t in range(TT):
                        c = 32 + 2 * hd + t
                        ins = nc.scalar.activation(xprob[:, hd, t, :], b[:, t * NMEM:(t + 1) * NMEM], ACT.Exp,
                                                   bias=stat[:, c:c + 1], scale=XSCALE,
                                                   accum_out=stat[:, c + 8:c + 9])
                    evac(ins, f"xs{l}_{hd}")
                if l == 0:
                    values(1, 0, 1)
                for hd in range(XH):
                    b = wait_filled(act, f"xp{l}_{hd}")
                    evac(copy(xprobT[:, hd % 2, :], b[:, :]), f"xp{l}_{hd}")

            def route(l):
                i = 3 if l == 0 else 6
                for t in range(TT):
                    wait_evac(act, f"xw{l}_{NH - 1}_{t}")
                    rms(i, h[:, t, :], t, xhat[:, t, :])
                if l == 0:
                    values(1, 1, 0)
                gained(f"nf{l}", R_FFN + l)
                act.wait_ge(route_diff, 2 * l + 1)
                nc.scalar.activation(rt[:, 8:16], rt[:, 0:8], ACT.Exp).then_inc(route_exp, 1)
                act.wait_ge(route_diff, 2 * l + 2)
                nc.scalar.activation(rt[:, 18:20], rt[:, 16:18], ACT.Exp).then_inc(route_exp, 1)
                if l == 0:
                    values(1, 1, 1)

            def run_part(pl):
                l = pl.s.l

                def gathered(q):
                    b = filled_at(act, pl, f"ga{q}_1")
                    for k in range(KD // 2, KD):
                        c = (k % (KD // 2)) * P
                        ins = nc.scalar.activation(xg[:, k, q * QUAD:(q + 1) * QUAD, :],
                                                   b[:, c:c + P].rearrange("p (e c) -> p e c", e=QUAD), ACT.Copy,
                                                   scale=gain_of[:, k, R_FFN + l:R_FFN + l + 1])
                    copied_at(ins, pl, f"ga{q}_1")

                def gate(q):
                    b = filled_at(act, pl, f"gu{q}")
                    nc.scalar.activation(gated[:, q, :], b[:, 0:FF], ACT.Silu).then_inc(pl.s.gate_ready, 1)

                def puts():
                    b = filled_at(act, pl, "st")
                    copied_at(copy(put.rearrange("p q t s -> p (q t s)"), b[:, :]), pl, "st")

                def mid(q):
                    b = filled_at(act, pl, f"ht{q}")
                    copied_at(copy(hmidT.rearrange("p a b -> p (a b)"), b[:, 0:FF]), pl, f"ht{q}")

                def y(q):
                    b = filled_at(act, pl, f"yd{q}_1")
                    copied_at(copy(yslot[:, q, HALF:], b[:, :]), pl, f"yd{q}_1")

                if pl.part != "prologue":
                    puts()
                    gate(1)
                    mid(0)
                    y(0)
                if pl.part != "epilogue":
                    gathered(0)
                if pl.part != "prologue":
                    mid(1)
                    y(1)
                if pl.part != "epilogue":
                    gate(0)
                    gathered(1)
                if pl.part == "prologue" and pl.repeat is None and pl.s.late:
                    for j in range(LATE_KEYS):
                        act.wait_ge(late_filled, j + 1)
                        copy(xkT[1][:, 2 * j:2 * j + 2, :], banks[LATE_BANK + j][:, :].rearrange("p (a b) -> p a b", a=2)).then_inc(late_kept, 1)

            def sweep(s, repeat=None):
                run_part(Place(s, "prologue", repeat=repeat))
                with act.Fori(0, TURNS - 1) as turn:
                    run_part(Place(s, "turn", turn, repeat))
                run_part(Place(s, "epilogue", repeat=repeat))

            def moe(l):
                a, b = sweeps[l]
                sweep(a)
                act.wait_ge(routed, l + 1)
                n = act.value_load(most[0:1, l:l + 1], min_val=0, max_val=T)
                with act.If(n > SLOTS):
                    act.wait_ge(act_freed, Place(a, "epilogue").freed("yd1_1")[0])
                    act.sem_inc(b.sem["act"], b.base["act"])
                    with act.Fori(0, REPEATS) as repeat:
                        sweep(b, repeat)
                    act.wait_ge(b.sem["dve"], b.base["dve"] + REPEATS * in_a_sweep["dve"])
                load_table(ACT.Sqrt)

            cross(0)
            route(0)
            moe(0)

            for t in range(TT):
                act.wait_ge(dve_freed, Place(sweeps[0][0], "epilogue").freed(f"sc1_{NH - 1}_{t}")[0])
                rms(4, h[:, t, :], t, xhat[:, t, :])
            gained("n4", R_MIX + 1)
            for t in range(TT):
                b = wait_filled(act, f"dnA_{t}")
                evac(copy(down[:, t, 0:HALF], b[:, :]), f"dnA_{t}")
                b = wait_filled(act, f"dnB_{t}")
                evac(copy(down[:, t, HALF:DOWN], b[:, 0:DOWN - HALF]), f"dnB_{t}")
                wait_evac(act, f"dnB_{t}")
                for q, (c0, c1) in enumerate(((0, QR), (QR, QR + KVR))):
                    root_mean_square(down[:, t, c0:c1], stat[:, 52 + 2 * t + q:53 + 2 * t + q], c1 - c0,
                                     squares_junk[:, 2 * t + q, 0:c1 - c0]).then_inc(down_rms_ready, 1)
            b = wait_filled(act, "cT_1")
            nc.scalar.activation(cT[:, 2, :], b[:, 0:T], ACT.Copy, scale=conv_of[:, 2, R_QN:R_QN + 1])
            evac(nc.scalar.activation(cT[:, 3, :], b[:, T:2 * T], ACT.Copy, scale=conv_of[:, 0, R_KVN:R_KVN + 1]), "cT_1")
            act.wait_ge(angles_ready, 1)
            for q in range(2):
                nc.scalar.activation(rope_t[:, 4 + q, :, :], rope_t[:, 2 + q, :, :], ACT.Sin).then_inc(sincos_ready, 1)
            load_table(ACT.Exp)
            for t in range(TT):
                for n in range(3):
                    b = wait_filled(act, f"uq_{n}_{t}")
                    evac(copy(qtok[:, t, n * HALF:(n + 1) * HALF], b[:, :]), f"uq_{n}_{t}")

            def heads(name, dst):
                for j in range(1, H // 2, 2):
                    b = wait_filled(act, f"{name}_{j}")
                    evac(copy(dst[0:QKD, 2 * j:2 * j + 2, :], b[0:QKD, :].rearrange("p (a b) -> p a b", a=2)), f"{name}_{j}")

            act.wait_ge(ktok_ready, TT)
            for n in range(4):
                b = wait_filled(act, f"ukv_{n}_1")
                src = b[:, :].rearrange("p (h c) -> p h c", h=4)
                copy(ktok[1].rearrange("p (h c) -> p h c", h=H)[:, 4 * n:4 * n + 4, 0:NOPE], src[:, :, 0:NOPE])
                evac(copy(vtok[:, 1, 4 * n * VD:4 * (n + 1) * VD].rearrange("p (h c) -> p h c", h=4), src[:, :, NOPE:]), f"ukv_{n}_1")
            heads("qT", qhT)
            heads("kT", khT)
            SPANS = [(0, P), (P, 3 * P)]

            def m_exp(hd):
                act.wait_ge(m_max_ready, hd + 1)
                if hd >= DEPTH:
                    wait_filled(act, f"mp_{hd - DEPTH}")
                for t in range(TT):
                    c = 32 + 4 * (hd % DEPTH) + t
                    a0, a1 = SPANS[t]
                    ins = nc.scalar.activation(prob[:, hd % DEPTH, a0:a1], score[:, hd % DEPTH, a0:a1], ACT.Exp,
                                               bias=stat[:, c:c + 1], scale=MSCALE, accum_out=stat[:, c + 2:c + 3])
                ins.then_inc(m_exp_ready, 1)

            m_exp(0)
            m_exp(1)
            for hd in range(H):
                if hd + 2 < H:
                    m_exp(hd + 2)
                b = wait_filled(act, f"mp_{hd}")
                if hd >= 2:
                    wait_filled(act, f"mo_{hd // 2 - 1}")
                evac(copy(probT[:, hd % 2, :], b[:, 0:3 * P]), f"mp_{hd}")
                if hd % 2:
                    b = wait_filled(act, f"mo_{hd // 2}")
                    evac(copy(hT[:, hd // 2, :], b[:, 0:T]), f"mo_{hd // 2}")
            act.dma_start(bcast_row[:, :], A["final_norm"].rearrange("(a n) -> a n", a=1).partition_broadcast(P)).then_inc(row_landed, 16)
            cross(1)
            route(1)
            moe(1)
            for t in range(TT):
                act.wait_ge(dve_freed, Place(sweeps[1][0], "epilogue").freed(f"sc1_{NH - 1}_{t}")[0])
                rms(7, h[:, t, :], t, xhat[:, t, :])

        @block.vector
        def _(dve):
            v = nc.vector
            n_steps = 0

            def mark(ins):
                nonlocal n_steps
                n_steps += 1
                ins.then_inc(dve_step, 1)
                return n_steps

            def step(ins):
                dve.wait_ge(dve_step, mark(ins))

            def norm(i, src, dst):
                for t in range(TT):
                    c = stat[:, 2 * i + t + 1:2 * i + t + 2]
                    dve.wait_ge(rms_ready, 2 * i + t + 1)
                    step(v.reciprocal(c, c))
                    v.tensor_scalar(dst[:, t, :], src[:, t, :], c, None, ALU.mult).then_inc(normed, 1)

            def gained(name, row):
                for j in (0, 2):
                    b = wait_filled(dve, f"{name}_{j}")
                    for q in range(2):
                        k = 2 * j + q
                        ins = v.tensor_scalar(hT[:, k, :], b[:, q * T:(q + 1) * T], gain_of[:, k, row:row + 1], None, ALU.mult)
                    evac(ins, f"{name}_{j}")

            def add_residual(name):
                for f in range(NH):
                    for t in range(TT):
                        b = wait_filled(dve, f"{name}_{f}_{t}")
                        s = h[:, t, f * HALF:(f + 1) * HALF]
                        evac(v.tensor_tensor(s, s, b[:, :], ALU.add), f"{name}_{f}_{t}")

            norm(0, h, xhat)
            b = wait_filled(dve, "prm")
            evac(v.tensor_copy(prmT[:, :], b[:, 0:KD * (NA_ROWS + NB_ROWS)]), "prm")
            wait_evac(dve, "prm")
            gained("n0", R_MIX)
            norm(1, mem_rows, mem_rows)

            dve.wait_ge(consts_ready, 4)
            done_tap = {}
            for m in range(KD // 2):
                for j in (2 * m, 2 * m + 1):
                    b = wait_filled(dve, f"glu_{j}")
                    dve.wait_ge(sig_ready, j + 1)
                    evac(v.scalar_tensor_tensor(out=u_pad[:, j, W - 1:], in0=b[:, 0:T], scalar=conv_of[:, j, R_BA:R_BA + 1],
                                                in1=sig[:, j % 2, :], op0=ALU.add, op1=ALU.mult), f"glu_{j}")
                    if j == 0:
                        for i in (0, 2):
                            b = wait_filled(dve, f"mem_{i}")
                            for q in range(2):
                                k = 2 * i + q
                                for l in range(2):
                                    ins = v.tensor_scalar(memT[l][:, k, :], b[:, q * NMEM:(q + 1) * NMEM],
                                                          gain_of[:, k, R_MEM + l:R_MEM + l + 1], None, ALU.mult)
                            evac(ins, f"mem_{i}")
                for tap in range(W):
                    for j in (x for x in (2 * m, 2 * m + 1) if x != POOLED):
                        taps = u_pad[:, j, tap:tap + T]
                        w = conv_of[:, j, tap:tap + 1]
                        if tap == 0:
                            wait_evac(dve, f"glu_{j}")
                            ins = v.tensor_scalar(conv[:, j, :], taps, w, conv_of[:, j, R_BDW:R_BDW + 1], ALU.mult, ALU.add)
                        else:
                            dve.wait_ge(dve_step, done_tap[j])
                            ins = v.scalar_tensor_tensor(out=conv[:, j, :], in0=taps, scalar=w, in1=conv[:, j, :],
                                                         op0=ALU.mult, op1=ALU.add)
                        if tap < W - 1:
                            done_tap[j] = mark(ins)
                        else:
                            ins.then_inc(conv_ready, 1)

            dve.wait_ge(conv_ready, KD - 1)
            dve.wait_ge(pooled_ready, 1)
            v.tensor_reduce(out=ln_sum, in_=conv.rearrange("p k t -> p t k"), axis=AX.X, op=ALU.add).then_inc(summed, 1)
            b = wait_filled(dve, "mu")
            for q in range(2):
                s = conv[:, 4 * q:4 * q + 4, :]
                ins = v.tensor_tensor(s, s, b[:, 0:T].unsqueeze(1).to_broadcast([P, 4, T]), ALU.subtract)
                if q == 0:
                    ins.then_inc(centred, 1)
            evac(ins, "mu")
            dve.wait_ge(squared, 2)
            v.tensor_reduce(out=ln_sum, in_=conv_sq.rearrange("p k t -> p t k"), axis=AX.X, op=ALU.add).then_inc(summed, 1)
            wait_evac(dve, "var")
            step(v.reciprocal(ln_rstd, ln_rstd))
            for q in range(2):
                s = conv[:, 4 * q:4 * q + 4, :]
                v.tensor_tensor(s, s, ln_rstd.unsqueeze(1).to_broadcast([P, 4, T]), ALU.mult).then_inc(ln_scaled, 1)
            dve.wait_ge(pos_landed, 16)
            dve.wait_ge(consts_ready, 4)
            ang, full, r, rc = (rope_t[:, q, :, :] for q in range(4))
            posf = stat[:, 50:50 + TT]
            step(v.tensor_copy(posf, pos_i[:, :]))
            step(v.tensor_tensor(full, ang, posf.unsqueeze(2).to_broadcast([P, TT, ROPE // 2]), ALU.mult))
            step(v.tensor_scalar(ang, full, float(1.0 / (2 * np.pi)), None, ALU.mult))
            step(v.tensor_copy(rope_i[:, :, :], ang))
            step(v.tensor_copy(ang, rope_i[:, :, :]))
            c1 = 6.28125
            c2 = float(np.float32(np.float64(2 * np.pi) - c1))
            c3 = float(np.float64(2 * np.pi) - c1 - np.float64(np.float32(c2)))
            src = full
            for c in (c1, c2, c3):
                step(v.scalar_tensor_tensor(out=r, in0=ang, scalar=-c, in1=src, op0=ALU.mult, op1=ALU.add))
                src = r

            def wrap(x):
                for cmp, lim, add in ((ALU.is_gt, float(np.pi), -2 * np.pi), (ALU.is_lt, -float(np.pi), 2 * np.pi)):
                    step(v.tensor_scalar(ang, x, lim, float(add), cmp, ALU.mult))
                    step(v.tensor_tensor(x, x, ang, ALU.add))
                return v.tensor_scalar(x, x, 3.1415925, -3.1415925, ALU.min, ALU.max)

            step(wrap(r))
            step(v.tensor_scalar(rc, r, float(np.pi / 2), None, ALU.add))
            wrap(rc).then_inc(angles_ready, 1)
            sin_t, cos_t = rope_t[:, 4, :, :], rope_t[:, 5, :, :]

            dve.wait_ge(bias_added, TT)
            add_residual("cout")

            def cross(l):
                i = 2 if l == 0 else 5
                norm(i, h, xhat)
                gained(f"nx{l}", R_XA + l)
                for j in (0, 2):
                    b = wait_filled(dve, f"xq{l}_{j}")
                    evac(v.tensor_copy(xqT[:, 2 * j:2 * j + 2, :], b[:, :].rearrange("p (a b) -> p a b", a=2)), f"xq{l}_{j}")
                for hd in range(XH):
                    b = wait_filled(dve, f"xs{l}_{hd}")
                    mx = stat[:, 32 + 2 * hd:34 + 2 * hd]
                    step(v.tensor_reduce(out=mx, in_=b[:, :].rearrange("p (t m) -> p t m", t=TT), axis=AX.X, op=ALU.max))
                    v.tensor_scalar(mx, mx, -XSCALE, None, ALU.mult).then_inc(x_max_ready, 1)
                for hd in range(XH):
                    wait_evac(dve, f"xs{l}_{hd}")
                    su = stat[:, 40 + 2 * hd:42 + 2 * hd]
                    step(v.reciprocal(su, su))
                    v.tensor_tensor(xprob[:, hd, :, :], xprob[:, hd, :, :],
                                    su.unsqueeze(2).to_broadcast([P, TT, NMEM]), ALU.mult).then_inc(x_prob_ready, 1)
                for hd in range(XH):
                    b = wait_filled(dve, f"xo{l}_{hd}")
                    evac(v.tensor_copy(hT[:, 2 * hd:2 * hd + 2, :], b[:, :].rearrange("p (a b) -> p a b", a=2)), f"xo{l}_{hd}")
                add_residual(f"xw{l}")

            gdiff, gexp = view(rt, 0, TT, G), view(rt, 8, TT, G)
            ediff, eexp = rt[:, 16:18], rt[:, 18:20]
            gmax, gsum, m1, m2, best, w1, w2 = (rt[:, 20 + 2 * q:22 + 2 * q] for q in range(7))
            logit = view(rt, 40, TT, G + E)
            group = view(rt, 112, TT, G)
            eq = view(rt, 120, TT, EG)
            mine = view(rt, 136, TT, EG)
            first, second, within, chosen = (view(rt, 152 + 16 * q, TT, EG) for q in range(4))
            masked = view(rt, 216, TT, G, EG)
            taken = view(rt, 280, TT, G, EG)
            weight = view(rt, 344, TT, G, EG)
            slot = view(rt, 408, TT, E)

            def over(x, n):
                return x.unsqueeze(2).to_broadcast([P, TT, n])

            def first_of(x, top, n, onehot):
                step(v.tensor_reduce(out=top, in_=x, axis=AX.X, op=ALU.max))
                e = eq[:, :, 0:n]
                step(v.tensor_tensor(e, x, over(top, n), ALU.is_equal))
                step(v.tensor_tensor(e, e, desc[:, EG - n:EG].unsqueeze(1).to_broadcast([P, TT, n]), ALU.mult))
                step(v.tensor_reduce(out=best, in_=e, axis=AX.X, op=ALU.max))
                step(v.tensor_tensor(onehot, e, over(best, n), ALU.is_equal))

            def route(l):
                i = 3 if l == 0 else 6
                norm(i, h, xhat)
                gained(f"nf{l}", R_FFN + l)
                b = wait_filled(dve, f"lg{l}")
                evac(v.tensor_tensor(logit, b[:, 0:TT * (G + E)].rearrange("p (t n) -> p t n", t=TT),
                                     router_b[:, l:l + 1, :].to_broadcast([P, TT, G + E]), ALU.add), f"lg{l}")
                wait_evac(dve, f"lg{l}")
                first_of(logit[:, :, 0:G], gmax, G, group)
                v.tensor_tensor(gdiff, logit[:, :, 0:G], over(gmax, G), ALU.subtract).then_inc(route_diff, 1)
                step(v.tensor_tensor(masked, logit[:, :, G:].rearrange("p t (g e) -> p t g e", g=G),
                                     group.unsqueeze(3).to_broadcast([P, TT, G, EG]), ALU.mult))
                step(v.tensor_reduce(out=mine, in_=masked.rearrange("p t g e -> p t e g"), axis=AX.X, op=ALU.add))
                first_of(mine, m1, EG, first)
                step(v.scalar_tensor_tensor(out=mine, in0=first, scalar=NEG, in1=mine, op0=ALU.mult, op1=ALU.add))
                first_of(mine, m2, EG, second)
                v.tensor_tensor(ediff, m2, m1, ALU.subtract).then_inc(route_diff, 1)
                step(v.tensor_tensor(chosen, first, second, ALU.add))
                v.tensor_tensor(taken, group.unsqueeze(3).to_broadcast([P, TT, G, EG]),
                                chosen.unsqueeze(2).to_broadcast([P, TT, G, EG]), ALU.mult).then_inc(assigned, 1)
                dve.wait_ge(assigned, l + 1)
                b = wait_filled(dve, f"rk{l}")
                flat = taken.rearrange("p t g e -> p t (g e)")
                step(v.scalar_tensor_tensor(out=slot, in0=b[:, 0:TT * E].rearrange("p (t n) -> p t n", t=TT), scalar=1.0,
                                            in1=flat, op0=ALU.add, op1=ALU.mult))
                step(v.tensor_scalar(slot, slot, -1.0, None, ALU.add))
                step(v.tensor_reduce(out=rt[:, 38:39], in_=b[:, TT * E:(TT + 1) * E], axis=AX.X, op=ALU.max))
                mark(v.tensor_copy(most[:, l:l + 1], rt[:, 38:39]))
                dve.wait_ge(dve_step, n_steps)
                evac(v.tensor_copy(rt[:, 39:40], rt[:, 38:39]), f"rk{l}")
                wait_evac(dve, f"rk{l}")
                v.tensor_copy(rt[:, 39:40], rt[:, 38:39]).then_inc(routed, 1)

            def weigh(l):
                dve.wait_ge(route_exp, 2 * l + 1)
                step(v.tensor_reduce(out=gsum, in_=gexp, axis=AX.X, op=ALU.add))
                dve.wait_ge(route_exp, 2 * l + 2)
                step(v.tensor_scalar(w1, eexp, 1.0, None, ALU.add))
                step(v.tensor_tensor(w1, w1, gsum, ALU.mult))
                step(v.reciprocal(w1, w1))
                step(v.tensor_tensor(w2, w1, eexp, ALU.mult))
                step(v.tensor_tensor(first, first, over(w1, EG), ALU.mult))
                step(v.tensor_tensor(second, second, over(w2, EG), ALU.mult))
                step(v.tensor_tensor(within, first, second, ALU.add))
                step(v.tensor_tensor(weight, group.unsqueeze(3).to_broadcast([P, TT, G, EG]),
                                     within.unsqueeze(2).to_broadcast([P, TT, G, EG]), ALU.mult))


            def run_part(pl):
                l, s = pl.s.l, pl.s
                wflat = weight.rearrange("p t g e -> p t (g e)")
                group = 0 if pl.part == "prologue" else None if pl.part == "epilogue" else pl.turn + 1

                def pick_tokens():
                    for t in range(TT):
                        p3 = pick[:, t, :].rearrange("p (e s) -> p e s", e=EG)
                        v.tensor_tensor(p3, slot_no[:, :].unsqueeze(1).to_broadcast([P, EG, SLOTS]),
                                        slot[:, t, bass.ds(group * EG, EG)].unsqueeze(2).to_broadcast([P, EG, SLOTS]),
                                        ALU.is_equal).then_inc(s.picked, 1)

                def gathered(q):
                    b = filled_at(dve, pl, f"ga{q}_0")
                    for k in range(KD // 2):
                        ins = v.tensor_scalar(xg[:, k, q * QUAD:(q + 1) * QUAD, :],
                                              b[:, k * P:(k + 1) * P].rearrange("p (e c) -> p e c", e=QUAD),
                                              gain_of[:, k, R_FFN + l:R_FFN + l + 1], None, ALU.mult)
                    copied_at(ins, pl, f"ga{q}_0")

                def weight_picked():
                    filled_at(dve, pl, "ga1_1")
                    for t in range(TT):
                        p3 = pick[:, t, :].rearrange("p (e s) -> p e s", e=EG)
                        v.tensor_tensor(p3, p3, wflat[:, t, bass.ds(group * EG, EG)].unsqueeze(2).to_broadcast([P, EG, SLOTS]),
                                        ALU.mult).then_inc(s.weighted, 1)

                def mid(q):
                    b = filled_at(dve, pl, f"gu{q}")
                    k = 1 if q or pl.part == "prologue" else QUADS
                    dve.wait_ge(s.gate_ready, pl.value(pl.nth(k, (1, QUADS, QUADS - 1))))
                    copied_at(v.tensor_tensor(hmid[:, q, :], gated[:, q, :], b[:, FF:2 * FF], ALU.mult), pl, f"gu{q}")

                def y(q):
                    b = filled_at(dve, pl, f"yd{q}_0")
                    copied_at(v.tensor_copy(yslot[:, q, 0:HALF], b[:, :]), pl, f"yd{q}_0")

                def scatter(q):
                    for f in range(NH):
                        for t in range(TT):
                            name = f"sc{q}_{f}_{t}"
                            b = filled_at(dve, pl, name)
                            c = h[:, t, f * HALF:(f + 1) * HALF]
                            const, a_turn, a_repeat = pl.freed(name)
                            dve.wait_ge(s.sem["dve"], pl.value((const - 1, a_turn, a_repeat)))
                            copied_at(v.tensor_tensor(c, c, b[:, :], ALU.add), pl, name)

                if pl.part == "prologue":
                    pick_tokens()
                    gathered(0)
                    if pl.repeat is None:
                        weigh(l)
                    mid(0)
                    gathered(1)
                    weight_picked()
                    return
                if pl.part == "turn":
                    filled_at(dve, pl, "st")
                    pick_tokens()
                mid(1)
                y(0)
                scatter(0)
                if pl.part == "turn":
                    gathered(0)
                y(1)
                if pl.part == "turn":
                    mid(0)
                    gathered(1)
                    weight_picked()
                scatter(1)

            def sweep(s, repeat=None):
                if repeat is not None:
                    v.tensor_scalar(slot, slot, -float(SLOTS), None, ALU.add).then_inc(s.shifted, 1)
                    dve.wait_ge(s.shifted, repeat + 1)
                run_part(Place(s, "prologue", repeat=repeat))
                with dve.Fori(0, TURNS - 1) as turn:
                    run_part(Place(s, "turn", turn, repeat))
                run_part(Place(s, "epilogue", repeat=repeat))

            def moe(l):
                a, b = sweeps[l]
                dve.wait_ge(routed, l + 1)
                sweep(a)
                n = dve.value_load(most[0:1, l:l + 1], min_val=0, max_val=T)
                with dve.If(n > SLOTS):
                    dve.wait_ge(dve_freed, Place(a, "epilogue").freed(f"sc1_{NH - 1}_{TT - 1}")[0])
                    dve.sem_inc(b.sem["dve"], b.base["dve"])
                    with dve.Fori(0, REPEATS) as repeat:
                        sweep(b, repeat)
                    dve.wait_ge(b.sem["dve"], b.base["dve"] + REPEATS * in_a_sweep["dve"])

            cross(0)
            route(0)
            moe(0)

            norm(4, h, xhat)
            gained("n4", R_MIX + 1)
            for t in range(TT):
                dve.wait_ge(down_rms_ready, 2 * (t + 1))
                c = stat[:, 52 + 2 * t:54 + 2 * t]
                step(v.reciprocal(c, c))
                for q, (c0, c1) in enumerate(((0, QR), (QR, QR + KVR))):
                    part = down[:, t, c0:c1]
                    ins = v.tensor_scalar(part, part, c[:, q:q + 1], None, ALU.mult)
                ins.then_inc(down_ready, 1)
            kr = down[:, :, QR + KVR:DOWN]
            HR = ROPE // 2

            def rotate(x1, x2, cs, sn, tmp):
                a, b_, c_, d_ = tmp
                v.tensor_tensor(a, x1, cs, ALU.mult)
                v.tensor_tensor(b_, x2, sn, ALU.mult)
                v.tensor_tensor(c_, x2, cs, ALU.mult)
                step(v.tensor_tensor(d_, x1, sn, ALU.mult))
                v.tensor_tensor(x1, a, b_, ALU.subtract)
                return v.tensor_tensor(x2, c_, d_, ALU.add)

            for j in (0, 2):
                b = wait_filled(dve, f"cT_{j}")
                chunk, row = (0, R_QN) if j == 0 else (1, R_KVN)
                ins = v.tensor_scalar(cT[:, 2 * j, :], b[:, 0:T], conv_of[:, chunk, row:row + 1], None, ALU.mult)
                if j == 0:
                    ins = v.tensor_scalar(cT[:, 1, :], b[:, T:2 * T], conv_of[:, 1, R_QN:R_QN + 1], None, ALU.mult)
                evac(ins, f"cT_{j}")
            dve.wait_ge(sincos_ready, 2)
            step(rotate(kr[:, :, 0:HR], kr[:, :, HR:ROPE], cos_t, sin_t, [rope_tmp[:, q, :, 0, :] for q in range(4)]))
            kh = [ktok[t].rearrange("p (h c) -> p h c", h=H) for t in range(TT)]
            wait_filled(dve, "cT_2")
            step(v.tensor_copy(shared_key, kr))
            for t in range(TT):
                v.tensor_copy(kh[t][:, :, NOPE:QKD], shared_key[:, t:t + 1, :].to_broadcast([P, H, ROPE])).then_inc(ktok_ready, 1)
            qh = qtok.rearrange("p t (h c) -> p t h c", h=H)
            for t in range(TT):
                cs = cos_t[:, t, :].unsqueeze(1).to_broadcast([P, H, HR])
                sn = sin_t[:, t, :].unsqueeze(1).to_broadcast([P, H, HR])
                wait_evac(dve, f"uq_2_{t}")
                rotate(qh[:, t, :, NOPE:NOPE + HR], qh[:, t, :, NOPE + HR:QKD], cs, sn,
                       [rope_tmp[:, q, t, :, :] for q in range(4)]).then_inc(roped, 1)

            def heads(name, dst):
                for j in range(0, H // 2, 2):
                    b = wait_filled(dve, f"{name}_{j}")
                    evac(v.tensor_copy(dst[0:QKD, 2 * j:2 * j + 2, :], b[0:QKD, :].rearrange("p (a b) -> p a b", a=2)), f"{name}_{j}")

            for n in range(4):
                b = wait_filled(dve, f"ukv_{n}_0")
                src = b[:, :].rearrange("p (h c) -> p h c", h=4)
                v.tensor_copy(kh[0][:, 4 * n:4 * n + 4, 0:NOPE], src[:, :, 0:NOPE])
                evac(v.tensor_copy(vtok[:, 0, 4 * n * VD:4 * (n + 1) * VD].rearrange("p (h c) -> p h c", h=4), src[:, :, NOPE:]), f"ukv_{n}_0")
            heads("qT", qhT)
            heads("kT", khT)

            def m_max(hd):
                b = wait_filled(dve, f"ms_{hd}")
                sc = score[:, hd % DEPTH, :]
                if hd >= DEPTH:
                    dve.wait_ge(m_exp_ready, hd - DEPTH + 1)
                evac(v.tensor_tensor(sc, b[:, 0:3 * P], causal[:, :], ALU.add), f"ms_{hd}")
                wait_evac(dve, f"ms_{hd}")
                c = 32 + 4 * (hd % DEPTH)
                v.tensor_reduce(out=stat[:, c:c + 1], in_=sc[:, 0:P], axis=AX.X, op=ALU.max)
                step(v.tensor_reduce(out=stat[:, c + 1:c + 2], in_=sc[:, P:3 * P], axis=AX.X, op=ALU.max))
                v.tensor_scalar(stat[:, c:c + 2], stat[:, c:c + 2], -MSCALE, None, ALU.mult).then_inc(m_max_ready, 1)

            for hd in range(AHEAD - 1):
                m_max(hd)
            for hd in range(H):
                dve.wait_ge(m_exp_ready, hd + 1)
                c = 34 + 4 * (hd % DEPTH)
                v.reciprocal(stat[:, c:c + 2], stat[:, c:c + 2]).then_inc(m_sum_ready, 1)
                if hd + AHEAD - 1 < H:
                    m_max(hd + AHEAD - 1)
            add_residual("mw")
            cross(1)
            route(1)
            moe(1)
            dve.wait_ge(row_landed, 32)
            for t in range(TT):
                i = 7
                c = stat[:, 2 * i + t + 1:2 * i + t + 2]
                dve.wait_ge(rms_ready, 2 * i + t + 1)
                step(v.reciprocal(c, c))
                v.scalar_tensor_tensor(out=xhat[:, t, :], in0=h[:, t, :], scalar=c, in1=bcast_row[:, :],
                                       op0=ALU.mult, op1=ALU.mult).then_inc(normed, 1)

        @block.tensor
        def _(pe):
            mm = nc.tensor.matmul

            def fill(ins):
                ins.then_inc(bank_filled, 1)

            def turn_rows(name, rows, i, between=None):
                bs = [open_bank(pe, f"{name}_{j}") for j in range(4)]
                for t in range(TT):
                    if t and between:
                        between()
                    pe.wait_ge(normed, 2 * i + t + 1)
                    for k in range(KD):
                        o = (k % 2) * T + t * P
                        ins = nc.tensor.transpose(bs[k // 2][:, o:o + P], rows[:, t, k::KD], ident[:, :])
                        if t == TT - 1 and k % 2:
                            fill(ins)

            def channel_major(name, u0, src, parts=range(4), copied=None):
                for j in parts:
                    b = open_bank(pe, f"{name}_{j}")
                    u = u0[j] if isinstance(u0, list) else u0 + j
                    wait_unit(pe, u)
                    w = unit(u, KD, 256)
                    for q in range(2):
                        for k in range(KD):
                            if copied and j == q == 0:
                                copied(k)
                            ins = mm(b[:, q * T:(q + 1) * T], lhsT=w[:, k, q * P:(q + 1) * P], rhs=src[:, k, :],
                                     start=(k == 0), stop=(k == KD - 1))
                    fill(ins)

            def token_tile(name, u0, src, f, t, copied=None):
                b = open_bank(pe, f"{name}_{f}_{t}")
                for k in range(KD):
                    if t == 0 and k % 4 == 0:
                        wait_unit(pe, u0 + k // 4)
                    if copied and f == t == 0:
                        copied(k)
                    ins = mm(b[:, :], lhsT=src[:, k, t * P:(t + 1) * P], rhs=unit(u0 + k // 4, 4, HALF)[:, k % 4, :],
                             start=(k == 0), stop=(k == KD - 1))
                fill(ins)

            def token_major(name, u0, src, copied):
                for f in range(NH):
                    for t in range(TT):
                        token_tile(name, u0 + 2 * f, src, f, t, copied)

            def turn_parameters(b):
                pe.wait_ge(prm_landed, 16 * 11)
                for k in range(KD):
                    nc.tensor.transpose(b[:, k * NA_ROWS:(k + 1) * NA_ROWS], prm_a[:, k::KD], ident[0:NA_ROWS, 0:NA_ROWS])
                o = KD * NA_ROWS
                for k in range(KD):
                    ins = nc.tensor.transpose(b[:, o + k * NB_ROWS:o + (k + 1) * NB_ROWS], prm_b[:, k * P:(k + 1) * P],
                                              ident[0:NB_ROWS, 0:NB_ROWS])
                fill(ins)

            pe.wait_ge(consts_ready, 2)
            prm_bank = open_bank(pe, "prm")
            turn_rows("n0", xhat, 0, between=lambda: turn_parameters(prm_bank))

            for j in range(KD):
                b = open_bank(pe, f"glu_{j}")
                for part in range(2):
                    i = U_CIN + 2 * (j // 2) + part
                    if j % 2 == 0:
                        wait_unit(pe, i)
                    w = unit(i, KD, 256)
                    c = (j % 2) * P
                    for k in range(KD):
                        if j == part == 0:
                            wait_evac(pe, f"n0_{k // 2}")
                        ins = mm(b[:, part * T:(part + 1) * T], lhsT=w[:, k, c:c + P], rhs=hT[:, k, :],
                                 start=(k == 0), stop=(k == KD - 1))
                fill(ins)
                if j == 0:
                    turn_rows("mem", mem_rows, 1)

            def keys(l, j):
                channel_major(f"xk{l}", U_XK[l], memT[l], [j])

            def values(l, f, t):
                token_tile(f"xv{l}", U_XV[l][f], memT[l], f, t)

            for j in (2, 3):
                wait_evac(pe, f"mem_{j}")
            for j in range(4):
                keys(0, j)
            for f in range(NH):
                for t in range(TT):
                    values(0, f, t)
            b = open_bank(pe, "mu")
            pe.wait_ge(summed, 1)
            fill(mm(b[:, 0:T], lhsT=mean_of[:, :], rhs=ln_sum, start=True, stop=True))
            keys(1, 2)
            b = open_bank(pe, "var")
            pe.wait_ge(summed, 2)
            fill(mm(b[:, 0:T], lhsT=mean_of[:, :], rhs=ln_sum, start=True, stop=True))
            keys(1, 3)
            token_major("cout", U_COUT, hT, lambda k: pe.wait_ge(swished, k + 1))

            def cross(l):
                i = 2 if l == 0 else 5
                if l == 0:
                    values(1, 0, 0)
                turn_rows(f"nx{l}", xhat, i)
                channel_major(f"xq{l}", U_XQ[l], hT, copied=lambda k: wait_evac(pe, f"nx{l}_{k // 2}"))
                for hd in range(XH):
                    wait_evac(pe, f"xq{l}_{hd}")
                    b = open_bank(pe, f"xs{l}_{hd}")
                    for t in range(TT):
                        for c in range(2):
                            ins = mm(b[:, t * NMEM:(t + 1) * NMEM], lhsT=xqT[:, 2 * hd + c, t * P:(t + 1) * P],
                                     rhs=xkT[l][:, 2 * hd + c, :], start=(c == 0), stop=(c == 1))
                    fill(ins)

                def probs_turned(hd):
                    b = open_bank(pe, f"xp{l}_{hd}")
                    pe.wait_ge(x_prob_ready, XH * l + hd + 1)
                    for c in range(2):
                        for t in range(TT):
                            ins = nc.tensor.transpose(b[:, c * T + t * P:c * T + (t + 1) * P],
                                                      xprob[:, hd, t, c * P:(c + 1) * P], ident[:, :])
                    fill(ins)

                if l == 0:
                    values(1, 0, 1)
                probs_turned(0)
                for hd in range(XH):
                    if hd + 1 < XH:
                        probs_turned(hd + 1)
                    b = open_bank(pe, f"xo{l}_{hd}")
                    wait_evac(pe, f"xp{l}_{hd}")
                    for c in range(2):
                        for m in range(2):
                            ins = mm(b[:, c * T:(c + 1) * T], lhsT=xv[l][:, m, hd * XHD + c * P:hd * XHD + (c + 1) * P],
                                     rhs=xprobT[:, hd % 2, m * T:(m + 1) * T], start=(m == 0), stop=(m == 1))
                    fill(ins)
                token_major(f"xw{l}", U_XO[l], hT, lambda k: wait_evac(pe, f"xo{l}_{k // 2}"))

            def route(l):
                i = 3 if l == 0 else 6
                if l == 0:
                    values(1, 1, 0)
                turn_rows(f"nf{l}", xhat, i)
                pe.wait_ge(small_landed, 16 * 8)
                b = open_bank(pe, f"lg{l}")
                n = G + E
                for t in range(TT):
                    for k in range(KD):
                        if t == 0:
                            wait_evac(pe, f"nf{l}_{k // 2}")
                        ins = mm(b[:, t * n:(t + 1) * n], lhsT=hT[:, k, t * P:(t + 1) * P], rhs=router[:, l, k, :],
                                 start=(k == 0), stop=(k == KD - 1))
                fill(ins)
                if l == 0:
                    values(1, 1, 1)
                pe.wait_ge(assigned, l + 1)
                taken = [rt[:, 280 + t * E:280 + (t + 1) * E] for t in range(TT)]
                b = open_bank(pe, f"rk{l}")
                mm(b[:, 0:E], lhsT=before[:, :], rhs=taken[0], start=True, stop=True)
                mm(b[:, E:2 * E], lhsT=ones[:, :], rhs=taken[0], start=True, stop=False)
                mm(b[:, E:2 * E], lhsT=before[:, :], rhs=taken[1], start=False, stop=True)
                mm(b[:, 2 * E:3 * E], lhsT=ones[:, :], rhs=taken[0], start=True, stop=False)
                ins = mm(b[:, 2 * E:3 * E], lhsT=ones[:, :], rhs=taken[1], start=False, stop=True)
                fill(ins)

            def run_part(pl):
                s = pl.s
                behind = len(FIRST_UNITS) + s.late
                at = {"prologue": 0, "turn": behind, "epilogue": behind + (TURNS - 1) * GU}[pl.part]

                def filled(ins):
                    ins.then_inc(s.sem["filled"], 1)

                def landed(what):
                    u = (FIRST_UNITS if pl.part == "prologue" else TURN_UNITS).index(what)
                    i = s.unit0 + at + u
                    slot = i % RING
                    a_turn = 16 * GU // RING if pl.part == "turn" else 0
                    a_repeat = 0 if pl.repeat is None else 16 * 3 * E // RING
                    pe.wait_ge(s.landed[slot], pl.value((16 * (i // RING + 1 - s.first_use[slot]), a_turn, a_repeat)))
                    return slot

                def gather(q):
                    if q == 0:
                        pe.wait_ge(s.picked, pl.value(pl.nth(TT, (TT, TT, 0))))
                    for half in range(2):
                        b, = ready_at(pe, pl, [f"ga{q}_{half}"])
                        for k in range(KD // 2):
                            for t in range(TT):
                                ins = mm(b[:, k * P:(k + 1) * P], lhsT=xhat[:, t, half * KD // 2 + k::KD],
                                         rhs=pick[:, t, q * P:(q + 1) * P], start=(t == 0), stop=(t == TT - 1))
                        filled(ins)

                def gate_up(q):
                    b, = ready_at(pe, pl, [f"gu{q}"])
                    if q:
                        for o in ("ga_dve", "ga_act"):
                            pe.wait_ge(s.sem[o], pl.value(pl.nth(0, s.parts_of[o], s.base[o])))
                            pe.nop()
                    for half in range(2):
                        if q == 0:
                            ready_at(pe, pl, [], [f"ga0_{half}"])
                        w = []
                        for pair in range(QUAD // 2):
                            slot = landed(("gate", q, pair, half))
                            landed(("up", q, pair, half))
                            w.append(ring[:, slot * UNIT:(slot + 2) * UNIT].rearrange("p (g e k n) -> p g e k n", g=2, e=2, k=KD // 2))
                        for k in range(KD // 2):
                            for e in range(QUAD):
                                ins = mm(b[e * SLOTS:(e + 1) * SLOTS, :].rearrange("p (g n) -> p g n", g=2),
                                         lhsT=xg[:, half * KD // 2 + k, q * QUAD + e, :], rhs=w[e // 2][:, :, e % 2, k, :],
                                         start=(half == k == 0), stop=(half == 1 and k == KD // 2 - 1), skip_group_check=True)
                        if half == 0:
                            ins.then_inc(s.half_used, 1)
                    filled(ins)

                def puts():
                    b, = ready_at(pe, pl, ["st"])
                    pe.wait_ge(s.weighted, pl.value(pl.nth(0, (TT, TT, 0))))
                    for q in range(QUADS):
                        for t in range(TT):
                            o = (q * TT + t) * P
                            ins = nc.tensor.transpose(b[:, o:o + P], pick[:, t, q * P:(q + 1) * P], ident[:, :])
                    filled(ins)

                def mid(q):
                    if q:
                        b, = ready_at(pe, pl, [f"ht{q}"], [f"gu{q}"])
                    else:
                        b, = ready_at(pe, pl, ["ht0"])
                        pe.wait_ge(s.sem["mid"], pl.value(pl.nth(0, s.parts_of["mid"], s.base["mid"])))
                    for c in range(FF // P):
                        ins = nc.tensor.transpose(b[:, c * P:(c + 1) * P], hmid[:, q, c * P:(c + 1) * P], ident[:, :])
                    filled(ins)

                def downs(q):
                    bs = ready_at(pe, pl, [f"yd{q}_{f}" for f in range(NH)], [f"ht{q}"])
                    w = [unit(landed(("down", q, e, 0)), FF // P, D) for e in range(QUAD)]
                    for f in range(NH):
                        for c in range(FF // P):
                            for e in range(QUAD):
                                ins = mm(bs[f][e * SLOTS:(e + 1) * SLOTS, :], lhsT=hmidT[:, c, e * SLOTS:(e + 1) * SLOTS],
                                         rhs=w[e][:, c, f * HALF:(f + 1) * HALF],
                                         start=(c == 0), stop=(c == FF // P - 1), skip_group_check=True)
                        filled(ins)

                def scatter(q):
                    for f in range(NH):
                        for t in range(TT):
                            b, = ready_at(pe, pl, [f"sc{q}_{f}_{t}"], [f"yd{q}_{f}"] if t == 0 else [])
                            filled(mm(b[:, :], lhsT=put[:, q, t, :], rhs=yslot[:, q, f * HALF:(f + 1) * HALF],
                                      start=True, stop=True))

                if pl.part == "prologue":
                    gather(0)
                    gate_up(0)
                    gather(1)
                    if s.late and pl.repeat is None:
                        for j in range(LATE_KEYS):
                            b = banks[LATE_BANK + j]
                            wait_unit(pe, U_XK[1][j])
                            w = unit(U_XK[1][j], KD, 256)
                            for q in range(2):
                                for k in range(KD):
                                    ins = mm(b[:, q * T:(q + 1) * T], lhsT=w[:, k, q * P:(q + 1) * P], rhs=memT[1][:, k, :],
                                             start=(k == 0), stop=(k == KD - 1))
                            ins.then_inc(late_filled, 1)
                    return
                puts()
                gate_up(1)
                mid(0)
                downs(0)
                scatter(0)
                if pl.part == "turn":
                    gather(0)
                mid(1)
                downs(1)
                if pl.part == "turn":
                    gate_up(0)
                    gather(1)
                scatter(1)
                if pl.part == "epilogue":
                    for o, last in (("dve", f"sc1_{NH - 1}_{TT - 1}"), ("act", "yd1_1")):
                        pe.wait_ge(s.sem[o], pl.value(pl.freed(last)))
                        pe.nop()

            def sweep(s, repeat=None):
                run_part(Place(s, "prologue", repeat=repeat))
                with pe.Fori(0, TURNS - 1) as turn:
                    run_part(Place(s, "turn", turn, repeat))
                run_part(Place(s, "epilogue", repeat=repeat))

            def moe(l):
                a, b = sweeps[l]
                wait_evac(pe, f"rk{l}")
                wait_evac(pe, f"nf{l}_3" if l else "xv1_1_1")
                sweep(a)
                pe.wait_ge(routed, l + 1)
                n = pe.value_load(most[0:1, l:l + 1], min_val=0, max_val=T)
                with pe.If(n > SLOTS):
                    pe.sem_inc(b.sem["filled"], b.base["filled"])
                    with pe.Fori(0, REPEATS) as repeat:
                        sweep(b, repeat)

            cross(0)
            route(0)
            moe(0)

            turn_rows("n4", xhat, 4)
            for t in range(TT):
                b = open_bank(pe, f"dnA_{t}")
                for k in range(KD):
                    if t == 0:
                        wait_evac(pe, f"n4_{k // 2}")
                    i = U_DOWN + k // 4
                    if t == 0 and k % 4 == 0:
                        wait_unit(pe, i)
                    ins = mm(b[:, :], lhsT=hT[:, k, t * P:(t + 1) * P], rhs=unit(i, 4, HALF)[:, k % 4, :],
                             start=(k == 0), stop=(k == KD - 1))
                fill(ins)
                if t == 0:
                    wait_unit(pe, U_DOWN + 2)
                b = open_bank(pe, f"dnB_{t}")
                for k in range(KD):
                    ins = mm(b[:, 0:DOWN - HALF], lhsT=hT[:, k, t * P:(t + 1) * P],
                             rhs=unit(U_DOWN + 2, KD, DOWN - HALF)[:, k, :], start=(k == 0), stop=(k == KD - 1))
                fill(ins)
            n = (QR + KVR) // P
            bs = [open_bank(pe, f"cT_{j}") for j in range(-(-n // 2))]
            for t in range(TT):
                pe.wait_ge(down_ready, t + 1)
                for c in range(n):
                    o = (c % 2) * T + t * P
                    ins = nc.tensor.transpose(bs[c // 2][:, o:o + P], down[:, t, c * P:(c + 1) * P], ident[:, :])
                    if t == TT - 1 and (c % 2 or c == n - 1):
                        fill(ins)
            for t in range(TT):
                for n in range(3):
                    if t == 0:
                        wait_unit(pe, U_UQ + n)
                    b = open_bank(pe, f"uq_{n}_{t}")
                    for k in range(3):
                        if t == n == 0:
                            wait_evac(pe, f"cT_{k // 2}")
                        ins = mm(b[:, :], lhsT=cT[:, k, t * P:(t + 1) * P], rhs=unit(U_UQ + n, 3, HALF)[:, k, :],
                                 start=(k == 0), stop=(k == 2))
                    fill(ins)

            def heads(name, rows):
                for j in range(H // 2):
                    b = open_bank(pe, f"{name}_{j}")
                    for q in range(2):
                        for t in range(TT):
                            c = (2 * j + q) * QKD
                            ins = nc.tensor.transpose(b[0:QKD, q * T + t * P:q * T + (t + 1) * P], rows[t][:, c:c + QKD], ident[:, :])
                    fill(ins)

            wait_evac(pe, "cT_2")
            for n in range(4):
                if n % 2 == 0:
                    wait_unit(pe, U_UKV + n // 2)
                for t in range(TT):
                    b = open_bank(pe, f"ukv_{n}_{t}")
                    for k in range(2):
                        c = (n % 2) * HALF
                        ins = mm(b[:, :], lhsT=cT[:, 3 + k, t * P:(t + 1) * P], rhs=unit(U_UKV + n // 2, 2, D)[:, k, c:c + HALF],
                                 start=(k == 0), stop=(k == 1))
                    fill(ins)
            pe.wait_ge(roped, TT)
            heads("qT", [qtok[:, t, :] for t in range(TT)])
            pe.wait_ge(ktok_ready, TT)
            for t in range(TT):
                wait_evac(pe, f"ukv_3_{t}")
            heads("kT", ktok)
            for j in (H // 2 - 2, H // 2 - 1):
                wait_evac(pe, f"qT_{j}")
                wait_evac(pe, f"kT_{j}")

            def scores(hd):
                b = open_bank(pe, f"ms_{hd}")
                mm(b[:, 0:P], lhsT=qhT[0:QKD, hd, 0:P], rhs=khT[0:QKD, hd, 0:P], start=True, stop=True)
                ins = mm(b[:, P:3 * P], lhsT=qhT[0:QKD, hd, P:2 * P], rhs=khT[0:QKD, hd, :], start=True, stop=True)
                fill(ins)

            for hd in range(AHEAD):
                scores(hd)
            for hd in range(H):
                if hd + AHEAD < H:
                    scores(hd + AHEAD)
                b = open_bank(pe, f"mp_{hd}")
                pe.wait_ge(m_prob_ready, hd + 1)
                for c in range(3):
                    ins = nc.tensor.transpose(b[:, c * P:(c + 1) * P], prob[:, hd % DEPTH, c * P:(c + 1) * P], ident[:, :])
                fill(ins)
                if hd % 2:
                    b = open_bank(pe, f"mo_{hd // 2}")
                    for g in range(2):
                        hh = hd - 1 + g
                        wait_evac(pe, f"mp_{hh}")
                        o = b[g * VD:(g + 1) * VD, :]
                        mm(o[:, 0:T], lhsT=vtok[:, 0, hh * VD:(hh + 1) * VD], rhs=probT[:, g, 0:T],
                           start=True, stop=False, skip_group_check=True)
                        ins = mm(o[:, P:T], lhsT=vtok[:, 1, hh * VD:(hh + 1) * VD], rhs=probT[:, g, T:3 * P],
                                 start=False, stop=True, skip_group_check=True)
                    fill(ins)
            token_major("mw", U_MO, hT, lambda k: wait_evac(pe, f"mo_{k}"))
            cross(1)
            route(1)
            moe(1)


_INS = ["x", "mem", "positions", "norm_mix", "conv_w_in", "conv_b_in", "conv_w_dw", "conv_b_dw", "conv_ln_g",
        "conv_ln_b", "conv_w_out", "conv_b_out", "mla_w_down", "mla_q_norm", "mla_w_uq", "mla_kv_norm",
        "mla_w_ukv", "mla_w_o", "norm_xa", "norm_mem", "xa_wq", "xa_wkv", "xa_wo", "norm_ffn", "moe_w_grp",
        "moe_b_grp", "moe_w_exp", "moe_b_exp", "moe_w_gate", "moe_w_up", "moe_w_down", "final_norm"]


def kernel(**inputs):
    import numpy as _np
    import concourse.bacc as _bacc
    from concourse import mybir as _mybir
    from concourse.bass_utils import run_bass_kernel_spmd as _run

    nc = _bacc.Bacc("TRN2", target_bir_lowering=False, num_devices=1)
    arrays, args = {}, {}
    for name in _INS:
        a = _np.ascontiguousarray(inputs[name])
        arrays[f"in_{name}_dram"] = a
        args[name] = nc.dram_tensor(f"in_{name}_dram", a.shape, _mybir.dt.from_np(a.dtype), kind="ExternalInput").ap()
    shape = tuple(inputs["x"].shape)
    out = nc.dram_tensor("out_0_dram", shape, _mybir.dt.from_np(_np.dtype("float32")), kind="ExternalOutput").ap()
    trunk(nc, args, out)
    r = _run(nc, [arrays], core_ids=[0])
    return r.results[0]["out_0_dram"]
```
